# Optimizing a Trainium2 kernel written in Bass

```python
import jax, jax.numpy as jnp
from jax import lax
import numpy as np

D_MODEL = 1024
BATCH = 1
SEQ = 1024
DEPTH = 1
DEC_BATCH = 8
DEC_SEQ = 1
PAST_LEN = 8192
PAGE_SIZE = 128

D_MLSTM = D_MODEL // 2
N_HEADS = 4
DK = D_MLSTM // N_HEADS
DV = DK
CHUNK = 128
D_CONV = D_MODEL - D_MLSTM
CONV_W = 31
D_IN = 4 * D_MLSTM + 2 * N_HEADS + 2 * D_CONV
N_GROUPS = 4
EXP_PER_GROUP = 8
N_EXPERTS = N_GROUPS * EXP_PER_GROUP
TOP_K = 2
D_EXPERT = 256
EPS = 1e-6

kernel_name = "hymba_mlstm_conformer_hiermoe_step"

def rms_norm(x, g):
    xf = x.astype(jnp.float32)
    y = xf * lax.rsqrt(jnp.mean(xf * xf, -1, keepdims=True) + EPS)
    return (y * g.astype(jnp.float32)).astype(x.dtype)

def layer_norm_f32(x, g, b=None):
    xf = x.astype(jnp.float32)
    mu = jnp.mean(xf, -1, keepdims=True)
    var = jnp.mean(jnp.square(xf - mu), -1, keepdims=True)
    y = (xf - mu) * lax.rsqrt(var + EPS) * g.astype(jnp.float32)
    if b is not None:
        y = y + b.astype(jnp.float32)
    return y

def mlstm_chunkwise(q, k, v, ig, fg, C0, n0, m0):
    B, H, T, _ = q.shape
    L = CHUNK if T % CHUNK == 0 else T
    nc = T // L
    logf = jax.nn.log_sigmoid(fg)

    def split(a):
        return jnp.moveaxis(a.reshape(B, H, nc, L, *a.shape[3:]), 2, 0)

    causal = jnp.tril(jnp.ones((L, L), dtype=bool))

    def step(carry, xs):
        C, n, m = carry
        qc, kc, vc, ic, lfc = xs
        b = jnp.cumsum(lfc, -1)
        dmat = b[..., :, None] - b[..., None, :] + ic[..., None, :]
        dmat = jnp.where(causal, dmat, -jnp.inf)
        inter = b + m[..., None]
        m_t = jnp.maximum(inter, jnp.max(dmat, -1))
        w = jnp.exp(dmat - m_t[..., None])
        a_inter = jnp.exp(inter - m_t)
        s = jnp.einsum('bhtd,bhsd->bhts', qc, kc) * w
        num = jnp.einsum('bhts,bhse->bhte', s, vc) + a_inter[..., None] * jnp.einsum('bhtd,bhde->bhte', qc, C)
        den = jnp.sum(s, -1) + a_inter * jnp.einsum('bhtd,bhd->bht', qc, n)
        h = num / jnp.maximum(jnp.abs(den), jnp.exp(-m_t))[..., None]
        m_new = m_t[..., -1]
        wl = jnp.exp(dmat[..., -1, :] - m_new[..., None])
        decay = jnp.exp(b[..., -1] + m - m_new)
        C_new = decay[..., None, None] * C + jnp.einsum('bhs,bhsd,bhse->bhde', wl, kc, vc)
        n_new = decay[..., None] * n + jnp.einsum('bhs,bhsd->bhd', wl, kc)
        return (C_new, n_new, m_new), h

    (C, n, m), hs = lax.scan(step, (C0, n0, m0), (split(q), split(k), split(v), split(ig), split(logf)))
    h = jnp.moveaxis(hs, 0, 2).reshape(B, H, T, DV)
    return h, C, n, m

def conformer_conv(u, buf, w_dw, b_dw, ln_g, ln_b):
    full = jnp.concatenate([buf.astype(u.dtype), u], axis=1)
    y = lax.conv_general_dilated(full, w_dw.astype(u.dtype), window_strides=(1,), padding='VALID',
                                 dimension_numbers=('NWC', 'WIO', 'NWC'),
                                 feature_group_count=D_CONV) + b_dw
    new_buf = full[:, -(CONV_W - 1):]
    y = jax.nn.silu(layer_norm_f32(y, ln_g, ln_b)).astype(u.dtype)
    return y, new_buf

def hier_moe(x, w_grp, b_grp, w_er, b_er, w_gate, w_up, w_down):
    N = x.shape[0]
    xf = x.astype(jnp.float32)
    g_logits = xf @ w_grp.astype(jnp.float32) + b_grp
    g_prob = jax.nn.softmax(g_logits, -1)
    g_sel = jnp.argmax(g_logits, -1)
    p_g = jnp.take_along_axis(g_prob, g_sel[:, None], -1)
    e_logits = (xf @ w_er.astype(jnp.float32) + b_er).reshape(N, N_GROUPS, EXP_PER_GROUP)
    e_sel = jnp.take_along_axis(e_logits, g_sel[:, None, None], 1)[:, 0]
    top_v, top_i = lax.top_k(e_sel, TOP_K)
    top_w = jax.nn.softmax(top_v, -1) * p_g
    e_idx = g_sel[:, None] * EXP_PER_GROUP + top_i
    combine = jnp.sum(jax.nn.one_hot(e_idx, N_EXPERTS, dtype=jnp.float32) * top_w[..., None], 1).astype(x.dtype)
    out = jnp.zeros_like(x)
    for grp in range(N_GROUPS):
        sl = slice(grp * EXP_PER_GROUP, (grp + 1) * EXP_PER_GROUP)
        hid = jax.nn.silu(jnp.einsum('nd,edf->nef', x, w_gate[sl])) * jnp.einsum('nd,edf->nef', x, w_up[sl])
        out = out + jnp.einsum('nef,efd->nd', hid * combine[:, sl, None], w_down[sl])
    return out

def hybrid_layer(x, c, C0, n0, m0, buf, w_ada, b_ada, norm1_g, w_in, b_igate, b_fgate, mh_norm_g,
                 w_dw, b_dw, conv_ln_g, conv_ln_b, w_out, norm2_g, w_grp_router, b_grp_router,
                 w_exp_router, b_exp_router, w_gate, w_up, w_down):
    B, T, _ = x.shape
    mod = jax.nn.silu(c) @ w_ada + b_ada
    sh1, sc1, g1, sh2, sc2, g2 = jnp.split(mod, 6, axis=-1)
    h = rms_norm(x, norm1_g) * (1 + sc1[:, None]) + sh1[:, None]
    z = h @ w_in
    cuts = [D_MLSTM, 2 * D_MLSTM, 3 * D_MLSTM, 4 * D_MLSTM, 4 * D_MLSTM + N_HEADS,
            4 * D_MLSTM + 2 * N_HEADS, 4 * D_MLSTM + 2 * N_HEADS + D_CONV]
    q, k, v, o, ig, fg, ga, gb = jnp.split(z, cuts, axis=-1)

    def heads(a):
        return a.reshape(B, T, N_HEADS, -1).transpose(0, 2, 1, 3).astype(jnp.float32)

    igh = (ig.astype(jnp.float32) + b_igate).transpose(0, 2, 1)
    fgh = (fg.astype(jnp.float32) + b_fgate).transpose(0, 2, 1)
    hm, C1, n1, m1 = mlstm_chunkwise(heads(q), heads(k) * DK ** -0.5, heads(v), igh, fgh,
                                     C0.astype(jnp.float32), n0.astype(jnp.float32), m0.astype(jnp.float32))
    hm = layer_norm_f32(hm, mh_norm_g[:, None, :])
    hm = hm.transpose(0, 2, 1, 3).reshape(B, T, D_MLSTM).astype(x.dtype) * jax.nn.sigmoid(o)

    u = ga * jax.nn.sigmoid(gb)
    hc, new_buf = conformer_conv(u, buf, w_dw, b_dw, conv_ln_g, conv_ln_b)

    x = x + g1[:, None] * (jnp.concatenate([hm, hc], axis=-1) @ w_out)
    h2 = rms_norm(x, norm2_g) * (1 + sc2[:, None]) + sh2[:, None]
    moe = hier_moe(h2.reshape(B * T, D_MODEL), w_grp_router, b_grp_router, w_exp_router, b_exp_router,
                   w_gate, w_up, w_down).reshape(B, T, D_MODEL)
    x = x + g2[:, None] * moe
    return x, C1, n1, m1, new_buf

def setup_inputs(seed: int = 0) -> dict:
    key = jax.random.key(seed)
    ks = jax.random.split(key, 32)
    f32 = jnp.float32

    def nrm(k, shape, scale):
        return jax.random.normal(k, shape, f32) * scale

    return {
        "x_prompt": nrm(ks[0], (BATCH, SEQ, D_MODEL), 1.0),
        "x_sample": nrm(ks[1], (DEC_BATCH, DEC_SEQ, D_MODEL), 1.0),
        "c_prompt": nrm(ks[2], (BATCH, D_MODEL), 1.0),
        "c_sample": nrm(ks[3], (DEC_BATCH, D_MODEL), 1.0),
        "state_mlstm_C": nrm(ks[4], (DEPTH, DEC_BATCH, N_HEADS, DK, DV), 0.1),
        "state_mlstm_n": nrm(ks[5], (DEPTH, DEC_BATCH, N_HEADS, DK), 0.1),
        "state_mlstm_m": nrm(ks[6], (DEPTH, DEC_BATCH, N_HEADS), 1.0),
        "cache_conv": nrm(ks[7], (DEPTH, DEC_BATCH, CONV_W - 1, D_CONV), 0.5),
        "w_ada": nrm(ks[8], (DEPTH, D_MODEL, 6 * D_MODEL), 0.5 * D_MODEL ** -0.5),
        "b_ada": nrm(ks[9], (DEPTH, 6 * D_MODEL), 0.02),
        "norm1_g": 1.0 + nrm(ks[10], (DEPTH, D_MODEL), 0.05),
        "w_in": nrm(ks[11], (DEPTH, D_MODEL, D_IN), D_MODEL ** -0.5),
        "b_igate": nrm(ks[12], (DEPTH, N_HEADS), 0.1),
        "b_fgate": 3.0 + nrm(ks[13], (DEPTH, N_HEADS), 0.5),
        "mh_norm_g": 1.0 + nrm(ks[14], (DEPTH, N_HEADS, DV), 0.05),
        "w_dw": nrm(ks[15], (DEPTH, CONV_W, 1, D_CONV), CONV_W ** -0.5),
        "b_dw": nrm(ks[16], (DEPTH, D_CONV), 0.02),
        "conv_ln_g": 1.0 + nrm(ks[17], (DEPTH, D_CONV), 0.05),
        "conv_ln_b": nrm(ks[18], (DEPTH, D_CONV), 0.02),
        "w_out": nrm(ks[19], (DEPTH, D_MODEL, D_MODEL), D_MODEL ** -0.5),
        "norm2_g": 1.0 + nrm(ks[20], (DEPTH, D_MODEL), 0.05),
        "w_grp_router": nrm(ks[21], (DEPTH, D_MODEL, N_GROUPS), D_MODEL ** -0.5),
        "b_grp_router": nrm(ks[22], (DEPTH, N_GROUPS), 0.01),
        "w_exp_router": nrm(ks[23], (DEPTH, D_MODEL, N_EXPERTS), D_MODEL ** -0.5),
        "b_exp_router": nrm(ks[24], (DEPTH, N_EXPERTS), 0.01),
        "w_gate": nrm(ks[25], (DEPTH, N_EXPERTS, D_MODEL, D_EXPERT), D_MODEL ** -0.5),
        "w_up": nrm(ks[26], (DEPTH, N_EXPERTS, D_MODEL, D_EXPERT), D_MODEL ** -0.5),
        "w_down": nrm(ks[27], (DEPTH, N_EXPERTS, D_EXPERT, D_MODEL), D_EXPERT ** -0.5),
        "final_g": 1.0 + nrm(ks[28], (D_MODEL,), 0.05),
    }

def reference(x_prompt, x_sample, c_prompt, c_sample, state_mlstm_C, state_mlstm_n, state_mlstm_m,
              cache_conv, w_ada, b_ada, norm1_g, w_in, b_igate, b_fgate, mh_norm_g, w_dw, b_dw,
              conv_ln_g, conv_ln_b, w_out, norm2_g, w_grp_router, b_grp_router, w_exp_router,
              b_exp_router, w_gate, w_up, w_down, final_g):
    f32 = jnp.float32
    xp, xs = x_prompt, x_sample
    Cp_l, np_l, mp_l, bp_l = [], [], [], []
    Cs_l, ns_l, ms_l, bs_l = [], [], [], []
    for l in range(DEPTH):
        w = (w_ada[l], b_ada[l], norm1_g[l], w_in[l], b_igate[l], b_fgate[l], mh_norm_g[l],
             w_dw[l], b_dw[l], conv_ln_g[l], conv_ln_b[l], w_out[l], norm2_g[l], w_grp_router[l],
             b_grp_router[l], w_exp_router[l], b_exp_router[l], w_gate[l], w_up[l], w_down[l])
        zC = jnp.zeros((BATCH, N_HEADS, DK, DV), f32)
        zn = jnp.zeros((BATCH, N_HEADS, DK), f32)
        zm = jnp.zeros((BATCH, N_HEADS), f32)
        zb = jnp.zeros((BATCH, CONV_W - 1, D_CONV), xp.dtype)
        xp, Cp, n_p, mp, bp = hybrid_layer(xp, c_prompt, zC, zn, zm, zb, *w)
        xs, Cs, n_s, ms, bs = hybrid_layer(xs, c_sample, state_mlstm_C[l], state_mlstm_n[l],
                                           state_mlstm_m[l], cache_conv[l], *w)
        Cp_l.append(Cp); np_l.append(n_p); mp_l.append(mp); bp_l.append(bp)
        Cs_l.append(Cs); ns_l.append(n_s); ms_l.append(ms); bs_l.append(bs)
    y_prompt = rms_norm(xp, final_g)
    y_sample = rms_norm(xs, final_g)
    return (y_prompt, y_sample,
            jnp.stack(Cp_l), jnp.stack(np_l), jnp.stack(mp_l), jnp.stack(bp_l),
            jnp.stack(Cs_l), jnp.stack(ns_l), jnp.stack(ms_l), jnp.stack(bs_l))


_drawn_inputs = setup_inputs


def setup_inputs(seed=0):
    import zlib

    import numpy as np

    out = dict(_drawn_inputs(seed))
    spreads = {}
    factors = {'mh_norm_g': 5.838,
     'b_dw': 6.632,
     'conv_ln_g': 6.049,
     'conv_ln_b': 8.0,
     'norm2_g': 3.067,
     'b_grp_router': 8.0,
     'b_exp_router': 8.0}
    for name, (base, spread) in spreads.items():
        noise = np.random.default_rng([zlib.crc32(name.encode()), seed]).standard_normal(out[name].shape)
        drawn = base * np.exp(spread * noise) if base else spread * noise
        out[name] = __import__('jax').numpy.asarray(drawn.astype(out[name].dtype))
    for name, factor in factors.items():
        out[name] = (out[name] * factor).astype(out[name].dtype)
    return out
```

```python
from contextlib import ExitStack

import concourse.bass as bass
from concourse import mybir

F32 = mybir.dt.float32
F32R = mybir.dt.float32r
BF16 = mybir.dt.bfloat16
I32 = mybir.dt.int32
ALU = mybir.AluOpType
ACT = mybir.ActivationFunctionType
AXX = mybir.AxisListType.X

P = 128
D = 1024
KD = D // P
T = 1024
NC_ = T // P
S = 8
NT = NC_ + 1
NTOK = T + S
H = 4
DH = 128
CB = 4
CW = 31
PAD = CW - 1
ZW = PAD + T + S
SC = PAD + T
DIN = 4 * H * DH + 2 * H + 2 * CB * P
EPS = 1e-6
QK = DH ** -0.5
U0, GB0, Q0, K0, V0, O0 = 0, 4, 8, 12, 16, 20
NZ = 24
VA = DH + 2
NG, EPG, NE, FE = 4, 8, 32, 256
NR = NG + NE
NOV = (2 * NTOK) // P
NOTOK = 4095
MT = NE + NOV
BIG = 1.0e30
LNEXP = "natural_log_exp_and_others"
NV = 80
VM, VB, VLG, VLB = 64, 68, 72, 76
AG = 2048
NAG = 6 * D // AG
MB = 6 * D // P


STEPS = {
    "PE": (
        "c9T_ps vT_ps cT_ps tails_ps mean_ps sumsq_ps rowsT_ps n0T_ps vtok_ps sdot_ps qc_ps nnew_ps "
        "smean_ps svar_ps rank_ps"),
    "DVE": (
        "modr_zero dve_consts lists_zero c9T_ready mod_ready u_ready conv_sum absf_ready centred "
        "rows_in conv_scaled sB_ready sprod_ready snew_ready sh_ready ssq_ready mlstm_done "
        "stage1_over gmax_ready ediff_ready mask_ready sidx_ready nov_ready glists_ready experts_go "
        "experts_done"),
    "ACT": (
        "csilu gates_ready softplus_ready squares crstd_ready srow_ready conv_done vtok_ready "
        "srstd_ready nnew_ready gexp_ready eexp_ready g2b_ready"),
    "POOL": (
        "gate_zeroed iota_ready"),
}
STEP = {name: (engine, n + 1) for engine, names in STEPS.items() for n, name in enumerate(names.split())}


class Chain:

    def __init__(self, eng, sem):
        self.eng, self.sem, self.n, self.base = eng, sem, 0, None

    def value(self):
        return self.n if self.base is None else self.base + self.n

    def __call__(self, ins):
        self.n += 1
        ins.then_inc(self.sem, 1)
        self.eng.wait_ge(self.sem, self.value())
        return ins

    def last(self, ins):
        self.n += 1
        ins.then_inc(self.sem, 1)
        return ins

    def wait(self):
        self.eng.wait_ge(self.sem, self.value())


def build(nc, x_prompt, x_sample, c_prompt, c_sample, C0, n0, m0, cache, w_ada, b_ada, norm1_g, w_in,
          b_ig, b_fg, mh_g, w_dw, b_dw, cln_g, cln_b, w_out, norm2_g, w_grp, b_grp, w_er, b_er,
          w_gate, w_up, w_down, final_g,
          y_p, y_s, C_p, n_p, m_p, conv_p, C_s, n_s, m_s, conv_s):
    x_d = [x_prompt[0, t * P:(t + 1) * P, :] for t in range(NC_)] + [x_sample[:, 0, :]]
    y_d = [y_p[0, t * P:(t + 1) * P, :] for t in range(NC_)] + [y_s[:, 0, :]]
    rows = [P] * NC_ + [S]
    x2_dram = nc.dram_tensor("x2_scratch", (NTOK, D), F32, kind="Internal").ap()
    h2_dram = nc.dram_tensor("h2_scratch", (NTOK, D), F32, kind="Internal").ap()
    list_dram = nc.dram_tensor("token_list", (P * MT, 1), I32, kind="Internal").ap()
    ye_dram = nc.dram_tensor("expert_results", (2 * NTOK, D), F32, kind="Internal").ap()

    with ExitStack() as ctx:
        sems = {}

        def sem(name):
            if name not in sems:
                sems[name] = ctx.enter_context(nc.semaphore(name))
            return sems[name]

        def step(name):
            return sem("steps_" + STEP[name][0])

        def after(name):
            return STEP[name][1]

        marks_used = [0]

        def mark():
            marks_used[0] += 1
            return marks[0:1, marks_used[0] - 1:marks_used[0]]

        def sb(scope, name, shape, dt=F32):
            return scope.enter_context(nc.sbuf_tensor(name, shape, dt))

        ctx.enter_context(nc.allow_non_contiguous_dma(reason="vectors of 32 and 512 elements, turned"))
        ps = ctx.enter_context(nc.psum_tensor("ps", [P, 8, 512], F32))

        marks = sb(ctx, "marks", [1, 64])
        rowmask = sb(ctx, "rowmask", [P, 1])
        ident = sb(ctx, "ident", [P, P])
        ones = sb(ctx, "ones", [P, P])
        ustrict = sb(ctx, "ustrict", [P, P])
        identb = sb(ctx, "identb", [P, P], BF16)
        causal = sb(ctx, "causal", [P, P], BF16)
        epst = sb(ctx, "epst", [P, 1])
        vT = sb(ctx, "vT", [P, NV])
        wdT = sb(ctx, "wdT", [P, CB, CW])
        modT = sb(ctx, "modT", [P, MB, 9])
        A1 = sb(ctx, "A1", [P, KD, 9])
        A2 = sb(ctx, "A2", [P, KD, 9])
        bi = sb(ctx, "bi", [H, 1])
        bf = sb(ctx, "bf", [H, 1])
        ssq = sb(ctx, "ssq", [P, 2, 2])
        logits = sb(ctx, "logits", [P, NT, NR])
        wts = sb(ctx, "wts", [P, 2, NT])
        slots = sb(ctx, "slots", [P, 2, NT], I32)
        sidx = sb(ctx, "sidx", [P, 2, NT], I32)
        tokid = sb(ctx, "tokid", [P, 2, NT], I32)
        lists = sb(ctx, "lists", [P, MT], I32)
        glists = sb(ctx, "glists", [P, MT], I32)
        gcur = sb(ctx, "gcur", [P, 2, 1], I32)
        scur = sb(ctx, "scur", [P, 2, 1], I32)
        passed = sb(ctx, "passed", [1, 2])
        ovx = sb(ctx, "ovx", [1, NOV], I32)
        nov = sb(ctx, "nov", [1, 1], I32)

        st1 = ExitStack()
        stA = ExitStack()
        wada = sb(stA, "wada", [P, 4, AG])
        c9 = sb(stA, "c9", [9, D])
        c9T = sb(stA, "c9T", [P, KD, 9])
        vecs = sb(stA, "vecs", [NV, P])
        wdw = sb(stA, "wdw", [CW, CB * P])
        modr = sb(stA, "modr", [P, NAG, 512])
        xt = sb(stA, "xt", [P, 2, D])
        xn = sb(stA, "xn", [P, 2, D])
        hf = sb(stA, "hf", [P, 2, KD, P])
        stA.close()
        z = sb(st1, "z", [P, NZ, ZW])
        stB = ExitStack()
        hhi = sb(stB, "hhi", [P, KD, NTOK], F32R)
        hlo = sb(stB, "hlo", [P, KD, NTOK], F32R)
        wgt = sb(stB, "wgt", [P, KD, 2 * H])
        wraw = sb(stB, "wraw", [P, 2, KD, 256])
        whi = sb(stB, "whi", [P, 2, KD, P], F32R)
        wlo = sb(stB, "wlo", [P, 2, KD, P], F32R)
        stB.close()
        wout = sb(st1, "wout", [P, KD, D])
        wr = sb(st1, "wr", [P, KD, NR])
        rbias = sb(st1, "rbias", [P, NR])
        bcv = sb(st1, "bcv", [P, 3, D])
        rows_ = sb(st1, "rows", [68, T])
        negM = sb(st1, "negM", [H, T])
        rowsT = sb(st1, "rowsT", [P, NC_, 68])
        dec = sb(st1, "dec", [P, H, NC_])
        srow = sb(st1, "srow", [H, 3, S])
        sB = sb(st1, "sB", [P, H, 3, S])
        sm = sb(st1, "sm", [P, 12, S * H])
        ntok = sb(st1, "ntok", [S * H, DH])
        vtok = sb(st1, "vtok", [S, H * DH])
        utail = sb(st1, "utail", [PAD, CB * P])
        usam = sb(st1, "usam", [S, CB * P])
        m0t = sb(st1, "m0t", [H, S])
        stG = ExitStack()
        gi = sb(stG, "gi", [H, NTOK])
        gf = sb(stG, "gf", [H, NTOK])
        gt = sb(stG, "gt", [H, NTOK])
        mrow = sb(stG, "mrow", [H, NTOK])
        brow = sb(stG, "brow", [H, NTOK])
        mprev = sb(stG, "mprev", [H, NC_])
        stG.close()
        kw = sb(st1, "kw", [P, H, DH])
        vaug = sb(st1, "vaug", [P, H, VA])
        wx = sb(st1, "wx", [P, H, P])
        sT = sb(st1, "sT", [P, H, P])
        caug = sb(st1, "caug", [P, H, VA])
        num = sb(st1, "num", [P, H, VA])
        n2s = sb(st1, "n2s", [P, H, VA])
        hn = sb(st1, "hn", [P, H, DH])
        lst = sb(st1, "lst", [P, 5, H])
        bst = sb(st1, "bst", [P, H, 6])
        bag = sb(st1, "bag", [P, H, 2])
        featT = sb(st1, "featT", [P, 2, H, P])
        stL = ExitStack()
        crow = sb(stL, "crow", [4 * PAD, 2, CB * P])
        crstd = sb(stL, "crstd", [P, NTOK])
        cT = sb(stL, "cT", [P, CB, S, CW])
        cprod = sb(stL, "cprod", [P, CB, S, CW])
        stL.close()
        stS = ExitStack()
        c0 = sb(stS, "c0", [P, S * H, DH])
        stS.close()
        x2 = sb(st1, "x2", [P, 2, D])
        h2 = sb(st1, "h2", [P, D])
        h2T = sb(st1, "h2T", [P, KD, P])
        st1.close()
        st2 = ExitStack()
        eraw = sb(st2, "eraw", [P, 2, KD, 2 * FE])
        draw = sb(st2, "draw", [P, 2, 2, D])
        ehi = sb(st2, "ehi", [P, 2, KD, 2 * FE], F32R)
        elo = sb(st2, "elo", [P, 2, KD, 2 * FE], F32R)
        dhi = sb(st2, "dhi", [P, 2, 2, D], F32R)
        dlo = sb(st2, "dlo", [P, 2, 2, D], F32R)
        stR = ExitStack()
        iot = sb(stR, "iot", [P, NE])
        ioti = sb(stR, "ioti", [P, NE], I32)
        ga_ = sb(stR, "ga_", [P, NT, NG])
        gb_ = sb(stR, "gb_", [P, NT, NG])
        ex = sb(stR, "ex", [P, NT, NE])
        oh = sb(stR, "oh", [P, 2, NT, NE])
        et = sb(stR, "et", [P, NT, NE])
        em_ = sb(stR, "em_", [P, NT, NE])
        pos = sb(stR, "pos", [P, NT, NE])
        tot = sb(stR, "tot", [P, NT + 1, NE])
        thr = sb(stR, "thr", [P, NE, NT])
        ov = sb(stR, "ov", [P, 4, NE])
        r9 = sb(stR, "r9", [P, 10, NT])
        ovc = sb(stR, "ovc", [1, NOV, NE])
        ovf = sb(stR, "ovf", [1, 2, NOV])
        sloti = sb(stR, "sloti", [P, 2, NT], I32)
        stR.close()
        xg = sb(st2, "xg", [P, 2, D])
        xhi = sb(st2, "xhi", [P, 2, KD, P], F32R)
        xlo = sb(st2, "xlo", [P, 2, KD, P], F32R)
        gs = sb(st2, "gs", [P, FE])
        hid = sb(st2, "hid", [P, FE])
        thi = sb(st2, "thi", [P, 2, P], F32R)
        tlo = sb(st2, "tlo", [P, 2, P], F32R)
        ysb = sb(st2, "ysb", [P, 2, D])
        st2.close()
        st3 = ExitStack()
        y12 = sb(st3, "y12", [P, 2, 2, D])
        xf = sb(st3, "xf", [P, 2, D])
        g2b = sb(st3, "g2b", [P, 2, D])
        fgb = sb(st3, "fgb", [P, D])
        of = sb(st3, "of", [P, 2, D])
        st3.close()

        w_in_v = w_in.rearrange("(k p) n -> p k n", p=P)
        C0_CONV = 4 * H * DH + 2 * H
        SPLITS = NZ // 4
        CROUNDS = 2

        def u_at(blk, w, n):
            return z[:, U0 + blk, w:w + n]

        def store_tile(sp, i):
            t = (NT - 1, *range(NC_))[i]
            sp.wait_ge(sem("x2_ready"), i + 1)
            sp.dma_start(x2_dram[t * P:t * P + rows[t], :], x2[0:rows[t], i % 2, :]).then_inc(sem(f"x2_out{i % 2}"), 16)
            sp.wait_ge(sem("h2_ready"), i + 1)
            sp.dma_start(h2_dram[t * P:t * P + rows[t], :], h2[0:rows[t], :]).then_inc(sem("h2_out"), 16)

        def bc(ap, n):
            return ap.broadcast_to([P, H, n])

        def hb(ap):
            return ap.rearrange("p (h b) -> p h b", h=H)

        TAILS, MEAN, GATES = 6, 2, 4

        def act_rest(act, chain):
            def signal(name):
                chain.wait()
                act.activation(mark(), epst[0:1, 0:1], ACT.Copy).then_inc(step(name) if name in STEP else sem(name), 1)

            act.wait_ge(sem("z_done"), NZ + 3)
            act.wait_ge(sem("gbias_in"), 32)
            act.preload_act_table_set(LNEXP)

            both = ps[:, GATES:GATES + 2, :].rearrange("p b n -> p (b n)")
            chain.last(act.activation(gi[:, 0:T], both[0:H, :], ACT.Identity, bias=bi[:, :]))
            chain.last(act.activation(gi[:, T:NTOK], ps[0:H, 0, 0:S], ACT.Identity, bias=bi[:, :]))
            chain.last(act.activation(gf[:, 0:T], both[32:32 + H, :], ACT.Copy))
            chain.last(act.activation(gf[:, T:NTOK], ps[32:32 + H, 0, 0:S], ACT.Copy))
            signal("gates_ready")
            act.wait_ge(step("tails_ps"), after("tails_ps"))
            act.activation(utail[:, :], ps[0:PAD, TAILS, :], ACT.Copy).then_inc(sem("tails_ready"), 1)
            act.activation(usam[:, :], ps[0:S, TAILS + 1, :], ACT.Copy).then_inc(sem("tails_ready"), 1)
            act.wait_ge(step("absf_ready"), after("absf_ready"))
            chain(act.activation(gt[:, :], gt[:, :], ACT.Exp, scale=-1.0))
            act.activation(gt[:, :], gt[:, :], ACT.Ln, bias=ones[0:H, 0:1]).then_inc(step("softplus_ready"), 1)
            act.wait_ge(step("centred"), after("centred"))
            act.activation(z[:, U0:U0 + CB, PAD:ZW], z[:, GB0:GB0 + CB, PAD:ZW], ACT.Square).then_inc(step("squares"), 1)
            act.wait_ge(step("sumsq_ps"), after("sumsq_ps"))
            chain.last(act.activation(crstd[:, 0:T], ps[:, MEAN:MEAN + 2, :].rearrange("p b n -> p (b n)"), ACT.Ln,
                                      bias=epst[:, :], scale=1.0 / (CB * P)))
            chain(act.activation(crstd[:, T:NTOK], ps[:, 6, 0:S], ACT.Ln, bias=epst[:, :], scale=1.0 / (CB * P)))
            act.activation(crstd[:, :], crstd[:, :], ACT.Exp, scale=-0.5).then_inc(step("crstd_ready"), 1)
            act.wait_ge(step("rows_in"), after("rows_in"))
            chain.last(act.activation(rows_[0:H, :], rows_[0:H, :], ACT.Exp))
            chain.last(act.activation(rows_[64:64 + H, :], rows_[64:64 + H, :], ACT.Exp, scale=-1.0))
            chain.last(act.activation(srow[:, :, :], srow[:, :, :], ACT.Exp))
            signal("srow_ready")
            act.wait_ge(step("conv_scaled"), after("conv_scaled"))
            for b in range(CB):
                chain.last(act.activation(z[:, GB0 + b, PAD:ZW], z[:, GB0 + b, PAD:ZW], ACT.Silu,
                                          scale=vT[:, VLG + b:VLG + b + 1], bias=vT[:, VLB + b:VLB + b + 1]))
            signal("conv_done")
            act.preload_act_table_set(LNEXP)
            act.wait_ge(step("vtok_ps"), after("vtok_ps"))
            act.activation(vtok[:, :], ps[0:S, 2, :], ACT.Copy).then_inc(step("vtok_ready"), 1)
            act.wait_ge(step("sB_ready"), after("sB_ready"))
            act.wait_ge(step("qc_ps"), after("qc_ps"))
            for b in range(S):
                for h in range(H):
                    m = c0[:, b * H + h, :]
                    act.activation(m, m, ACT.Copy, scale=sB[:, h, 1, b:b + 1]).then_inc(sem("c0_scaled"), 1)
            act.wait_ge(step("svar_ps"), after("svar_ps"))
            chain(act.activation(sm[:, 8, :], ps[:, 6, 384:416], ACT.Ln, bias=epst[:, :], scale=1.0 / DH))
            act.activation(sm[:, 8, :], sm[:, 8, :], ACT.Exp, scale=-0.5).then_inc(step("srstd_ready"), 1)
            act.wait_ge(step("nnew_ps"), after("nnew_ps"))
            act.activation(ntok[:, :], ps[0:S * H, 2, 0:DH], ACT.Copy).then_inc(step("nnew_ready"), 1)

            def broadcasts(k, n):
                for i in range(3):
                    act.wait_ge(sem("bcv_ps"), 3 * k + i + 1)
                    act.activation(bcv[0:n, i, :], ps[0:n, 6:8, :].rearrange("p b n -> p (b n)"), ACT.Copy)\
                       .then_inc(sem("bcv_ready"), 1)

            def tile_stats(i, n):
                act.wait_ge(sem("x2_ready"), i + 1)
                b = i % 2
                chain(act.activation(h2[0:n, :], x2[0:n, b, :], ACT.Square, accum_out=ssq[0:n, b, 0:1]))
                chain(act.activation(ssq[0:n, b, 1:2], ssq[0:n, b, 0:1], ACT.Ln, bias=epst[0:n, :], scale=1.0 / D))
                act.activation(ssq[0:n, b, 1:2], ssq[0:n, b, 1:2], ACT.Exp, scale=-0.5).then_inc(sem("rs2_ready"), 1)

            def tile_h2T(i, n):
                act.wait_ge(sem("h2T_ps"), i + 1)
                act.activation(h2T[:, :, 0:n],
                               ps[:, 6:8, :].rearrange("p a (k n) -> p (a k) n", k=4)[:, :, 0:n], ACT.Copy)\
                   .then_inc(sem("h2T_ready"), 1)

            broadcasts(0, S)
            tile_stats(0, S)
            tile_h2T(0, S)
            broadcasts(1, P)
            for c in range(NC_):
                act.wait_ge(sem("w_ps"), c + 1)
                if c:
                    act.wait_ge(sem("kw_ready"), c)
                for h in range(H):
                    act.activation(wx[:, h, :], ps[:, 1, h * P:(h + 1) * P], ACT.Exp, bias=rowsT[:, c, 32 + h:33 + h])\
                       .then_inc(sem("wx_ready"), 1)
                act.wait_ge(sem("v_ps"), c + 1)
                if c:
                    act.wait_ge(sem("kv_ps"), c)
                act.activation(vaug[:, :, 0:DH], ps[:, 3, :].rearrange("p (h d) -> p h d", h=H), ACT.Copy)\
                   .then_inc(sem("vaug_ready"), 1)
                if c:
                    tile_stats(c, P)
                act.wait_ge(sem("n2_ps"), c + 1)
                if c:
                    act.wait_ge(sem("num_ready"), c)
                for h in range(H):
                    act.activation(n2s[:, h, :], ps[:, h // 2, (h % 2) * VA:(h % 2) * VA + VA], ACT.Copy,
                                   scale=rowsT[:, c, h:h + 1]).then_inc(sem("n2_ready"), 1)
                if c:
                    tile_h2T(c, P)
                act.wait_ge(sem("var_ready"), c + 1)
                chain(act.activation(lst[:, 2, :], bag[:, :, 1], ACT.Ln, bias=epst[:, :]))
                act.activation(lst[:, 3, :], lst[:, 2, :], ACT.Exp, scale=-0.5).then_inc(sem("hrstd_ready"), 1)
            tile_stats(NC_, P)
            tile_h2T(NC_, P)
            moe_act(act, chain)

        def dve_rest(dve, chain):
            def signal(name):
                chain.wait()
                dve.memset(mark(), 0.0).then_inc(step(name) if name in STEP else sem(name), 1)

            zc = z[:, GB0:GB0 + CB, :]
            dve.wait_ge(step("cT_ps"), after("cT_ps"))
            for g in range(2):
                chain.last(dve.tensor_copy(
                    cT[:, :, 4 * g:4 * g + 4, 0:PAD],
                    ps[:, 2 + g, 0:4 * 4 * PAD].rearrange("p (k b w) -> p k b w", k=CB, b=4)))
            chain(dve.tensor_copy(cT[:, :, :, PAD], z[:, U0:U0 + CB, SC:ZW]))
            for b in range(CB):
                chain.last(dve.tensor_tensor(cprod[:, b, :, :], cT[:, b, :, :],
                                             wdT[:, b:b + 1, :].broadcast_to([P, S, CW]), ALU.mult))
            chain.wait()
            chain(dve.tensor_reduce(zc[:, :, SC:ZW], cprod[:, :, :, :], AXX, ALU.add))
            chain(dve.tensor_tensor(zc[:, :, SC:ZW], zc[:, :, SC:ZW],
                                    vT[:, VB:VB + CB].rearrange("p (b o) -> p b o", o=1).broadcast_to([P, CB, S]), ALU.add))
            signal("conv_sum")
            dve.wait_ge(step("gates_ready"), after("gates_ready"))
            chain(dve.tensor_scalar(gf[:, :], gf[:, :], bf[:, :], None, ALU.add))
            dve.scalar_tensor_tensor(out=gt[:, :], in0=gf[:, :], scalar=-1.0, in1=gf[:, :], op0=ALU.mult, op1=ALU.max).then_inc(step("absf_ready"), 1)
            dve.wait_ge(step("mean_ps"), after("mean_ps"))
            for k in range(3):
                a, b = (PAD + 512 * k, PAD + 512 * (k + 1)) if k < 2 else (SC, ZW)
                src = ps[:, MEAN + k, :] if k < 2 else ps[:, 6, 0:S]
                n = b - a
                chain.last(dve.scalar_tensor_tensor(
                    out=zc[:, :, a:b], in0=src.rearrange("p (o n) -> p o n", o=1).broadcast_to([P, CB, n]),
                    scalar=-1.0 / (CB * P), in1=zc[:, :, a:b], op0=ALU.mult, op1=ALU.add))
            signal("centred")
            dve.wait_ge(step("softplus_ready"), after("softplus_ready"))
            chain(dve.scalar_tensor_tensor(out=gf[:, :], in0=gf[:, :], scalar=0.0, in1=gt[:, :], op0=ALU.min,
                                           op1=ALU.subtract))
            chain.last(dve.tensor_tensor_scan(mrow[:, 0:T], gf[:, 0:T], gi[:, 0:T], 0.0, ALU.add, ALU.max))
            chain.last(dve.memset(rows_[:, :], 0.0))
            chain(dve.memset(gt[:, :], 0.0))
            for c in range(NC_):
                chain.last(dve.tensor_tensor_scan(brow[:, c * P:(c + 1) * P], gf[:, c * P:(c + 1) * P],
                                                  gt[:, c * P:(c + 1) * P], 0.0, ALU.add, ALU.add))
            chain.last(dve.memset(mprev[:, 0:1], 0.0))
            chain(dve.tensor_copy(mprev[:, 1:NC_], mrow[:, P - 1:T - 1:P]))
            chain(dve.tensor_tensor(negM[:, :], brow[:, 0:T], mrow[:, 0:T], ALU.subtract))
            chain.last(dve.tensor_tensor(rows_[0:H, :].rearrange("h (c t) -> h c t", c=NC_),
                                         negM[:, :].rearrange("h (c t) -> h c t", c=NC_),
                                         mprev[:, :].rearrange("h (c o) -> h c o", o=1).broadcast_to([H, NC_, P]), ALU.add))
            chain(dve.tensor_tensor(gt[:, 0:T], gi[:, 0:T], brow[:, 0:T], ALU.subtract))
            chain.last(dve.tensor_copy(rows_[32:32 + H, :], gt[:, 0:T]))
            chain.last(dve.tensor_copy(rows_[64:64 + H, :], mrow[:, 0:T]))
            dve.wait_ge(sem("m0_in"), 16)
            chain(dve.tensor_tensor(srow[:, 1, :], gf[:, T:NTOK], m0t[:, :], ALU.add))
            chain(dve.tensor_tensor(mrow[:, T:NTOK], srow[:, 1, :], gi[:, T:NTOK], ALU.max))
            chain.last(dve.tensor_tensor(srow[:, 1, :], srow[:, 1, :], mrow[:, T:NTOK], ALU.subtract))
            chain.last(dve.tensor_tensor(srow[:, 0, :], gi[:, T:NTOK], mrow[:, T:NTOK], ALU.subtract))
            chain.last(dve.tensor_scalar(srow[:, 2, :], mrow[:, T:NTOK], -1.0, None, ALU.mult))
            signal("rows_in")
            dve.wait_ge(step("crstd_ready"), after("crstd_ready"))
            chain(dve.tensor_tensor(zc[:, :, PAD:ZW], zc[:, :, PAD:ZW],
                                    crstd[:, :].rearrange("p (o n) -> p o n", o=1).broadcast_to([P, CB, NTOK]), ALU.mult))
            signal("conv_scaled")
            dve.wait_ge(sem("sig_o"), H)
            for h in range(H):
                chain.last(dve.tensor_scalar(z[:, O0 + h, PAD:ZW], z[:, O0 + h, PAD:ZW], vT[:, VM + h:VM + h + 1],
                                             None, ALU.mult))
            dve.wait_ge(step("rowsT_ps"), after("rowsT_ps"))
            for g in range(2):
                chain.last(dve.tensor_copy(rowsT[:, 4 * g:4 * g + 4, :],
                                           ps[:, 2 + g, 0:4 * 72].rearrange("p (c r) -> p c r", c=4)[:, :, 0:68]))
            chain.last(dve.tensor_copy(dec[:, :, :], ps[:, 6, 0:H * NC_].rearrange("p (h c) -> p h c", h=H)))
            chain.last(dve.tensor_copy(sB[:, :, :, :], ps[:, 6, 64:64 + H * 3 * S].rearrange("p (h f b) -> p h f b", h=H, f=3)))
            chain.wait()
            dve.wait_ge(sem("m_out"), 32)
            dve.memset(mark(), 0.0).then_inc(step("sB_ready"), 1)
            chain.last(dve.memset(caug[:, :, :], 0.0))
            chain.last(dve.memset(vaug[:, :, DH:DH + 1], 1.0))
            chain.last(dve.memset(vaug[:, :, DH + 1:VA], 0.0))
            signal("caug_ready")
            q, k, v = (z[:, o:o + H, SC:ZW] for o in (Q0, K0, V0))
            w_, ai, em = (sB[:, :, f, :] for f in range(3))
            dve.wait_ge(step("n0T_ps"), after("n0T_ps"))
            n0v = ps[:, 7, 0:S * H].rearrange("p (b h) -> p h b", h=H)
            chain.last(dve.tensor_tensor(hb(sm[:, 0, :]), q, k, ALU.mult))
            chain.last(dve.tensor_tensor(hb(sm[:, 1, :]), n0v, q, ALU.mult))
            chain.last(dve.tensor_copy(hb(sm[:, 2, :]), n0v))
            signal("sprod_ready")
            chain(dve.scalar_tensor_tensor(out=hb(sm[:, 9, :]), in0=k, scalar=QK, in1=w_, op0=ALU.mult, op1=ALU.mult))
            chain(dve.tensor_tensor(hb(sm[:, 10, :]), hb(sm[:, 2, :]), ai, ALU.mult))
            chain(dve.tensor_tensor(sm[:, 11, :].rearrange("p (b h) -> p h b", h=H), hb(sm[:, 10, :]), hb(sm[:, 9, :]), ALU.add))
            signal("snew_ready")
            dve.wait_ge(step("sdot_ps"), after("sdot_ps"))
            dve.wait_ge(step("qc_ps"), after("qc_ps"))
            dots = ps[:, 6, 256:320].rearrange("p (f h b) -> p f h b", f=2, h=H)
            chain.last(dve.scalar_tensor_tensor(out=hb(sm[:, 3, :]), in0=dots[:, 0], scalar=QK, in1=w_, op0=ALU.mult, op1=ALU.mult))
            chain.last(dve.tensor_tensor(hb(sm[:, 4, :]), dots[:, 1], ai, ALU.mult))
            chain(dve.tensor_tensor(hb(sm[:, 6, :]), ps[:, 7, 64:96].rearrange("p (h b) -> p h b", h=H), ai, ALU.mult))
            chain.last(dve.tensor_tensor(hb(sm[:, 7, :]), hb(sm[:, 3, :]), v, ALU.mult))
            chain(dve.tensor_tensor(sm[:, 4, :], sm[:, 4, :], sm[:, 3, :], ALU.add))
            chain(dve.scalar_tensor_tensor(out=sm[:, 4, :], in0=sm[:, 4, :], scalar=-1.0, in1=sm[:, 4, :],
                                           op0=ALU.mult, op1=ALU.max))
            chain(dve.tensor_tensor(hb(sm[:, 4, :]), hb(sm[:, 4, :]), em, ALU.max))
            chain.last(dve.reciprocal(sm[:, 5, :], sm[:, 4, :]))
            chain(dve.tensor_tensor(sm[:, 6, :], sm[:, 6, :], sm[:, 7, :], ALU.add))
            chain(dve.tensor_tensor(sm[:, 6, :], sm[:, 6, :], sm[:, 5, :], ALU.mult))
            signal("sh_ready")
            dve.wait_ge(step("smean_ps"), after("smean_ps"))
            chain(dve.scalar_tensor_tensor(out=sm[:, 6, :], in0=ps[:, 6, 320:352], scalar=-1.0 / DH, in1=sm[:, 6, :],
                                           op0=ALU.mult, op1=ALU.add))
            chain(dve.tensor_tensor(sm[:, 7, :], sm[:, 6, :], sm[:, 6, :], ALU.mult))
            signal("ssq_ready")
            dve.wait_ge(step("srstd_ready"), after("srstd_ready"))
            chain(dve.tensor_tensor(sm[:, 6, :], sm[:, 6, :], sm[:, 8, :], ALU.mult))
            dve.tensor_tensor(featT[:, 0, :, 0:S], hb(sm[:, 6, :]), z[:, O0:O0 + H, SC:ZW], ALU.mult)\
               .then_inc(sem("feat_ready"), 1)
            for b in range(S):
                for h in range(H):
                    dve.wait_ge(sem("c0_scaled"), b * H + h + 1)
                    if h == 0:
                        dve.wait_ge(sem("vB_ps"), b + 1)
                    m = c0[:, b * H + h, :]
                    dve.scalar_tensor_tensor(out=m, in0=ps[:, 4 + b % 2, h * DH:(h + 1) * DH],
                                             scalar=sm[:, 9, h * S + b:h * S + b + 1], in1=m, op0=ALU.mult, op1=ALU.add)\
                       .then_inc(sem("cnew_ready"), 1)

            def tile_x2(i, n):
                b = i % 2
                dve.wait_ge(sem("y_ps"), i + 1)
                if i < 2:
                    dve.wait_ge(sem("bcv_ready"), 3 * (i + 1))
                if i:
                    dve.wait_ge(sem("h2_out"), 16 * i)
                    dve.wait_ge(sem("h2T_ps"), i)
                else:
                    dve.wait_ge(sem("c_out"), 16)
                chain(dve.tensor_tensor(h2[0:n, :], ps[0:n, 6:8, :].rearrange("p b n -> p (b n)"), bcv[0:n, 0, :], ALU.mult))
                dve.wait_ge(sem(f"xr_in{b}"), 16 * (i // 2 + 1))
                dve.tensor_tensor(x2[0:n, b, :], x2[0:n, b, :], h2[0:n, :], ALU.add).then_inc(sem("x2_ready"), 1)
                dve.wait_ge(sem("rs2_ready"), i + 1)

                def dp(ap):
                    return ap.rearrange("t (p k) -> t p k", k=KD)
                hv = h2[0:n, :].rearrange("t (k p) -> t p k", k=KD)
                chain(dve.scalar_tensor_tensor(out=hv, in0=dp(x2[0:n, b, :]), scalar=ssq[0:n, b, 1:2],
                                               in1=dp(bcv[0:n, 1, :]), op0=ALU.mult, op1=ALU.mult))
                dve.tensor_tensor(hv, hv, dp(bcv[0:n, 2, :]), ALU.add).then_inc(sem("h2_ready"), 1)

            def tile_logits(i, n):
                dve.wait_ge(sem("lg_ps"), i + 1)
                t = NT - 1 if i == 0 else i - 1
                dve.wait_ge(sem("wr_in"), 64)
                dve.tensor_tensor(logits[0:n, t, :], ps[0:n, 6, 0:NR], rbias[0:n, :], ALU.add).then_inc(sem("logit_ready"), 1)

            chain(dve.memset(logits[:, :, :], 0.0))
            tile_x2(0, S)
            tile_logits(0, S)
            for c in range(NC_):
                dve.wait_ge(sem("s_ps"), c + 1)
                dve.wait_ge(sem("wx_ready"), 4 * (c + 1))
                if c:
                    dve.wait_ge(sem("num_ps"), c)
                dve.scalar_tensor_tensor(out=sT[:, :, :], in0=ps[:, 0, :].rearrange("p (h t) -> p h t", h=H), scalar=QK,
                                         in1=wx[:, :, :], op0=ALU.mult, op1=ALU.mult).then_inc(sem("sT_ready"), 1)
                dve.wait_ge(sem("k_ps"), c + 1)
                if c:
                    dve.wait_ge(sem("kv_ps"), c)
                dve.scalar_tensor_tensor(out=kw[:, :, :], in0=ps[:, 2, :].rearrange("p (h t) -> p h t", h=H), scalar=QK,
                                         in1=bc(wx[:, :, P - 1:P], DH), op0=ALU.mult, op1=ALU.mult).then_inc(sem("kw_ready"), 1)
                if c:
                    tile_x2(c, P)
                dve.wait_ge(sem("num_ps"), c + 1)
                dve.wait_ge(sem("n2_ready"), 4 * (c + 1))
                dve.tensor_tensor(num[:, :, :].rearrange("p (a h) d -> p a h d", a=2),
                                  ps[:, 4:6, 0:2 * VA].rearrange("p a (h d) -> p a h d", h=2),
                                  n2s[:, :, :].rearrange("p (a h) d -> p a h d", a=2), ALU.add).then_inc(sem("num_ready"), 1)
                dve.wait_ge(sem("kv_ps"), c + 1)
                for h in range(H):
                    dve.scalar_tensor_tensor(out=caug[:, h, :], in0=caug[:, h, :], scalar=dec[:, h, c:c + 1],
                                             in1=ps[:, 2 + h // 2, (h % 2) * VA:(h % 2) * VA + VA],
                                             op0=ALU.mult, op1=ALU.add).then_inc(sem("caug_ready"), 1)
                dve.wait_ge(sem("num_ready"), c + 1)
                chain(dve.scalar_tensor_tensor(out=lst[:, 0, :], in0=num[:, :, DH], scalar=-1.0, in1=num[:, :, DH],
                                               op0=ALU.mult, op1=ALU.max))
                chain(dve.tensor_tensor(lst[:, 0, :], lst[:, 0, :], rowsT[:, c, 64:64 + H], ALU.max))
                chain(dve.reciprocal(lst[:, 1, :], lst[:, 0, :]))
                if c:
                    dve.wait_ge(sem("hT_ps"), c)
                chain(dve.tensor_tensor(hn[:, :, :], num[:, :, 0:DH],
                                        bc(lst[:, 1, :].rearrange("p (h o) -> p h o", o=1), DH), ALU.mult))
                for h in range(H):
                    chain.last(dve.bn_stats(bst[:, h, :], hn[:, h, :]))
                chain.wait()
                for h in range(H):
                    chain.last(dve.bn_aggr(bag[:, h, :], bst[:, h, :]))
                signal("var_ready")
                chain(dve.tensor_tensor(hn[:, :, :], hn[:, :, :], bc(bag[:, :, 0:1], DH), ALU.subtract))
                dve.wait_ge(sem("hrstd_ready"), c + 1)
                dve.tensor_tensor(hn[:, :, :], hn[:, :, :], bc(lst[:, 3, :].rearrange("p (h o) -> p h o", o=1), DH),
                                  ALU.mult).then_inc(sem("hn_ready"), 1)
                if c:
                    tile_logits(c, P)
                dve.wait_ge(sem("hT_ps"), c + 1)
                dve.tensor_tensor(featT[:, (c + 1) % 2, :, :], ps[:, 4, :].rearrange("p (h t) -> p h t", h=H),
                                  z[:, O0:O0 + H, PAD + c * P:PAD + (c + 1) * P], ALU.mult).then_inc(sem("feat_ready"), 1)
            dve.wait_ge(sem("caug_ready"), 1 + H * NC_)
            dve.memset(mark(), 0.0).then_inc(step("mlstm_done"), 1)
            tile_x2(NC_, P)
            tile_logits(NC_, P)
            moe_dve(dve, chain)

        def pe_rest(pe):
            def on_all(h, n):
                return ident[0:n, h:h + 1].broadcast_to([n, P])

            pe.wait_ge(sem("crow_in"), 16)
            pe.wait_ge(sem("z_evac"), NZ + 2)
            pe.wait_ge(step("u_ready"), after("u_ready"))
            for g in range(2):
                for b in range(CB):
                    mm = pe.transpose(ps[:, 2 + g, b * 4 * PAD:(b + 1) * 4 * PAD], crow[:, g, b * P:(b + 1) * P],
                                      ident[0:4 * PAD, 0:4 * PAD])
            mm.then_inc(step("cT_ps"), 1)
            for b in range(CB):
                pe.transpose(ps[0:PAD, TAILS, b * P:(b + 1) * P], z[:, U0 + b, T:SC], ident[:, :])
                mm = pe.transpose(ps[0:S, TAILS + 1, b * P:(b + 1) * P], z[:, U0 + b, SC:ZW], ident[:, :])
            mm.then_inc(step("tails_ps"), 1)

            def channel_sums(first, name):
                for k in range(3):
                    a, n = (PAD + 512 * k, 512) if k < 2 else (SC, S)
                    out = ps[:, MEAN + k, :] if k < 2 else ps[:, 6, 0:S]
                    for b in range(CB):
                        mm = pe.matmul(out, ones[:, :], z[:, first + b, a:a + n], start=(b == 0), stop=(b == CB - 1))
                mm.then_inc(step(name), 1)

            pe.wait_ge(sem("tails_ready"), 2)
            pe.wait_ge(step("conv_sum"), after("conv_sum"))
            channel_sums(GB0, "mean_ps")
            pe.wait_ge(step("squares"), after("squares"))
            channel_sums(U0, "sumsq_ps")
            pe.wait_ge(step("crstd_ready"), after("crstd_ready"))
            pe.wait_ge(step("srow_ready"), after("srow_ready"))
            for c in range(NC_):
                pe.transpose(ps[:, 2 + c // 4, (c % 4) * 72:(c % 4) * 72 + 68], rows_[:, c * P:(c + 1) * P], ident[0:68, 0:68])
            for h in range(H):
                pe.matmul(ps[:, 6, h * NC_:(h + 1) * NC_], on_all(h, H), rows_[0:H, P - 1:T:P], start=True, stop=True)
                mm = pe.matmul(ps[:, 6, 64 + h * 3 * S:64 + (h + 1) * 3 * S], on_all(h, H),
                               srow[:, :, :].rearrange("h f b -> h (f b)"), start=True, stop=True)
            mm.then_inc(step("rowsT_ps"), 1)
            pe.wait_ge(sem("n0_in"), 16)
            pe.transpose(ps[:, 7, 0:S * H], ntok[:, :], ident[0:S * H, 0:S * H]).then_inc(step("n0T_ps"), 1)
            pe.wait_ge(step("sB_ready"), after("sB_ready"))
            for h in range(H):
                mm = pe.transpose(ps[0:S, 2, h * DH:(h + 1) * DH], z[:, V0 + h, SC:ZW], ident[:, :])
            mm.then_inc(step("vtok_ps"), 1)
            pe.wait_ge(step("sprod_ready"), after("sprod_ready"))
            pe.matmul(ps[:, 6, 256:320], ones[:, :], sm[:, 0:2, :].rearrange("p f n -> p (f n)"), start=True, stop=True)\
              .then_inc(step("sdot_ps"), 1)
            pe.wait_ge(sem("c0_in"), 16)
            for b in range(S):
                for h in range(H):
                    mm = pe.matmul(ps[:, 7, 64 + h * S + b:65 + h * S + b], c0[:, b * H + h, :],
                                   z[:, Q0 + h, SC + b:SC + b + 1], start=True, stop=True)
            mm.then_inc(step("qc_ps"), 1)
            pe.wait_ge(step("vtok_ready"), after("vtok_ready"))
            pe.wait_ge(step("snew_ready"), after("snew_ready"))
            pe.transpose(ps[0:S * H, 2, 0:DH], sm[:, 11, :], ident[:, :]).then_inc(step("nnew_ps"), 1)
            pe.wait_ge(step("sh_ready"), after("sh_ready"))
            pe.matmul(ps[:, 6, 320:352], ones[:, :], sm[:, 6, :], start=True, stop=True).then_inc(step("smean_ps"), 1)
            pe.wait_ge(step("ssq_ready"), after("ssq_ready"))
            pe.matmul(ps[:, 6, 384:416], ones[:, :], sm[:, 7, :], start=True, stop=True).then_inc(step("svar_ps"), 1)
            for b in range(S):
                if b >= 2:
                    pe.wait_ge(sem("cnew_ready"), H * (b - 1))
                pe.matmul(ps[:, 4 + b % 2, :], on_all(b, S), vtok[:, :], start=True, stop=True).then_inc(sem("vB_ps"), 1)

            def broadcasts(k):
                for i, (src, at) in enumerate(((modT, 2 * KD), (A2, 0), (modT, 3 * KD))):
                    if i or k:
                        pe.wait_ge(sem("bcv_ready"), 3 * k + i)
                    for q in range(KD):
                        if k == 0:
                            out, lhs = ps[0:S, 6 + q // 4, (q % 4) * P:(q % 4 + 1) * P], src[:, at + q, 1:9]
                        else:
                            out = ps[:, 6 + q // 4, (q % 4) * P:(q % 4 + 1) * P]
                            lhs = src[:, at + q, 0:1].broadcast_to([P, P])
                        mm = pe.matmul(out, lhs, ident[:, :], start=True, stop=True)
                    mm.then_inc(sem("bcv_ps"), 1)

            def out_proj(i, n):
                t = NT - 1 if i == 0 else i - 1
                pe.wait_ge(sem("feat_ready"), i + 1)
                if i < 2:
                    pe.wait_ge(sem("wout_in"), 16)
                    pe.wait_ge(step("conv_done"), after("conv_done"))
                    pe.wait_ge(sem("bcv_ready"), 3 * (i + 1))
                if i:
                    pe.wait_ge(sem("logit_ready"), i)
                for k in range(KD):
                    lhs = featT[:, i % 2, k, 0:n] if k < H else z[:, GB0 + k - H, PAD + t * P:PAD + t * P + n]
                    for a in range(2):
                        mm = pe.matmul(ps[0:n, 6 + a, :], lhs, wout[:, k, a * 512:(a + 1) * 512],
                                       start=(k == 0), stop=(k == KD - 1))
                mm.then_inc(sem("y_ps"), 1)

            def router(i, n):
                pe.wait_ge(sem("h2_ready"), i + 1)
                for k in range(KD):
                    mm = pe.transpose(ps[:, 6 + k // 4, (k % 4) * P:(k % 4) * P + n], h2[0:n, k * P:(k + 1) * P],
                                      ident[0:n, 0:n])
                mm.then_inc(sem("h2T_ps"), 1)
                pe.wait_ge(sem("h2T_ready"), i + 1)
                if i == 0:
                    pe.wait_ge(sem("wr_in"), 64)
                for k in range(KD):
                    mm = pe.matmul(ps[0:n, 6, 0:NR], h2T[:, k, 0:n], wr[:, k, :], start=(k == 0), stop=(k == KD - 1))
                mm.then_inc(sem("lg_ps"), 1)

            broadcasts(0)
            out_proj(0, S)
            router(0, S)
            pe.wait_ge(sem("logit_ready"), 1)
            broadcasts(1)
            pe.wait_ge(sem("caug_ready"), 1)
            for c in range(NC_):
                tok = slice(PAD + c * P, PAD + (c + 1) * P)
                if c:
                    pe.wait_ge(sem("n2_ready"), 4 * c)
                    pe.wait_ge(sem("caug_ready"), 1 + H * c)
                else:
                    pe.wait_ge(step("nnew_ready"), after("nnew_ready"))
                for h in range(H):
                    mm = pe.matmul(ps[:, 0, h * P:(h + 1) * P], z[:, K0 + h, tok], z[:, Q0 + h, tok], start=True, stop=True)
                mm.then_inc(sem("s_ps"), 1)
                pe.matmul(ps[:, 1, :], identb[:, :], causal[:, :].rearrange("p (o n) -> p o n", o=1).broadcast_to([P, H, P]),
                          start=True, stop=False, skip_group_check=True)
                for h in range(H):
                    mm = pe.matmul(ps[:, 1, h * P:(h + 1) * P], on_all(h, H), negM[:, c * P:(c + 1) * P], start=False,
                                   stop=(h == H - 1), skip_group_check=True)
                mm.then_inc(sem("w_ps"), 1)
                for h in range(H):
                    mm = pe.transpose(ps[:, 3, h * P:(h + 1) * P], z[:, V0 + h, tok], ident[:, :])
                mm.then_inc(sem("v_ps"), 1)
                for h in range(H):
                    mm = pe.transpose(ps[:, 2, h * P:(h + 1) * P], z[:, K0 + h, tok], ident[:, :])
                mm.then_inc(sem("k_ps"), 1)
                if c:
                    out_proj(c, P)
                pe.wait_ge(sem("sT_ready"), c + 1)
                for h in range(H):
                    mm = pe.matmul(ps[:, h // 2, (h % 2) * VA:(h % 2) * VA + VA], z[:, Q0 + h, tok], caug[:, h, :],
                                   start=True, stop=True)
                mm.then_inc(sem("n2_ps"), 1)
                pe.wait_ge(sem("vaug_ready"), c + 1)
                if c:
                    pe.wait_ge(sem("feat_ready"), c + 1)
                for h in range(H):
                    mm = pe.matmul(ps[:, 4 + h // 2, (h % 2) * VA:(h % 2) * VA + VA], sT[:, h, :], vaug[:, h, :],
                                   start=True, stop=True)
                mm.then_inc(sem("num_ps"), 1)
                pe.wait_ge(sem("kw_ready"), c + 1)
                for h in range(H):
                    mm = pe.matmul(ps[:, 2 + h // 2, (h % 2) * VA:(h % 2) * VA + VA], kw[:, h, :], vaug[:, h, :],
                                   start=True, stop=True)
                mm.then_inc(sem("kv_ps"), 1)
                if c:
                    router(c, P)
                pe.wait_ge(sem("hn_ready"), c + 1)
                for h in range(H):
                    mm = pe.transpose(ps[:, 4, h * P:(h + 1) * P], hn[:, h, :], ident[:, :])
                mm.then_inc(sem("hT_ps"), 1)
            out_proj(NC_, P)
            router(NC_, P)
            moe_pe(pe)

        PAIRS = NE // 2

        def weights(sp, e, b, free):
            def part(dst, w):
                src = w[bass.ds(e, 1), :, :].rearrange("o (p k) f -> p (o k) f", p=P)
                sp.dma_start(dst, src).then_inc(sem(f"w_in{b}"), 16)

            if free is not None:
                sp.wait_ge(sem("elo_ready"), free)
            part(eraw[:, b, :, 0:FE], w_gate)
            part(eraw[:, b, :, FE:2 * FE], w_up)
            if free is not None:
                sp.wait_ge(sem("dlo_ready"), free)
            part(draw[:, b, :, :], w_down)

        def moe_loads(sp):
            sp.wait_ge(sem("y_ps"), NT)
            for e in range(2):
                weights(sp, e, e, None)
            sp.wait_ge(step("sidx_ready"), after("sidx_ready"))
            sp.wait_ge(sem("list_done"), 16 * 2 * NT)
            sp.dma_start(lists[:, :], list_dram.rearrange("(p m) o -> p (m o)", p=P)).then_inc(sem("lists_in"), 16)
            with sp.Fori(1, PAIRS) as r:
                for b in range(2):
                    weights(sp, r * 2 + b, b, r * 2 - 1 + b)
            sp.wait_ge(step("nov_ready"), after("nov_ready"))
            n = sp.value_load(nov[0:1, 0:1], min_val=0, max_val=NOV)
            with sp.Fori(0, NOV) as j:
                with sp.If(n > j):
                    e = sp.value_load(ovx[0:1, bass.ds(j, 1)], min_val=0, max_val=NE - 1)
                    weights(sp, e, 0, j + NE)
            sp.wait_ge(sem("ye_out0"), n * 16 + 16 * PAIRS)
            sp.wait_ge(sem("ye_out1"), 16 * PAIRS)
            sp.dma_start(fgb[:, :], final_g.rearrange("(o n) -> o n", o=1).broadcast_to([P, D])).then_inc(sem("fg_in"), 16)
            sp.wait_ge(sem("x2_out0"), 16 * 5)
            for t in range(NT):
                b, m = t % 2, rows[t]
                if t >= 2:
                    sp.wait_ge(sem(f"y_out{b}"), 16 * (t // 2))
                sp.dma_start(xf[0:m, b, :], x2_dram[t * P:t * P + m, :]).then_inc(sem(f"xf_in{b}"), 16)
                sp.dma_start(y12[0:m, b, :, :].rearrange("p c n -> p (c n)"),
                             ye_dram[2 * t * P:2 * (t * P + m), :].rearrange("(t c) n -> t (c n)", c=2))\
                  .then_inc(sem(f"y12_in{b}"), 16)
                if t == 0:
                    sp.wait_ge(step("g2b_ready"), after("g2b_ready"))
                if t >= 1:
                    y_out(sp, t - 1)
            y_out(sp, NT - 1)
            for s, v in (("out_done", 16 * 4), ("m_out", 32), ("c_out", 16), ("state_out", 32), ("x2_out1", 16 * 4),
                         ("h2_out", 16 * NT), ("y_out0", 16 * 5), ("y_out1", 16 * 4)):
                sp.wait_ge(sem(s), v)

        def y_out(sp, t):
            sp.wait_ge(sem("of_ready"), t + 1)
            sp.dma_start(y_d[t], of[0:rows[t], t % 2, :]).then_inc(sem(f"y_out{t % 2}"), 16)

        def moe_pool(pool, chain):
            pool.wait_ge(step("lists_zero"), after("lists_zero"))
            pool.dma_start(list_dram.rearrange("(p m) o -> p (m o)", p=P), lists[:, :]).then_inc(sem("list_init"), 16)
            pool.wait_ge(step("stage1_over"), after("stage1_over"))
            pool.iota(ioti[:, :], pattern=[[1, NE]], base=0, channel_multiplier=0).then_inc(step("iota_ready"), 1)
            pool.wait_ge(sem("list_init"), 16)
            pool.wait_ge(step("sidx_ready"), after("sidx_ready"))
            for t in range(NT):
                for c in range(2):
                    pool.indirect_dma_start(
                        out=list_dram, out_offset=bass.IndirectOffsetOnAxis(ap=sidx[0:rows[t], c, t:t + 1], axis=0),
                        in_=tokid[0:rows[t], c, t:t + 1], in_offset=None).then_inc(sem("list_done"), 16)

            def gather(e, b, free):
                if free is not None:
                    pool.wait_ge(sem("xgT_ps"), free)
                pool.tensor_copy(gcur[:, b, :], glists[:, bass.ds(e, 1)]).then_inc(sem("gcur_ready"), 1)
                pool.wait_ge(sem("gcur_ready"), e * 2 + 1)
                pool.tensor_tensor(passed[0:1, 0:1], ones[0:1, 0:1], ones[0:1, 0:1], ALU.add).then_inc(sem("gcur_ready"), 1)
                pool.wait_ge(sem("h2_out"), 16 * NT)
                pool.indirect_dma_start(out=xg[:, b, :], out_offset=None, in_=h2_dram,
                                        in_offset=bass.IndirectOffsetOnAxis(ap=gcur[:, b, :], axis=0),
                                        bounds_check=NTOK - 1, oob_is_err=False).then_inc(sem(f"xg_in{b}"), 16)

            def scatter(e, b, free):
                if free is not None:
                    pool.wait_ge(sem(f"ye_out{b}"), free)
                pool.tensor_copy(scur[:, b, :], lists[:, bass.ds(e, 1)]).then_inc(sem("scur_ready"), 1)
                pool.wait_ge(sem("scur_ready"), e * 2 + 1)
                pool.wait_ge(sem("y_sb"), e * 2 + 2)
                pool.tensor_tensor(passed[0:1, 1:2], ones[0:1, 0:1], ones[0:1, 0:1], ALU.add).then_inc(sem("scur_ready"), 1)
                pool.indirect_dma_start(out=ye_dram, in_=ysb[:, b, :], in_offset=None,
                                        out_offset=bass.IndirectOffsetOnAxis(ap=scur[:, b, :], axis=0),
                                        bounds_check=2 * NTOK - 1, oob_is_err=False).then_inc(sem(f"ye_out{b}"), 16)

            def dlo_part(e, b):
                pool.wait_ge(sem("ehi_ready"), e * 2 + 2)
                pool.tensor_tensor(dlo[:, b, :, :], draw[:, b, :, :], dhi[:, b, :, :].bitcast(F32), ALU.subtract)\
                    .then_inc(sem("dlo_ready"), 1)

            pool.memset(xg[:, :, :], 0.0).then_inc(sem("xg_zero"), 1)
            pool.wait_ge(sem("xg_zero"), 1)
            pool.wait_ge(step("glists_ready"), after("glists_ready"))
            for b in range(2):
                gather(b, b, None)
            dlo_part(0, 0)
            gather(2, 0, 1)
            dlo_part(1, 1)
            gather(3, 1, 2)
            scatter(0, 0, None)
            for b in range(2):
                dlo_part(2 + b, b)
                gather(4 + b, b, 3 + b)
                scatter(1 + b, 1 - b, 16 if b else None)
            with pool.Fori(2, PAIRS - 1) as r:
                for b in range(2):
                    dlo_part(r * 2 + b, b)
                    gather(r * 2 + (b + 2), b, r * 2 + (b + 1))
                    scatter(r * 2 + (b - 1), 1 - b, r * 16 + (16 * b - 16))
            dlo_part(NE - 2, 0)
            scatter(NE - 3, 1, 16 * (PAIRS - 2))
            dlo_part(NE - 1, 1)
            scatter(NE - 2, 0, 16 * (PAIRS - 1))
            scatter(NE - 1, 1, 16 * (PAIRS - 1))
            pool.wait_ge(step("nov_ready"), after("nov_ready"))
            n = pool.value_load(nov[0:1, 0:1], min_val=0, max_val=NOV)
            with pool.Fori(0, NOV) as j:
                with pool.If(n > j):
                    gather(j + NE, 0, j + NE)
                    dlo_part(j + NE, 0)
                    scatter(j + NE, 0, j * 16 + 16 * PAIRS)

        def moe_act(act, chain):
            act.wait_ge(step("gmax_ready"), after("gmax_ready"))
            act.activation(gb_[:, :, :], gb_[:, :, :], ACT.Exp).then_inc(step("gexp_ready"), 1)
            act.wait_ge(step("ediff_ready"), after("ediff_ready"))
            act.activation(r9[:, 5, :], r9[:, 5, :], ACT.Exp).then_inc(step("eexp_ready"), 1)

            def e_hi(e, b, landed, free):
                act.wait_ge(sem(f"w_in{b}"), landed)
                if free is not None:
                    act.wait_ge(sem("gu_ps"), free)
                act.activation(ehi[:, b, :, :], eraw[:, b, :, :], ACT.Copy).then_inc(sem("ehi_ready"), 1)

            def d_hi(e, b, free):
                if free is not None:
                    act.wait_ge(sem("down_ps"), free)
                act.activation(dhi[:, b, :, :], draw[:, b, :, :], ACT.Copy).then_inc(sem("ehi_ready"), 1)

            def x_hi(e, b):
                act.wait_ge(sem("xgT_ps"), e + 1)
                act.activation(xhi[:, b, :, :], ps[:, 0:2, :].rearrange("p a (k n) -> p (a k) n", k=4), ACT.Copy)\
                   .then_inc(sem("xhi_ready"), 1)

            def silu(e):
                act.wait_ge(sem("gu_ps"), e + 1)
                act.activation(gs[:, :], ps[:, 2, 0:FE], ACT.Silu).then_inc(sem("gs_ready"), 1)

            def t_hi(e):
                act.wait_ge(sem("hidT_ps"), e + 1)
                act.activation(thi[:, :, :], ps[:, 3, 0:2 * P].rearrange("p (j n) -> p j n", j=2), ACT.Copy)\
                   .then_inc(sem("thi_ready"), 1)

            def y_copy(e, b, free):
                act.wait_ge(sem("down_ps"), e + 1)
                if free is not None:
                    act.wait_ge(sem(f"ye_out{b}"), free)
                act.activation(ysb[:, b, 0:512], ps[:, 4 + 2 * b, :], ACT.Copy).then_inc(sem("y_sb"), 1)

            act.wait_ge(step("experts_go"), after("experts_go"))
            for b in range(2):
                e_hi(b, b, 48, None)
                d_hi(b, b, None)
            x_hi(0, 0)
            silu(0)
            x_hi(1, 1)
            t_hi(0)

            def expert(e, b, landed, free):
                e_hi(e + 1, 1 - b, landed, e)
                silu(e)
                x_hi(e + 1, 1 - b)
                y_copy(e - 1, 1 - b, free)
                d_hi(e + 1, 1 - b, e)
                t_hi(e)

            for e in (1, 2, 3):
                expert(e, e % 2, 48 * ((e + 1) // 2 + 1), 16 if e == 3 else None)
            with act.Fori(2, PAIRS - 1) as r:
                for b in range(2):
                    expert(r * 2 + b, b, r * 48 + (48 + 48 * b), r * 16 - 16 + 16 * b)
            expert(NE - 2, 0, 48 * PAIRS, 16 * (PAIRS - 2))
            silu(NE - 1)
            y_copy(NE - 2, 0, 16 * (PAIRS - 1))
            t_hi(NE - 1)
            y_copy(NE - 1, 1, 16 * (PAIRS - 1))
            act.wait_ge(step("nov_ready"), after("nov_ready"))
            n = act.value_load(nov[0:1, 0:1], min_val=0, max_val=NOV)
            with act.Fori(0, NOV) as j:
                with act.If(n > j):
                    e_hi(j + NE, 0, j * 48 + 48 * (PAIRS + 1), j + NE)
                    d_hi(j + NE, 0, j + NE)
                    x_hi(j + NE, 0)
                    silu(j + NE)
                    t_hi(j + NE)
                    y_copy(j + NE, 0, j * 16 + 16 * PAIRS)
            act.wait_ge(step("experts_done"), after("experts_done"))
            act.preload_act_table_set(LNEXP)
            for k in range(2):
                act.wait_ge(sem("g2b_ps"), k + 1)
                m = (S, P)[k]
                act.activation(g2b[0:m, 1 - k, :], ps[0:m, 4 + 2 * k:6 + 2 * k, :].rearrange("p b n -> p (b n)"), ACT.Copy)\
                   .then_inc(sem("g2b_copied"), 1)
            act.wait_ge(sem("g2b_copied"), 2)
            act.activation(mark(), epst[0:1, 0:1], ACT.Copy).then_inc(step("g2b_ready"), 1)
            for t in range(NT):
                b, m = t % 2, rows[t]
                act.wait_ge(sem("xsum_ready"), t + 1)
                if t >= 2:
                    act.wait_ge(sem(f"y_out{b}"), 16 * (t // 2))
                chain(act.activation(of[0:m, b, :], xf[0:m, b, :], ACT.Square, accum_out=ssq[0:m, b, 0:1]))
                chain(act.activation(ssq[0:m, b, 1:2], ssq[0:m, b, 0:1], ACT.Ln, bias=epst[0:m, :], scale=1.0 / D))
                act.activation(ssq[0:m, b, 1:2], ssq[0:m, b, 1:2], ACT.Exp, scale=-0.5).then_inc(sem("rf_ready"), 1)

        def moe_dve(dve, chain):
            def signal(name):
                chain.wait()
                dve.memset(mark(), 0.0).then_inc(step(name) if name in STEP else sem(name), 1)

            def by9(ap, n):
                return ap.rearrange("p (t o) -> p t o", o=1).broadcast_to([P, NT, n])

            def cols(ap, n):
                return ap.rearrange("p (o n) -> p o n", o=1).broadcast_to([P, NT, n])

            for s, v in (("state_out", 32), ("x2_out0", 16 * 5), ("x2_out1", 16 * 4), ("h2_out", 16 * NT)):
                dve.wait_ge(sem(s), v)
            signal("stage1_over")
            dve.wait_ge(step("iota_ready"), after("iota_ready"))
            chain(dve.tensor_copy(iot[:, :], ioti[:, :]))
            lg, le = logits[:, :, 0:NG], logits[:, :, NG:NR]

            def first_max(vals, best, tmp, onehot, n):
                chain(dve.tensor_reduce(best, vals, AXX, ALU.max))
                chain(dve.tensor_tensor(tmp, vals, by9(best, n), ALU.is_equal))
                chain(dve.tensor_scalar(tmp, tmp, -float(n), float(n), ALU.mult, ALU.add))
                chain(dve.tensor_tensor(tmp, tmp, cols(iot[:, 0:n], n), ALU.add))
                chain(dve.tensor_reduce(r9[:, 9, :], tmp, AXX, ALU.min))
                chain(dve.tensor_tensor(onehot, cols(iot[:, 0:n], n), by9(r9[:, 9, :], n), ALU.is_equal))

            first_max(lg, r9[:, 0, :], gb_[:, :, :], ga_[:, :, :], NG)
            chain(dve.tensor_tensor(gb_[:, :, :], lg, by9(r9[:, 0, :], NG), ALU.subtract))
            signal("gmax_ready")
            chain(dve.tensor_scalar(ga_[:, :, :], ga_[:, :, :], BIG, -BIG, ALU.mult, ALU.add))
            for g in range(NG):
                chain.last(dve.tensor_tensor(ex[:, :, g * EPG:(g + 1) * EPG], le[:, :, g * EPG:(g + 1) * EPG],
                                             ga_[:, :, g:g + 1].broadcast_to([P, NT, EPG]), ALU.add))
            chain.wait()
            first_max(ex[:, :, :], r9[:, 1, :], et[:, :, :], oh[:, 0, :, :], NE)
            chain(dve.scalar_tensor_tensor(out=ex[:, :, :], in0=oh[:, 0, :, :], scalar=-2 * BIG, in1=ex[:, :, :],
                                           op0=ALU.mult, op1=ALU.add))
            first_max(ex[:, :, :], r9[:, 2, :], et[:, :, :], oh[:, 1, :, :], NE)
            chain(dve.tensor_tensor(r9[:, 5, :], r9[:, 2, :], r9[:, 1, :], ALU.subtract))
            signal("ediff_ready")
            dve.wait_ge(step("gexp_ready"), after("gexp_ready"))
            chain(dve.tensor_reduce(r9[:, 3, :], gb_[:, :, :], AXX, ALU.add))
            dve.wait_ge(step("eexp_ready"), after("eexp_ready"))
            chain(dve.tensor_scalar(r9[:, 6, :], r9[:, 5, :], 1.0, None, ALU.add))
            chain(dve.tensor_tensor(r9[:, 6, :], r9[:, 6, :], r9[:, 3, :], ALU.mult))
            chain(dve.reciprocal(wts[:, 0, :], r9[:, 6, :]))
            chain(dve.tensor_tensor(wts[:, 1, :], wts[:, 0, :], r9[:, 5, :], ALU.mult))
            chain(dve.tensor_tensor(em_[:, :, :], oh[:, 0, :, :], oh[:, 1, :, :], ALU.add))
            chain(dve.tensor_scalar(em_[:, NT - 1, :], em_[:, NT - 1, :], rowmask[:, :], None, ALU.mult))
            signal("mask_ready")
            dve.wait_ge(step("rank_ps"), after("rank_ps"))
            chain.last(dve.memset(tot[:, 0, :], 0.0))
            chain(dve.tensor_copy(pos[:, :, :], ps[:, 1, 0:NT * NE].rearrange("p (t e) -> p t e", t=NT)))
            for t in range(NT):
                chain(dve.tensor_tensor(tot[:, t + 1, :], tot[:, t, :], ps[:, 0, t * NE:(t + 1) * NE], ALU.add))
            chain(dve.tensor_tensor(pos[:, :, :], pos[:, :, :], tot[:, 0:NT, :], ALU.add))
            cnt = tot[:, NT, :]
            for j in range(NT):
                chain.last(dve.tensor_scalar(thr[:, :, j], cnt, float(P * (j + 1)), None, ALU.is_gt))
            chain.wait()
            chain(dve.tensor_reduce(ov[:, 0, :], thr[:, :, :], AXX, ALU.add))
            chain.last(dve.memset(ov[:, 3, :], 0.0))
            chain.wait()
            chain(dve.tensor_tensor_scan(ov[:, 1, :], ov[:, 0, :], ov[:, 3, :], 0.0, ALU.add, ALU.add))
            chain(dve.tensor_tensor(ov[:, 2, :], ov[:, 1, :], ov[:, 0, :], ALU.subtract))
            chain(dve.tensor_tensor(ov[:, 2, :], ov[:, 2, :], iot[:, :], ALU.subtract))
            chain(dve.tensor_scalar(ov[:, 2, :], ov[:, 2, :], float(NE - 1), float(P), ALU.add, ALU.mult))
            chain(dve.tensor_scalar(et[:, :, :], pos[:, :, :], float(P), None, ALU.is_ge))
            chain(dve.tensor_tensor(et[:, :, :], et[:, :, :], cols(ov[:, 2, :], NE), ALU.mult))
            chain(dve.tensor_tensor(et[:, :, :], et[:, :, :], pos[:, :, :], ALU.add))
            chain(dve.tensor_scalar(ov[:, 3, :], iot[:, :], float(P), None, ALU.mult))
            chain(dve.tensor_tensor(et[:, :, :], et[:, :, :], cols(ov[:, 3, :], NE), ALU.add))
            for c in range(2):
                chain(dve.tensor_tensor(oh[:, c, :, :], oh[:, c, :, :], et[:, :, :], ALU.mult))
                chain(dve.tensor_reduce(r9[:, 7 + c, :], oh[:, c, :, :], AXX, ALU.add))
            chain(dve.tensor_copy(slots[:, :, :], r9[:, 7:9, :]))
            chain.last(dve.tensor_scalar(sidx[:, :, :], slots[:, :, :], P - 1, None, ALU.bitwise_and))
            chain(dve.tensor_scalar(sloti[:, :, :], slots[:, :, :], 7, None, ALU.logical_shift_right))
            chain(dve.tensor_scalar(sidx[:, :, :], sidx[:, :, :], MT, None, ALU.mult))
            chain(dve.tensor_tensor(sidx[:, :, :], sidx[:, :, :], sloti[:, :, :], ALU.add))
            signal("sidx_ready")
            for j in range(NOV):
                chain.last(dve.tensor_scalar(ovc[:, j, :], ov[0:1, 1, :], float(j), None, ALU.is_le))
            chain.wait()
            chain(dve.tensor_reduce(ovf[:, 0, :], ovc[:, :, :], AXX, ALU.add))
            chain(dve.tensor_scalar(ovf[:, 0, :], ovf[:, 0, :], float(NE - 1), None, ALU.min))
            chain.last(dve.tensor_copy(ovx[:, :], ovf[:, 0, :]))
            chain.last(dve.tensor_copy(nov[:, :], ov[0:1, 1, NE - 1:NE]))
            signal("nov_ready")
            dve.wait_ge(sem("list_done"), 16 * 2 * NT)
            dve.wait_ge(sem("lists_in"), 16)
            dve.tensor_scalar(glists[:, :], lists[:, :], 1, None, ALU.logical_shift_right).then_inc(step("glists_ready"), 1)
            signal("experts_go")

            def split_lo(e, b):
                dve.wait_ge(sem("ehi_ready"), e * 2 + 1)
                dve.tensor_tensor(elo[:, b, :, :], eraw[:, b, :, :], ehi[:, b, :, :].bitcast(F32), ALU.subtract)\
                   .then_inc(sem("elo_ready"), 1)

            def x_lo(e, b):
                dve.wait_ge(sem("xhi_ready"), e + 1)
                dve.tensor_tensor(xlo[:, b, :, :], ps[:, 0:2, :].rearrange("p a (k n) -> p (a k) n", k=4),
                                  xhi[:, b, :, :].bitcast(F32), ALU.subtract).then_inc(sem("xlo_ready"), 1)

            def hidden(e):
                dve.wait_ge(sem("gs_ready"), e + 1)
                dve.tensor_tensor(hid[:, :].rearrange("t (j p) -> t p j", j=2), gs[:, :].rearrange("t (p j) -> t p j", j=2),
                                  ps[:, 2, FE:2 * FE].rearrange("t (p j) -> t p j", j=2), ALU.mult).then_inc(sem("hid_ready"), 1)

            def t_lo(e):
                dve.wait_ge(sem("thi_ready"), e + 1)
                dve.tensor_tensor(tlo[:, :, :], ps[:, 3, 0:2 * P].rearrange("p (j n) -> p j n", j=2),
                                  thi[:, :, :].bitcast(F32), ALU.subtract).then_inc(sem("tlo_ready"), 1)

            def y_copy(e, b, free):
                dve.wait_ge(sem("down_ps"), e + 1)
                if free is not None:
                    dve.wait_ge(sem(f"ye_out{b}"), free)
                dve.tensor_copy(ysb[:, b, 512:D], ps[:, 5 + 2 * b, :]).then_inc(sem("y_sb"), 1)

            for b in range(2):
                split_lo(b, b)
            x_lo(0, 0)
            hidden(0)
            x_lo(1, 1)
            t_lo(0)

            def expert(e, b, free):
                split_lo(e + 1, 1 - b)
                hidden(e)
                x_lo(e + 1, 1 - b)
                y_copy(e - 1, 1 - b, free)
                t_lo(e)

            for e in (1, 2, 3):
                expert(e, e % 2, 16 if e == 3 else None)
            with dve.Fori(2, PAIRS - 1) as r:
                for b in range(2):
                    expert(r * 2 + b, b, r * 16 - 16 + 16 * b)
            expert(NE - 2, 0, 16 * (PAIRS - 2))
            hidden(NE - 1)
            y_copy(NE - 2, 0, 16 * (PAIRS - 1))
            t_lo(NE - 1)
            y_copy(NE - 1, 1, 16 * (PAIRS - 1))
            n = dve.value_load(nov[0:1, 0:1], min_val=0, max_val=NOV)
            with dve.Fori(0, NOV) as j:
                with dve.If(n > j):
                    split_lo(j + NE, 0)
                    x_lo(j + NE, 0)
                    hidden(j + NE)
                    t_lo(j + NE)
                    y_copy(j + NE, 0, j * 16 + 16 * PAIRS)
            dve.wait_ge(sem("ye_out0"), n * 16 + 16 * PAIRS)
            dve.wait_ge(sem("ye_out1"), 16 * PAIRS)
            dve.memset(mark(), 0.0).then_inc(step("experts_done"), 1)
            dve.wait_ge(step("g2b_ready"), after("g2b_ready"))
            dve.wait_ge(sem("fg_in"), 16)
            for t in range(NT):
                b, m = t % 2, rows[t]
                dve.wait_ge(sem(f"y12_in{b}"), 16 * (t // 2 + 1))
                ya, yb = y12[0:m, b, 0, :], y12[0:m, b, 1, :]
                chain(dve.tensor_scalar(ya, ya, wts[0:m, 0, t:t + 1], None, ALU.mult))
                chain(dve.scalar_tensor_tensor(out=ya, in0=yb, scalar=wts[0:m, 1, t:t + 1], in1=ya, op0=ALU.mult, op1=ALU.add))
                chain(dve.tensor_tensor(ya, ya, g2b[0:m, t // NC_, :], ALU.mult))
                dve.wait_ge(sem(f"xf_in{b}"), 16 * (t // 2 + 1))
                dve.tensor_tensor(xf[0:m, b, :], xf[0:m, b, :], ya, ALU.add).then_inc(sem("xsum_ready"), 1)
                dve.wait_ge(sem("rf_ready"), t + 1)
                dve.scalar_tensor_tensor(out=of[0:m, b, :], in0=xf[0:m, b, :], scalar=ssq[0:m, b, 1:2], in1=fgb[0:m, :],
                                         op0=ALU.mult, op1=ALU.mult).then_inc(sem("of_ready"), 1)

        def moe_pe(pe):
            pe.wait_ge(step("mask_ready"), after("mask_ready"))
            m = em_[:, :, :].rearrange("p t e -> p (t e)")
            pe.matmul(ps[:, 1, 0:NT * NE], ustrict[:, :], m, start=True, stop=True)
            pe.matmul(ps[:, 0, 0:NT * NE], ones[:, :], m, start=True, stop=True).then_inc(step("rank_ps"), 1)

            def x_transpose(e, b, landed):
                pe.wait_ge(sem(f"xg_in{b}"), landed)
                pe.wait_ge(sem("xlo_ready"), e)
                for k in range(KD):
                    mm = pe.transpose(ps[:, k // 4, (k % 4) * P:(k % 4 + 1) * P], xg[:, b, k * P:(k + 1) * P], ident[:, :])
                mm.then_inc(sem("xgT_ps"), 1)

            def gate_up(e, b):
                pe.wait_ge(sem("xlo_ready"), e + 1)
                pe.wait_ge(sem("ehi_ready"), e * 2 + 1)
                pe.wait_ge(sem("elo_ready"), e + 1)
                pe.wait_ge(sem("hid_ready"), e)
                for i, (x, w) in enumerate(((xhi, ehi), (xlo, ehi), (xhi, elo))):
                    for k in range(KD):
                        mm = pe.matmul(ps[:, 2, :], x[:, b, k, :], w[:, b, k, :], start=(i + k == 0),
                                       stop=(i == 2 and k == KD - 1))
                mm.then_inc(sem("gu_ps"), 1)

            def hid_transpose(e):
                pe.wait_ge(sem("hid_ready"), e + 1)
                pe.wait_ge(sem("tlo_ready"), e)
                for j in range(2):
                    mm = pe.transpose(ps[:, 3, j * P:(j + 1) * P], hid[:, j * P:(j + 1) * P], ident[:, :])
                mm.then_inc(sem("hidT_ps"), 1)

            def down(e, b, free):
                pe.wait_ge(sem("tlo_ready"), e + 1)
                pe.wait_ge(sem("dlo_ready"), e + 1)
                if free is not None:
                    pe.wait_ge(sem("y_sb"), free)
                for a in range(2):
                    for i, (x, w) in enumerate(((thi, dhi), (tlo, dhi), (thi, dlo))):
                        for j in range(2):
                            mm = pe.matmul(ps[:, 4 + 2 * b + a, :], x[:, j, :], w[:, b, j, a * 512:(a + 1) * 512],
                                           start=(i + j == 0), stop=(i == 2 and j == 1))
                mm.then_inc(sem("down_ps"), 1)

            pe.wait_ge(step("experts_go"), after("experts_go"))
            x_transpose(0, 0, 16)
            gate_up(0, 0)
            x_transpose(1, 1, 16)
            hid_transpose(0)

            def expert(e, b, landed, free):
                gate_up(e, b)
                x_transpose(e + 1, 1 - b, landed)
                down(e - 1, 1 - b, free)
                hid_transpose(e)

            for e in (1, 2, 3):
                expert(e, e % 2, 16 * ((e + 1) // 2 + 1), 2 if e == 3 else None)
            with pe.Fori(2, PAIRS - 1) as r:
                for b in range(2):
                    expert(r * 2 + b, b, r * 16 + (16 + 16 * b), r * 4 + (2 * b - 4))
            expert(NE - 2, 0, 16 * PAIRS, 2 * (NE - 4))
            gate_up(NE - 1, 1)
            down(NE - 2, 0, 2 * (NE - 3))
            hid_transpose(NE - 1)
            down(NE - 1, 1, 2 * (NE - 2))
            n = pe.value_load(nov[0:1, 0:1], min_val=0, max_val=NOV)
            with pe.Fori(0, NOV) as j:
                with pe.If(n > j):
                    x_transpose(j + NE, 0, j * 16 + 16 * (PAIRS + 1))
                    gate_up(j + NE, 0)
                    hid_transpose(j + NE)
                    down(j + NE, 0, j * 2 + 2 * NE)
            pe.wait_ge(step("experts_done"), after("experts_done"))
            for k in range(2):
                n_ = (S, P)[k]
                for q in range(KD):
                    lhs = modT[:, 5 * KD + q, 1:9] if k == 0 else modT[:, 5 * KD + q, 0:1].broadcast_to([P, P])
                    mm = pe.matmul(ps[0:n_, 4 + 2 * k + q // 4, (q % 4) * P:(q % 4 + 1) * P], lhs, ident[:, :],
                                   start=True, stop=True)
                mm.then_inc(sem("g2b_ps"), 1)

        block = ctx.enter_context(nc.Block())

        @block.sync
        def _(sp):
            def load(dst, src, s):
                sp.dma_start(dst, src).then_inc(sem(s), 16)

            load(c9[0:1, :], c_prompt, "c_in")
            load(c9[1:9, :], c_sample, "c_in")
            for at, n, v in ((0, MB, b_ada), (MB, KD, norm1_g), (MB + KD, KD, norm2_g), (MB + 2 * KD, H, mh_g),
                             (MB + 2 * KD + 4, CB, b_dw), (MB + 2 * KD + 8, CB, cln_g),
                             (MB + 2 * KD + 12, CB, cln_b)):
                load(vecs[at:at + n, :], v if len(v.shape) == 2 else v.rearrange("(b p) -> b p", p=P), "vec_in")
            load(wdw[:, :], w_dw, "vec_in")
            load(bi[:, :], b_ig.rearrange("(h o) -> h o", o=1), "gbias_in")
            load(bf[:, :], b_fg.rearrange("(h o) -> h o", o=1), "gbias_in")
            for n in range(NAG * KD):
                g, k = divmod(n, KD)
                if n >= 4:
                    sp.wait_ge(sem("ada_used"), n - 3)
                load(wada[:, n % 4, :], w_ada[k * P:(k + 1) * P, g * AG:(g + 1) * AG], f"wada_in{n % 4}")
                if n == KD:
                    for t in range(2):
                        load(xt[0:rows[t], t, :], x_d[t], f"x_in{t}")
            load(wgt[:, :, :], w_in_v[:, :, 4 * H * DH:4 * H * DH + 2 * H], "wgt_in")
            for u in range(2):
                load(wraw[:, u, :, :], w_in_v[:, :, C0_CONV + 256 * u:C0_CONV + 256 * (u + 1)], f"wraw_in{u}")
            for t in range(2, NT):
                sp.wait_ge(sem("xn_done"), t - 1)
                load(xt[0:rows[t], t % 2, :], x_d[t], f"x_in{t % 2}")
            for m0_, m1_, col in ((1, CROUNDS, C0_CONV), (CROUNDS, SPLITS, -512 * CROUNDS)):
                with sp.Fori(m0_, m1_) as m:
                    for u in range(2):
                        sp.wait_ge(sem("whi_ready"), m * 4 - 2 + 2 * u)
                        sp.wait_ge(sem("wlo_ready"), m * 4 - 2 + 2 * u)
                        sp.dma_start(wraw[:, u, :, :], w_in_v[:, :, bass.ds(m * 512 + (col + 256 * u), 256)])\
                          .then_inc(sem(f"wraw_in{u}"), 16)
            sp.wait_ge(sem("z_done"), NZ + 3)
            load(crow[:, :, :], cache.rearrange("(g b) w c -> (b w) g c", g=2), "crow_in")
            load(m0t[:, :], m0.rearrange("b h -> h b"), "m0_in")
            load(wout[:, :, :], w_out.rearrange("(k p) n -> p k n", p=P), "wout_in")
            load(wr[:, :, 0:NG], w_grp.rearrange("(p k) n -> p k n", p=P), "wr_in")
            load(wr[:, :, NG:NR], w_er.rearrange("(p k) n -> p k n", p=P), "wr_in")
            load(rbias[:, 0:NG], b_grp.rearrange("(o n) -> o n", o=1).broadcast_to([P, NG]), "wr_in")
            load(rbias[:, NG:NR], b_er.rearrange("(o n) -> o n", o=1).broadcast_to([P, NE]), "wr_in")
            load(conv_s[:, 0:PAD - 1, :], cache[:, 1:PAD, :], "out_done")
            load(ntok[:, :], n0.rearrange("b h d -> (b h) d"), "n0_in")
            sp.wait_ge(step("conv_done"), after("conv_done"))
            load(c0[:, :, :], C0.rearrange("b h d e -> d (b h) e"), "c0_in")
            sp.wait_ge(sem("tails_ready"), 2)
            load(conv_p, utail[:, :], "out_done")
            load(conv_s[:, PAD - 1, :], usam[:, :], "out_done")
            sp.wait_ge(step("srow_ready"), after("srow_ready"))
            load(m_p.rearrange("(h o) -> h o", o=1), mrow[:, T - 1:T], "m_out")
            load(m_s.rearrange("b h -> h b"), mrow[:, T:NTOK], "m_out")
            sp.wait_ge(sem("cnew_ready"), S * H)
            load(C_s.rearrange("b h d e -> d (b h) e"), c0[:, :, :], "c_out")
            sp.wait_ge(step("nnew_ready"), after("nnew_ready"))
            load(n_s.rearrange("b h d -> (b h) d"), ntok[:, :], "out_done")
            for i, t in enumerate([NT - 1] + list(range(NC_))):
                b = i % 2
                if i == 0:
                    sp.wait_ge(sem("c_out"), 16)
                if i >= 2:
                    sp.wait_ge(sem(f"x2_out{b}"), 16 * (i // 2))
                    sp.wait_ge(sem("h2_ready"), i - 1)
                load(x2[0:rows[t], b, :], x_d[t], f"xr_in{b}")
                if i >= 1:
                    store_tile(sp, i - 1)
            store_tile(sp, NT - 1)
            sp.wait_ge(step("mlstm_done"), after("mlstm_done"))
            load(C_p.rearrange("h d e -> d h e"), caug[:, :, 0:DH], "state_out")
            load(n_p.rearrange("h d -> d h"), caug[:, :, DH], "state_out")
            moe_loads(sp)

        @block.gpsimd
        def _(pool):
            chain = Chain(pool, sem("pool_chain"))
            pool.memset(ident[:, :], 0.0).then_inc(sem("pool_chain"), 1)
            pool.memset(identb[:, :], 0.0).then_inc(sem("pool_chain"), 1)
            pool.memset(causal[:, :], 0.0).then_inc(sem("pool_chain"), 1)
            pool.memset(ones[:, :], 1.0).then_inc(sem("pool_chain"), 1)
            chain.n = 4
            chain.wait()
            for m in (ident, identb):
                pool.affine_select(out=m[:, :], in_=m[:, :], compare_op=ALU.not_equal, fill=1.0, base=0,
                                   pattern=[[-1, P]], channel_multiplier=1).then_inc(sem("consts"), 1)
            pool.affine_select(out=causal[:, :], in_=causal[:, :], compare_op=ALU.is_ge, fill=-BIG, base=0,
                               pattern=[[1, P]], channel_multiplier=-1).then_inc(sem("consts"), 1)
            pool.affine_select(out=ustrict[:, :], in_=ones[:, :], compare_op=ALU.is_gt, fill=0.0, base=0,
                               pattern=[[1, P]], channel_multiplier=-1).then_inc(sem("consts"), 1)
            pool.iota(tokid[:, :, :], pattern=[[1, 2], [2 * P, NT]], base=0, channel_multiplier=2).then_inc(sem("consts"), 1)
            for t in range(NT):
                b, n = t % 2, rows[t]
                pool.wait_ge(sem("hhi_done"), t + 1)
                pool.tensor_tensor(hlo[:, :, t * P:t * P + n], hf[:, b, :, 0:n],
                                   hhi[:, :, t * P:t * P + n].bitcast(F32), ALU.subtract).then_inc(sem("hlo_done"), 1)
            def lo(j, u, v):
                pool.wait_ge(sem("whi_ready"), j + 1)
                pool.tensor_tensor(wlo[:, v, :, :], wraw[:, u, :, v * P:(v + 1) * P],
                                   whi[:, v, :, :].bitcast(F32), ALU.subtract).then_inc(sem("wlo_ready"), 1)

            with pool.Fori(0, SPLITS) as m:
                for q in range(4):
                    lo(m * 4 + q, q // 2, q % 2)
            pool.wait_ge(sem("z_done"), NZ + 1)
            chain.last(pool.memset(wlo[:, 0, :, :].bitcast(F32), 0.0))
            chain(pool.memset(whi[:, 0, :, :].bitcast(F32), 0.0))
            pool.memset(mark(), 0.0).then_inc(step("gate_zeroed"), 1)
            pool.wait_ge(sem("whi_ready"), NZ + 2)
            for i in range(2):
                pool.tensor_tensor(wlo[:, 0, :, 32 * i:32 * i + H], wgt[:, :, i * H:(i + 1) * H],
                                   whi[:, 0, :, 32 * i:32 * i + H].bitcast(F32), ALU.subtract)\
                    .then_inc(sem("wlo_ready"), 1)
            moe_pool(pool, chain)

        @block.scalar
        def _(act):
            chain = Chain(act, sem("act_chain"))
            act.wait_ge(sem("c_in"), 32)
            act.activation(c9[:, :], c9[:, :], ACT.Silu).then_inc(step("csilu"), 1)
            for g in range(NAG):
                act.wait_ge(sem("ada_used"), KD * (g + 1))
                if g == 0:
                    act.wait_ge(step("modr_zero"), after("modr_zero"))
                for j in range(4):
                    act.activation(modr[32 * j:32 * j + 9, g, :], ps[32 * j:32 * j + 9, g, :], ACT.Copy)\
                       .then_inc(sem("modr_ready"), 1)

            def stats(t):
                b, n = t % 2, rows[t]
                act.wait_ge(sem(f"x_in{b}"), 16 * (t // 2 + 1))
                if t >= 2:
                    act.wait_ge(sem("xT_done"), t - 1)
                chain(act.activation(xn[0:n, b, :], xt[0:n, b, :], ACT.Square, accum_out=ssq[0:n, b, 0:1]))
                chain(act.activation(ssq[0:n, b, 1:2], ssq[0:n, b, 0:1], ACT.Ln, bias=epst[0:n, :], scale=1.0 / D))
                act.activation(ssq[0:n, b, 1:2], ssq[0:n, b, 1:2], ACT.Exp, scale=-0.5).then_inc(sem("rstd_ready"), 1)

            act.wait_ge(step("dve_consts"), after("dve_consts"))
            act.preload_act_table_set(LNEXP)
            for t in range(NT + 1):
                if t < NT:
                    stats(t)
                if t >= 1:
                    b, n = (t - 1) % 2, rows[t - 1]
                    act.wait_ge(sem("hf_ready"), t)
                    act.activation(hhi[:, :, (t - 1) * P:(t - 1) * P + n], hf[:, b, :, 0:n], ACT.Copy)\
                       .then_inc(sem("hhi_done"), 1)

            def hi(j, u, v, landed):
                act.wait_ge(sem(f"wraw_in{u}"), landed)
                act.wait_ge(sem("z_done"), j + 1)
                act.activation(whi[:, v, :, :], wraw[:, u, :, v * P:(v + 1) * P], ACT.Copy)\
                   .then_inc(sem("whi_ready"), 1)

            def evac(j, at, v):
                act.wait_ge(sem("z_done"), j + 3)
                act.activation(z[:, at, PAD:SC], ps[:, 4 + 2 * v:6 + 2 * v, :].rearrange("p b n -> p (b n)"), ACT.Copy)
                act.activation(z[:, at, SC:ZW], ps[:, v, 0:S], ACT.Copy).then_inc(sem("z_evac"), 1)

            for _ in range(2):
                act.activation(mark(), epst[0:1, 0:1], ACT.Copy).then_inc(sem("z_evac"), 1)
            hi(0, 0, 0, 16)

            def split_rounds(first, end):
                with act.Fori(first, end) as m:
                    for q in range(4):
                        n = q + 1
                        hi(m * 4 + n, (n // 2) % 2, n % 2, m * 16 + (16 if n < 4 else 32))
                        j = m * 4 + q
                        act.wait_ge(sem("z_done"), j + 3)
                        v = q % 2
                        act.activation(z[:, bass.ds(j, 1), PAD:SC].rearrange("p o n -> p (o n)"),
                                       ps[:, 4 + 2 * v:6 + 2 * v, :].rearrange("p b n -> p (b n)"), ACT.Copy)
                        act.activation(z[:, bass.ds(j, 1), SC:ZW].rearrange("p o n -> p (o n)"), ps[:, v, 0:S],
                                       ACT.Copy).then_inc(sem("z_evac"), 1)

            split_rounds(0, CROUNDS)
            act.wait_ge(sem("z_evac"), 2 + 4 * CROUNDS)
            for b in range(CB):
                act.activation(z[:, GB0 + b, PAD:ZW], z[:, GB0 + b, PAD:ZW], ACT.Sigmoid).then_inc(sem("sig_gb"), 1)
            split_rounds(CROUNDS, SPLITS - 1)
            for q in range(3):
                n, m = q + 1, SPLITS - 1
                hi(m * 4 + n, n // 2, n % 2, 16 * (m + 1))
                evac(m * 4 + q, m * 4 + q, q % 2)
            act.wait_ge(step("gate_zeroed"), after("gate_zeroed"))
            act.wait_ge(sem("wgt_in"), 16)
            for i in range(2):
                act.activation(whi[:, 0, :, 32 * i:32 * i + H], wgt[:, :, i * H:(i + 1) * H], ACT.Copy)\
                   .then_inc(sem("whi_ready"), 1)
            evac(NZ - 1, NZ - 1, 1)
            act.wait_ge(sem("z_evac"), NZ + 2)
            for b in range(H):
                act.activation(z[:, O0 + b, PAD:ZW], z[:, O0 + b, PAD:ZW], ACT.Sigmoid).then_inc(sem("sig_o"), 1)
            act_rest(act, chain)

        @block.vector
        def _(dve):
            chain = Chain(dve, sem("dve_chain"))
            dve.memset(modr[:, :, :], 0.0).then_inc(step("modr_zero"), 1)
            dve.memset(epst[:, :], EPS).then_inc(step("dve_consts"), 1)
            dve.memset(lists[:, :], NOTOK).then_inc(step("lists_zero"), 1)
            chain(dve.memset(rowmask[:, :], 0.0))
            chain.last(dve.memset(rowmask[0:S, :], 1.0))
            dve.wait_ge(step("c9T_ps"), after("c9T_ps"))
            dve.tensor_copy(c9T[:, :, :], ps[:, 7, 0:16 * KD].rearrange("p (k r) -> p k r", k=KD)[:, :, 0:9])\
               .then_inc(step("c9T_ready"), 1)
            dve.wait_ge(step("vT_ps"), after("vT_ps"))
            chain.last(dve.tensor_copy(vT[:, :], ps[:, 6, 0:NV]))
            chain(dve.tensor_copy(wdT[:, :, :], ps[:, 6, P:P + 32 * CB].rearrange("p (b w) -> p b w", b=CB)[:, :, 0:CW]))
            for g in range(NAG):
                dve.wait_ge(sem("modT_ps"), g + 1)
                chain(dve.tensor_tensor(
                    modT[:, 16 * g:16 * g + 16, :].rearrange("p (j q) r -> p j q r", j=4),
                    ps[:, 3 + g, :].rearrange("p (q j r) -> p j q r", q=4, j=4)[:, :, :, 0:9],
                    vT[:, 16 * g:16 * g + 16].rearrange("p (j q o) -> p j q o", j=4, o=1).broadcast_to([P, 4, 4, 9]),
                    ALU.add))
            for a, sc, nrm in ((A1, KD, MB), (A2, 4 * KD, MB + KD)):
                last = chain(dve.scalar_tensor_tensor(
                    out=a[:, :, :], in0=modT[:, sc:sc + KD, :], scalar=1.0,
                    in1=vT[:, nrm:nrm + KD].rearrange("p (k o) -> p k o", o=1).broadcast_to([P, KD, 9]),
                    op0=ALU.add, op1=ALU.mult))
            dve.memset(mark(), 0.0).then_inc(step("mod_ready"), 1)
            def xnorm(t):
                b, n = t % 2, rows[t]
                dve.wait_ge(sem("rstd_ready"), t + 1)
                dve.tensor_scalar(xn[0:n, b, :], xt[0:n, b, :], ssq[0:n, b, 1:2], None, ALU.mult)\
                   .then_inc(sem("xn_done"), 1)

            xnorm(0)
            for t in range(NT):
                b, n = t % 2, rows[t]
                if t + 1 < NT:
                    xnorm(t + 1)
                dve.wait_ge(sem("xT_done"), t + 1)
                if t >= 2:
                    dve.wait_ge(sem("hhi_done"), t - 1)
                    dve.wait_ge(sem("hlo_done"), t - 1)
                r = slice(0, 1) if t < NC_ else slice(1, 9)
                src = ps[:, 2 * b:2 * b + 2, :].rearrange("p a (k n) -> p (a k) n", k=4)[:, :, 0:n]
                chain(dve.tensor_tensor(hf[:, b, :, 0:n], src, A1[:, :, r].broadcast_to([P, KD, n]), ALU.mult))
                dve.tensor_tensor(hf[:, b, :, 0:n], hf[:, b, :, 0:n], modT[:, 0:KD, r].broadcast_to([P, KD, n]),
                                  ALU.add).then_inc(sem("hf_ready"), 1)
            dve.wait_ge(sem("z_evac"), 2 + 4 * CROUNDS)
            chain.last(dve.memset(z[:, U0:U0 + CB, 0:PAD], 0.0))
            dve.wait_ge(sem("sig_gb"), CB)
            chain(dve.tensor_tensor(z[:, U0:U0 + CB, PAD:ZW], z[:, U0:U0 + CB, PAD:ZW], z[:, GB0:GB0 + CB, PAD:ZW], ALU.mult))
            dve.memset(mark(), 0.0).then_inc(step("u_ready"), 1)
            for b in range(CB):
                chain.last(dve.tensor_scalar(z[:, GB0 + b, PAD:SC], u_at(b, 0, T), wdT[:, b, 0:1],
                                             vT[:, VB + b:VB + b + 1], ALU.mult, ALU.add))
            n0_ = chain.n
            with dve.Fori(1, CW) as w:
                for b in range(CB):
                    dve.wait_ge(sem("dve_chain"), w * CB + (n0_ - 2 * CB + b + 1))
                    dve.scalar_tensor_tensor(
                        out=z[:, GB0 + b, PAD:SC], in0=z[:, U0 + b, bass.ds(w, T)], scalar=wdT[:, b, bass.ds(w, 1)],
                        in1=z[:, GB0 + b, PAD:SC], op0=ALU.mult, op1=ALU.add).then_inc(sem("dve_chain"), 1)
            chain.n += CB * (CW - 1)
            chain.wait()
            dve_rest(dve, chain)

        @block.tensor
        def _(pe):
            pe.wait_ge(sem("consts"), 5)
            pe.wait_ge(step("csilu"), after("csilu"))
            for k in range(KD):
                mm = pe.transpose(ps[:, 7, 16 * k:16 * k + 9], c9[:, k * P:(k + 1) * P], ident[0:9, 0:9])
            mm.then_inc(step("c9T_ps"), 1)
            pe.wait_ge(sem("vec_in"), 16 * 8)
            pe.transpose(ps[:, 6, 0:NV], vecs[:, :], ident[0:NV, 0:NV])
            for b in range(CB):
                mm = pe.transpose(ps[:, 6, P + 32 * b:P + 32 * b + CW], wdw[:, b * P:(b + 1) * P], ident[0:CW, 0:CW])
            mm.then_inc(step("vT_ps"), 1)
            pe.wait_ge(step("c9T_ready"), after("c9T_ready"))
            for n in range(NAG * KD):
                g, k = divmod(n, KD)
                pe.wait_ge(sem(f"wada_in{n % 4}"), 16 * (n // 4 + 1))
                for j in range(4):
                    mm = pe.matmul(ps[32 * j:32 * j + 9, g, :], c9T[:, k, :], wada[:, n % 4, j * 512:(j + 1) * 512],
                                   start=(k == 0), stop=(k == KD - 1), skip_group_check=True)
                mm.then_inc(sem("ada_used"), 1)
            for g in range(NAG):
                pe.wait_ge(sem("modr_ready"), 4 * g + 4)
                for q in range(4):
                    mm = pe.transpose(ps[:, 3 + g, q * P:(q + 1) * P], modr[:, g, q * P:(q + 1) * P], ident[:, :])
                mm.then_inc(sem("modT_ps"), 1)
            pe.wait_ge(step("mod_ready"), after("mod_ready"))
            for t in range(NT):
                b, n = t % 2, rows[t]
                pe.wait_ge(sem("xn_done"), t + 1)
                if t >= 2:
                    pe.wait_ge(sem("hf_ready"), t - 1)
                for k in range(KD):
                    mm = pe.transpose(ps[:, 2 * b + k // 4, (k % 4) * P:(k % 4) * P + n], xn[0:n, b, k * P:(k + 1) * P],
                                      ident[0:n, 0:n])
                mm.then_inc(sem("xT_done"), 1)
            pe.wait_ge(sem("hf_ready"), NT)
            pe.wait_ge(sem("hlo_done"), NT)
            for _ in range(2):
                mm = pe.matmul(ps[0:1, 7, 0:1], ones[0:1, 0:1], ones[0:1, 0:1], start=True, stop=True)
                mm.then_inc(sem("z_done"), 1)

            def project(j, v, hi_ready, lo_ready):
                pe.wait_ge(sem("whi_ready"), hi_ready)
                pe.wait_ge(sem("wlo_ready"), lo_ready)
                pe.wait_ge(sem("z_evac"), j + 1)
                for k in range(KD):
                    for i, (w, h) in enumerate(((whi, hhi), (whi, hlo), (wlo, hhi))):
                        first, last = k == 0 and i == 0, k == KD - 1 and i == 2
                        for c, out in ((0, ps[:, 4 + 2 * v, :]), (512, ps[:, 5 + 2 * v, :]), (T, ps[:, v, 0:S])):
                            mm = pe.matmul(out, w[:, v, k, :], h[:, k, c:min(c + 512, NTOK)], start=first, stop=last)
                mm.then_inc(sem("z_done"), 1)

            with pe.Fori(0, SPLITS) as m:
                for q in range(4):
                    project(m * 4 + q, q % 2, m * 4 + (q + 1), m * 4 + (q + 1))
            project(NZ, 0, NZ + 2, NZ + 2)
            pe_rest(pe)


_INS = ["x_prompt", "x_sample", "c_prompt", "c_sample", "state_mlstm_C", "state_mlstm_n", "state_mlstm_m", "cache_conv",
        "w_ada", "b_ada", "norm1_g", "w_in", "b_igate", "b_fgate", "mh_norm_g", "w_dw", "b_dw", "conv_ln_g",
        "conv_ln_b", "w_out", "norm2_g", "w_grp_router", "b_grp_router", "w_exp_router", "b_exp_router", "w_gate",
        "w_up", "w_down", "final_g"]
_OUTS = [(1, T, D), (S, 1, D), (1, 1, H, DH, DH), (1, 1, H, DH), (1, 1, H), (1, 1, PAD, CB * P),
         (1, S, H, DH, DH), (1, S, H, DH), (1, S, H), (1, S, PAD, CB * P)]
_NO_DEPTH = {"x_prompt", "x_sample", "c_prompt", "c_sample", "final_g"}


def kernel(**inputs):
    import numpy as _np
    import concourse.bacc as _bacc
    from concourse.bass_utils import run_bass_kernel_spmd as _run

    nc = _bacc.Bacc("TRN2", target_bir_lowering=False, num_devices=1)
    arrays, args = {}, []
    for name in _INS:
        a = _np.ascontiguousarray(inputs[name])
        arrays[f"in_{name}"] = a
        ap = nc.dram_tensor(f"in_{name}", a.shape, mybir.dt.from_np(a.dtype), kind="ExternalInput").ap()
        if name == "w_dw":
            ap = ap[0, :, 0, :]
        elif name not in _NO_DEPTH:
            ap = ap[0]
        args.append(ap)
    outs = []
    for i, shape in enumerate(_OUTS):
        ap = nc.dram_tensor(f"out_{i}", shape, F32, kind="ExternalOutput").ap()
        outs.append(ap if i < 2 else ap[0] if i >= 6 else ap[0, 0])
    build(nc, *args, *outs)
    r = _run(nc, [arrays], core_ids=[0])
    return tuple(r.results[0][f"out_{i}"] for i in range(len(_OUTS)))
```

```python
from contextlib import ExitStack

import concourse.bass as bass
from concourse import mybir

F32 = mybir.dt.float32
F32R = mybir.dt.float32r
BF16 = mybir.dt.bfloat16
I32 = mybir.dt.int32
ALU = mybir.AluOpType
ACT = mybir.ActivationFunctionType
AXX = mybir.AxisListType.X

P = 128
D = 1024
KD = D // P
T = 1024
NC_ = T // P
S = 8
NT = NC_ + 1
NTOK = T + S
TW = NTOK // 3
H = 4
DH = 128
CB = 4
CW = 31
PAD = CW - 1
ZW = PAD + T + S
SC = PAD + T
DIN = 4 * H * DH + 2 * H + 2 * CB * P
EPS = 1e-6
QK = DH ** -0.5
ACC = (6, 7, 6)
TAPS1 = 11
U0, GB0, Q0, K0, V0, O0 = 0, 4, 8, 12, 16, 20
NZ = 24
VA = DH + 2
NG, EPG, NE, FE = 4, 8, 32, 256
NR = NG + NE
NOV = (2 * NTOK) // P
NOTOK = 4095
MT = NE + NOV + 2
BIG = 1.0e30
LNEXP = "natural_log_exp_and_others"
NV = 80
VM, VB, VLG, VLB = 64, 68, 72, 76
AG = 2048
NAG = 6 * D // AG
MB = 6 * D // P


STEPS = {
    "PE": (
        "c9T_ps vT_ps gates_ps rowsT_ps cT_ps tails_ps mean_ps sumsq_ps n0T_ps vtok_ps qc_ps nnew_ps "
        "smean_ps svar_ps rank_ps"),
    "DVE": (
        "modr_zero dve_consts lists_zero c9T_ready u_ready rows_in sB_ready conv_sum centred "
        "conv_scaled snew_ready sh_ready ssq_ready feats_ready mlstm_done stage1_over gmax_ready "
        "ediff_ready mask_ready sidx_ready nov_ready glists_ready experts_go experts_done"),
    "ACT": (
        "csilu softplus_ready srow_ready squares crstd_ready vtok_ready conv_done nnew_ready "
        "srstd_ready gexp_ready eexp_ready g2b_ready"),
    "POOL": (
        "gate_zeroed iota_ready"),
}
STEP = {name: (engine, n + 1) for engine, names in STEPS.items() for n, name in enumerate(names.split())}


class Chain:

    def __init__(self, eng, sem):
        self.eng, self.sem, self.n, self.base = eng, sem, 0, None

    def value(self):
        return self.n if self.base is None else self.base + self.n

    def __call__(self, ins):
        self.n += 1
        ins.then_inc(self.sem, 1)
        self.eng.wait_ge(self.sem, self.value())
        return ins

    def last(self, ins):
        self.n += 1
        ins.then_inc(self.sem, 1)
        return ins

    def wait(self):
        self.eng.wait_ge(self.sem, self.value())


def build(nc, x_prompt, x_sample, c_prompt, c_sample, C0, n0, m0, cache, w_ada, b_ada, norm1_g, w_in,
          b_ig, b_fg, mh_g, w_dw, b_dw, cln_g, cln_b, w_out, norm2_g, w_grp, b_grp, w_er, b_er,
          w_gate, w_up, w_down, final_g,
          y_p, y_s, C_p, n_p, m_p, conv_p, C_s, n_s, m_s, conv_s):
    x_d = [x_prompt[0, t * P:(t + 1) * P, :] for t in range(NC_)] + [x_sample[:, 0, :]]
    y_d = [y_p[0, t * P:(t + 1) * P, :] for t in range(NC_)] + [y_s[:, 0, :]]
    rows = [P] * NC_ + [S]
    x2_dram = nc.dram_tensor("x2_scratch", (NTOK, D), F32, kind="Internal").ap()
    h2_dram = nc.dram_tensor("h2_scratch", (NTOK, D), F32, kind="Internal").ap()
    list_dram = nc.dram_tensor("token_list", (P * MT, 1), I32, kind="Internal").ap()
    ye_dram = nc.dram_tensor("expert_results", (2 * NTOK, D), F32, kind="Internal").ap()

    with ExitStack() as ctx:
        sems = {}

        def sem(name):
            if name not in sems:
                sems[name] = ctx.enter_context(nc.semaphore(name))
            return sems[name]

        def step(name):
            return sem("steps_" + STEP[name][0])

        def after(name):
            return STEP[name][1]

        def once(name):
            return step(name), after(name)

        marks_used = [0]

        def mark():
            marks_used[0] += 1
            return marks[0:1, marks_used[0] - 1:marks_used[0]]

        def sb(scope, name, shape, dt=F32):
            return scope.enter_context(nc.sbuf_tensor(name, shape, dt))

        def both(scope, raw, lo, shape):
            place = ExitStack()
            first = sb(place, raw, shape)
            place.close()
            return first, sb(scope, lo, shape, F32R)

        ctx.enter_context(nc.allow_non_contiguous_dma(reason="vectors of 32 and 512 elements, turned"))
        ps = ctx.enter_context(nc.psum_tensor("ps", [P, 8, 512], F32))

        marks = sb(ctx, "marks", [1, 64])
        rowmask = sb(ctx, "rowmask", [P, 1])
        ident = sb(ctx, "ident", [P, P])
        ones = sb(ctx, "ones", [P, P])
        ustrict = sb(ctx, "ustrict", [P, P])
        identb = sb(ctx, "identb", [P, P], BF16)
        causal = sb(ctx, "causal", [P, P], BF16)
        epst = sb(ctx, "epst", [P, 1])
        vT = sb(ctx, "vT", [P, NV])
        wdT = sb(ctx, "wdT", [P, CB, CW])
        modT = sb(ctx, "modT", [P, MB, 9])
        A1 = sb(ctx, "A1", [P, KD, 9])
        A2 = sb(ctx, "A2", [P, KD, 9])
        bi = sb(ctx, "bi", [H, 1])
        bf = sb(ctx, "bf", [H, 1])
        ssq = sb(ctx, "ssq", [P, 2, 2])
        logits = sb(ctx, "logits", [P, NT, NR])
        wts = sb(ctx, "wts", [P, 2, NT])
        slots = sb(ctx, "slots", [P, 2, NT], I32)
        sidx = sb(ctx, "sidx", [P, 2, NT], I32)
        tokid = sb(ctx, "tokid", [P, 2, NT], I32)
        lists = sb(ctx, "lists", [P, MT], I32)
        glists = sb(ctx, "glists", [P, MT], I32)
        gcur = sb(ctx, "gcur", [P, 2, 1], I32)
        scur = sb(ctx, "scur", [P, 2, 1], I32)
        passed = sb(ctx, "passed", [1, 2])
        ovx = sb(ctx, "ovx", [1, NOV + 2], I32)
        nov = sb(ctx, "nov", [1, 1], I32)

        st1 = ExitStack()
        negM = sb(st1, "negM", [H, T])
        rowsT = sb(st1, "rowsT", [P, NC_, 68])
        dec = sb(st1, "dec", [P, H, NC_])
        srow = sb(st1, "srow", [H, 3, S])
        sB = sb(st1, "sB", [P, H, 3, S])
        m0t = sb(st1, "m0t", [H, S])
        stA = ExitStack()
        c9 = sb(stA, "c9", [9, D])
        vecs = sb(stA, "vecs", [NV, P])
        wdw = sb(stA, "wdw", [CW, CB * P])
        xt = sb(stA, "xt", [P, 2, D])
        xn = sb(stA, "xn", [P, 2, D])
        taken = D + P + CB * P + 4 * D
        sb(stA, "blocks_0_7", [P, 8 * ZW - taken])
        wada = sb(stA, "wada", [P, 8, AG])
        c9T = sb(stA, "c9T", [P, KD, 9])
        modr = sb(stA, "modr", [P, 512])
        stA.close()
        stG = ExitStack()
        sb(stG, "blocks_0_15", [P, 16 * ZW])
        rows_ = sb(stG, "rows", [68, T])
        gi = sb(stG, "gi", [H, NTOK])
        gf = sb(stG, "gf", [H, NTOK])
        gt = sb(stG, "gt", [H, NTOK])
        mrow = sb(stG, "mrow", [H, NTOK])
        brow = sb(stG, "brow", [H, NTOK])
        mprev = sb(stG, "mprev", [H, NC_])
        ghi = sb(stG, "ghi", [P, KD, 32 + H], F32R)
        glo = sb(stG, "glo", [P, KD, 32 + H], F32R)
        stG.close()
        z = sb(st1, "z", [P, NZ, ZW])
        stB = ExitStack()
        hhi = sb(stB, "hhi", [P, KD, NTOK], F32R)
        hf, hlo = both(stB, "hf", "hlo", [P, KD, NTOK])
        wgt = sb(stB, "wgt", [P, KD, 2 * H])
        wraw, wlo = both(stB, "wraw", "wlo", [P, 2, KD, 256])
        whi = sb(stB, "whi", [P, 2, KD, P], F32R)
        stB.close()
        wout = sb(st1, "wout", [P, KD, D])
        wr = sb(st1, "wr", [P, KD, NR])
        rbias = sb(st1, "rbias", [P, NR])
        bcv = sb(st1, "bcv", [P, 3, D])
        sm = sb(st1, "sm", [P, 12, S * H])
        ntok = sb(st1, "ntok", [S * H, DH])
        vtok = sb(st1, "vtok", [S, H * DH])
        utail = sb(st1, "utail", [PAD, CB * P])
        usam = sb(st1, "usam", [S, CB * P])
        kw = sb(st1, "kw", [P, H, DH])
        vaug = sb(st1, "vaug", [P, H, VA])
        wx = sb(st1, "wx", [P, H, P])
        sT = sb(st1, "sT", [P, H, P])
        caug = sb(st1, "caug", [P, H, VA])
        num = sb(st1, "num", [P, H, VA])
        n2s = sb(st1, "n2s", [P, H, VA])
        hn = sb(st1, "hn", [P, H, DH])
        lst = sb(st1, "lst", [P, 5, H])
        bst = sb(st1, "bst", [P, H, 6])
        bag = sb(st1, "bag", [P, H, 2])
        featT = sb(st1, "featT", [P, 2, H, P])
        featS = sb(st1, "featS", [P, H, S])
        stL = ExitStack()
        crow = sb(stL, "crow", [4 * PAD, 2, CB * P])
        crstd = sb(stL, "crstd", [P, NTOK])
        cT = sb(stL, "cT", [P, CB, S, CW])
        cprod = sb(stL, "cprod", [P, CB, S, CW])
        stL.close()
        x2 = sb(st1, "x2", [P, 2, D])
        h2 = sb(st1, "h2", [P, D])
        h2T = sb(st1, "h2T", [P, KD, P])
        st1.close()
        st2 = ExitStack()
        eraw = sb(st2, "eraw", [P, 2, KD, 2 * FE])
        draw = sb(st2, "draw", [P, 2, 2, D])
        ehi = sb(st2, "ehi", [P, 2, KD, 2 * FE], F32R)
        elo = sb(st2, "elo", [P, 2, KD, 2 * FE], F32R)
        dhi = sb(st2, "dhi", [P, 2, 2, D], F32R)
        dlo = sb(st2, "dlo", [P, 2, 2, D], F32R)
        stR = ExitStack()
        iot = sb(stR, "iot", [P, NE])
        ioti = sb(stR, "ioti", [P, NE], I32)
        ga_ = sb(stR, "ga_", [P, NT, NG])
        gb_ = sb(stR, "gb_", [P, NT, NG])
        ex = sb(stR, "ex", [P, NT, NE])
        oh = sb(stR, "oh", [P, 2, NT, NE])
        et = sb(stR, "et", [P, NT, NE])
        em_ = sb(stR, "em_", [P, NT, NE])
        pos = sb(stR, "pos", [P, NT, NE])
        tot = sb(stR, "tot", [P, NT + 1, NE])
        thr = sb(stR, "thr", [P, NE, NT])
        ov = sb(stR, "ov", [P, 4, NE])
        r9 = sb(stR, "r9", [P, 10, NT])
        ovc = sb(stR, "ovc", [1, NOV + 2, NE])
        ovf = sb(stR, "ovf", [1, NOV + 2])
        sloti = sb(stR, "sloti", [P, 2, NT], I32)
        stR.close()
        xg = sb(st2, "xg", [P, 2, D])
        xhi = sb(st2, "xhi", [P, 2, KD, P], F32R)
        xlo = sb(st2, "xlo", [P, 2, KD, P], F32R)
        gs = sb(st2, "gs", [P, FE])
        hid = sb(st2, "hid", [P, FE])
        thi = sb(st2, "thi", [P, 2, P], F32R)
        tlo = sb(st2, "tlo", [P, 2, P], F32R)
        ysb = sb(st2, "ysb", [P, 2, D])
        st2.close()
        st3 = ExitStack()
        y12 = sb(st3, "y12", [P, 2, 2, D])
        xf = sb(st3, "xf", [P, 2, D])
        g2b = sb(st3, "g2b", [P, 2, D])
        fgb = sb(st3, "fgb", [P, D])
        of = sb(st3, "of", [P, 2, D])
        st3.close()

        w_in_v = w_in.rearrange("(k p) n -> p k n", p=P)
        C0_CONV = 4 * H * DH + 2 * H
        SPLITS = NZ // 4
        CROUNDS = 2
        GROUND = 3

        def u_at(blk, w, n):
            return z[:, U0 + blk, w:w + n]

        def store_tile(sp, i):
            t = i
            sp.wait_ge(sem("x2_ready"), i + 1)
            sp.dma_start(x2_dram[t * P:t * P + rows[t], :], x2[0:rows[t], i % 2, :]).then_inc(sem(f"x2_out{i % 2}"), 16)
            sp.wait_ge(sem("h2_ready"), i + 1)
            sp.dma_start(h2_dram[t * P:t * P + rows[t], :], h2[0:rows[t], :]).then_inc(sem("h2_out"), 16)

        def bc(ap, n):
            return ap.broadcast_to([P, H, n])

        def hb(ap):
            return ap.rearrange("p (h b) -> p h b", h=H)

        TAILS, MEAN, YB, BB = 4, 6, 6, (6, 0)

        def c0(b, h):
            return z[:, U0 + b // 2, ((b % 2) * H + h) * DH:((b % 2) * H + h + 1) * DH]


        def bcs(i):
            return z[0:S, U0 + i, 0:D]

        def on_all(h, n):
            return ident[0:n, h:h + 1].broadcast_to([n, P])

        def gate_rows(dve, chain):
            dve.wait_ge(sem("gates_ready"), 2)
            dve.wait_ge(step("softplus_ready"), after("softplus_ready"))
            chain(dve.scalar_tensor_tensor(out=gf[:, :], in0=gf[:, :], scalar=0.0, in1=gt[:, :], op0=ALU.min,
                                           op1=ALU.subtract))
            chain.last(dve.tensor_tensor_scan(mrow[:, 0:T], gf[:, 0:T], gi[:, 0:T], 0.0, ALU.add, ALU.max))
            chain.last(dve.memset(rows_[:, :], 0.0))
            chain(dve.memset(gt[:, :], 0.0))
            for c in range(NC_):
                chain.last(dve.tensor_tensor_scan(brow[:, c * P:(c + 1) * P], gf[:, c * P:(c + 1) * P],
                                                  gt[:, c * P:(c + 1) * P], 0.0, ALU.add, ALU.add))
            chain.last(dve.memset(mprev[:, 0:1], 0.0))
            chain(dve.tensor_copy(mprev[:, 1:NC_], mrow[:, P - 1:T - 1:P]))
            chain(dve.tensor_tensor(negM[:, :], brow[:, 0:T], mrow[:, 0:T], ALU.subtract))
            chain.last(dve.tensor_tensor(rows_[0:H, :].rearrange("h (c t) -> h c t", c=NC_),
                                         negM[:, :].rearrange("h (c t) -> h c t", c=NC_),
                                         mprev[:, :].rearrange("h (c o) -> h c o", o=1).broadcast_to([H, NC_, P]), ALU.add))
            chain(dve.tensor_tensor(gt[:, 0:T], gi[:, 0:T], brow[:, 0:T], ALU.subtract))
            chain.last(dve.tensor_copy(rows_[32:32 + H, :], gt[:, 0:T]))
            chain.last(dve.tensor_copy(rows_[64:64 + H, :], mrow[:, 0:T]))
            dve.wait_ge(sem("m0_in"), 16)
            chain(dve.tensor_tensor(srow[:, 1, :], gf[:, T:NTOK], m0t[:, :], ALU.add))
            chain(dve.tensor_tensor(mrow[:, T:NTOK], srow[:, 1, :], gi[:, T:NTOK], ALU.max))
            chain.last(dve.tensor_tensor(srow[:, 1, :], srow[:, 1, :], mrow[:, T:NTOK], ALU.subtract))
            chain.last(dve.tensor_tensor(srow[:, 0, :], gi[:, T:NTOK], mrow[:, T:NTOK], ALU.subtract))
            chain.last(dve.tensor_scalar(srow[:, 2, :], mrow[:, T:NTOK], -1.0, None, ALU.mult))
            chain.wait()
            dve.memset(mark(), 0.0).then_inc(step("rows_in"), 1)

        def act_rest(act, chain):
            def signal(name):
                chain.wait()
                act.activation(mark(), epst[0:1, 0:1], ACT.Copy).then_inc(step(name) if name in STEP else sem(name), 1)

            act.wait_ge(step("tails_ps"), after("tails_ps"))
            act.activation(utail[:, :], ps[0:PAD, TAILS, :], ACT.Copy).then_inc(sem("tails_ready"), 1)
            act.activation(usam[:, :], ps[0:S, TAILS + 1, :], ACT.Copy).then_inc(sem("tails_ready"), 1)
            act.wait_ge(step("centred"), after("centred"))
            act.activation(z[:, U0:U0 + CB, PAD:ZW], z[:, GB0:GB0 + CB, PAD:ZW], ACT.Square).then_inc(step("squares"), 1)

            def conv_rstd():
                act.wait_ge(step("sumsq_ps"), after("sumsq_ps"))
                chain.last(act.activation(crstd[:, 0:T], ps[:, MEAN:MEAN + 2, :].rearrange("p b n -> p (b n)"), ACT.Ln,
                                          bias=epst[:, :], scale=1.0 / (CB * P)))
                chain(act.activation(crstd[:, T:NTOK], ps[:, 5, 0:S], ACT.Ln, bias=epst[:, :], scale=1.0 / (CB * P)))
                act.activation(crstd[:, :], crstd[:, :], ACT.Exp, scale=-0.5).then_inc(step("crstd_ready"), 1)

            def conv_swish():
                act.wait_ge(step("conv_scaled"), after("conv_scaled"))
                for b in range(CB):
                    chain.last(act.activation(z[:, GB0 + b, PAD:ZW], z[:, GB0 + b, PAD:ZW], ACT.Silu,
                                              scale=vT[:, VLG + b:VLG + b + 1], bias=vT[:, VLB + b:VLB + b + 1]))
                signal("conv_done")
                act.preload_act_table_set(LNEXP)

            def broadcasts(k, out):
                for i in range(3):
                    act.wait_ge(sem("bcv_ps"), 3 * k + i + 1)
                    n = (P, S)[k]
                    act.activation(out(i), ps[0:n, BB[k]:BB[k] + 2, :].rearrange("p b n -> p (b n)"), ACT.Copy)\
                       .then_inc(sem("bcv_ready"), 1)

            def sample_stage(c):
                if c == 0:
                    act.wait_ge(step("vtok_ps"), after("vtok_ps"))
                    act.activation(vtok[:, :], ps[0:S, 1, :], ACT.Copy).then_inc(step("vtok_ready"), 1)
                if c == 2:
                    act.wait_ge(step("nnew_ps"), after("nnew_ps"))
                    act.activation(ntok[:, :], ps[0:S * H, 1, 128:128 + DH], ACT.Copy).then_inc(step("nnew_ready"), 1)
                if c in (2, 3):
                    act.wait_ge(step("qc_ps"), after("qc_ps"))
                    for b in range(4 * c - 8, 4 * c - 4):
                        for h in range(H):
                            act.activation(c0(b, h), c0(b, h), ACT.Copy, scale=sB[:, h, 1, b:b + 1])\
                               .then_inc(sem("c0_scaled"), 1)
                if c == 3:
                    act.wait_ge(step("svar_ps"), after("svar_ps"))
                    chain(act.activation(sm[:, 8, :], ps[:, 0, 384:416], ACT.Ln, bias=epst[:, :], scale=1.0 / DH))
                    act.activation(sm[:, 8, :], sm[:, 8, :], ACT.Exp, scale=-0.5).then_inc(step("srstd_ready"), 1)
                if c == NC_ - 1:
                    act.wait_ge(sem("c_out"), 64)
                    broadcasts(1, bcs)

            def tile_stats(i, n):
                act.wait_ge(sem("x2_ready"), i + 1)
                b = i % 2
                chain(act.activation(h2[0:n, :], x2[0:n, b, :], ACT.Square, accum_out=ssq[0:n, b, 0:1]))
                chain(act.activation(ssq[0:n, b, 1:2], ssq[0:n, b, 0:1], ACT.Ln, bias=epst[0:n, :], scale=1.0 / D))
                act.activation(ssq[0:n, b, 1:2], ssq[0:n, b, 1:2], ACT.Exp, scale=-0.5).then_inc(sem("rs2_ready"), 1)

            def tile_h2T(i, n):
                act.wait_ge(sem("h2T_ps"), i + 1)
                if i:
                    act.wait_ge(sem("lg_ps"), i)
                act.activation(h2T[:, :, 0:n],
                               ps[:, 6:8, :].rearrange("p a (k n) -> p (a k) n", k=4)[:, :, 0:n], ACT.Copy)\
                   .then_inc(sem("h2T_ready"), 1)

            for c in range(NC_):
                act.wait_ge(sem("w_ps"), c + 1)
                if c:
                    act.wait_ge(sem("kw_ready"), c)
                for h in range(H):
                    act.activation(wx[:, h, :], ps[:, 1, h * P:(h + 1) * P], ACT.Exp, bias=rowsT[:, c, 32 + h:33 + h])\
                       .then_inc(sem("wx_ready"), 1)
                act.wait_ge(sem("v_ps"), c + 1)
                if c:
                    act.wait_ge(sem("kv_ps"), c)
                act.activation(vaug[:, :, 0:DH], ps[:, 3, :].rearrange("p (h d) -> p h d", h=H), ACT.Copy)\
                   .then_inc(sem("vaug_ready"), 1)
                act.wait_ge(sem("n2_ps"), c + 1)
                if c:
                    act.wait_ge(sem("num_ready"), c)
                for h in range(H):
                    act.activation(n2s[:, h, :], ps[:, h // 2, (h % 2) * VA:(h % 2) * VA + VA], ACT.Copy,
                                   scale=rowsT[:, c, h:h + 1]).then_inc(sem("n2_ready"), 1)
                if c >= 2:
                    tile_h2T(c - 2, P)
                if c == 0:
                    conv_rstd()
                    broadcasts(0, lambda i: bcv[:, i, :])
                    sample_stage(c)
                act.wait_ge(sem("var_ready"), c + 1)
                chain(act.activation(lst[:, 2, :], bag[:, :, 1], ACT.Ln, bias=epst[:, :]))
                act.activation(lst[:, 3, :], lst[:, 2, :], ACT.Exp, scale=-0.5).then_inc(sem("hrstd_ready"), 1)
                if c == 0:
                    conv_swish()
                else:
                    sample_stage(c)
                if c:
                    tile_stats(c - 1, P)
            tile_h2T(NC_ - 2, P)
            tile_stats(NC_ - 1, P)
            tile_h2T(NC_ - 1, P)
            tile_stats(NC_, S)
            tile_h2T(NC_, S)
            moe_act(act, chain)

        def dve_rest(dve, chain):
            def signal(name):
                chain.wait()
                dve.memset(mark(), 0.0).then_inc(step(name) if name in STEP else sem(name), 1)

            dve.wait_ge(step("rowsT_ps"), after("rowsT_ps"))
            for g in range(2):
                chain.last(dve.tensor_copy(rowsT[:, 4 * g:4 * g + 4, :],
                                           ps[:, 6 + g, 0:4 * 72].rearrange("p (c r) -> p c r", c=4)[:, :, 0:68]))
            chain.last(dve.tensor_copy(dec[:, :, :], ps[:, 6, 300:300 + H * NC_].rearrange("p (h c) -> p h c", h=H)))
            chain.last(dve.tensor_copy(sB[:, :, :, :], ps[:, 7, 300:300 + H * 3 * S].rearrange("p (h f b) -> p h f b", h=H, f=3)))
            signal("sB_ready")
            zc = z[:, GB0:GB0 + CB, :]
            dve.wait_ge(step("cT_ps"), after("cT_ps"))
            for g in range(2):
                chain.last(dve.tensor_copy(
                    cT[:, :, 4 * g:4 * g + 4, 0:PAD],
                    ps[:, 2 + g, 0:4 * 4 * PAD].rearrange("p (k b w) -> p k b w", k=CB, b=4)))
            chain(dve.tensor_copy(cT[:, :, :, PAD], z[:, U0:U0 + CB, SC:ZW]))
            for b in range(CB):
                chain.last(dve.tensor_tensor(cprod[:, b, :, :], cT[:, b, :, :],
                                             wdT[:, b:b + 1, :].broadcast_to([P, S, CW]), ALU.mult))
            chain.wait()
            chain(dve.tensor_reduce(zc[:, :, SC:ZW], cprod[:, :, :, :], AXX, ALU.add))
            chain(dve.tensor_tensor(zc[:, :, SC:ZW], zc[:, :, SC:ZW],
                                    vT[:, VB:VB + CB].rearrange("p (b o) -> p b o", o=1).broadcast_to([P, CB, S]), ALU.add))
            signal("conv_sum")
            dve.wait_ge(step("mean_ps"), after("mean_ps"))
            for k in range(3):
                a, b = (PAD + 512 * k, PAD + 512 * (k + 1)) if k < 2 else (SC, ZW)
                src = ps[:, MEAN + k, :] if k < 2 else ps[:, 5, 0:S]
                n = b - a
                chain.last(dve.scalar_tensor_tensor(
                    out=zc[:, :, a:b], in0=src.rearrange("p (o n) -> p o n", o=1).broadcast_to([P, CB, n]),
                    scalar=-1.0 / (CB * P), in1=zc[:, :, a:b], op0=ALU.mult, op1=ALU.add))
            signal("centred")
            dve.wait_ge(sem("sig_o"), H)
            for h in range(H):
                chain.last(dve.tensor_scalar(z[:, O0 + h, PAD:ZW], z[:, O0 + h, PAD:ZW], vT[:, VM + h:VM + h + 1],
                                             None, ALU.mult))
            chain.last(dve.memset(caug[:, :, :], 0.0))
            chain.last(dve.memset(vaug[:, :, DH:DH + 1], 1.0))
            chain.last(dve.memset(vaug[:, :, DH + 1:VA], 0.0))
            signal("caug_ready")
            def conv_scale():
                dve.wait_ge(step("crstd_ready"), after("crstd_ready"))
                chain(dve.tensor_tensor(zc[:, :, PAD:ZW], zc[:, :, PAD:ZW],
                                        crstd[:, :].rearrange("p (o n) -> p o n", o=1).broadcast_to([P, CB, NTOK]), ALU.mult))
                signal("conv_scaled")

            def sample_stage(c):
                q, k, v = (z[:, o:o + H, SC:ZW] for o in (Q0, K0, V0))
                w_, ai, em = (sB[:, :, f, :] for f in range(3))
                if c == 0:
                    dve.wait_ge(step("n0T_ps"), after("n0T_ps"))
                    n0v = ps[:, 0, 0:S * H].rearrange("p (b h) -> p h b", h=H)
                    chain.last(dve.tensor_tensor(hb(sm[:, 0, :]), q, k, ALU.mult))
                    chain.last(dve.tensor_tensor(hb(sm[:, 1, :]), n0v, q, ALU.mult))
                    chain.last(dve.tensor_copy(hb(sm[:, 2, :]), n0v))
                    chain(dve.scalar_tensor_tensor(out=hb(sm[:, 9, :]), in0=k, scalar=QK, in1=w_, op0=ALU.mult, op1=ALU.mult))
                    chain(dve.tensor_tensor(hb(sm[:, 10, :]), hb(sm[:, 2, :]), ai, ALU.mult))
                    chain(dve.tensor_tensor(sm[:, 11, :].rearrange("p (b h) -> p h b", h=H), hb(sm[:, 10, :]),
                                            hb(sm[:, 9, :]), ALU.add))
                    signal("snew_ready")
                if c == 1:
                    dve.wait_ge(step("qc_ps"), after("qc_ps"))
                    dots = ps[:, 0, 256:320].rearrange("p (f h b) -> p f h b", f=2, h=H)
                    chain.last(dve.scalar_tensor_tensor(out=hb(sm[:, 3, :]), in0=dots[:, 0], scalar=QK, in1=w_,
                                                        op0=ALU.mult, op1=ALU.mult))
                    chain.last(dve.tensor_tensor(hb(sm[:, 4, :]), dots[:, 1], ai, ALU.mult))
                    chain(dve.tensor_tensor(hb(sm[:, 6, :]), ps[:, 1, 64:96].rearrange("p (h b) -> p h b", h=H), ai, ALU.mult))
                    chain.last(dve.tensor_tensor(hb(sm[:, 7, :]), hb(sm[:, 3, :]), v, ALU.mult))
                    chain(dve.tensor_tensor(sm[:, 4, :], sm[:, 4, :], sm[:, 3, :], ALU.add))
                    chain(dve.scalar_tensor_tensor(out=sm[:, 4, :], in0=sm[:, 4, :], scalar=-1.0, in1=sm[:, 4, :],
                                                   op0=ALU.mult, op1=ALU.max))
                    chain(dve.tensor_tensor(hb(sm[:, 4, :]), hb(sm[:, 4, :]), em, ALU.max))
                    chain.last(dve.reciprocal(sm[:, 5, :], sm[:, 4, :]))
                    chain(dve.tensor_tensor(sm[:, 6, :], sm[:, 6, :], sm[:, 7, :], ALU.add))
                    chain(dve.tensor_tensor(sm[:, 6, :], sm[:, 6, :], sm[:, 5, :], ALU.mult))
                    signal("sh_ready")
                if c == 2:
                    dve.wait_ge(step("smean_ps"), after("smean_ps"))
                    chain(dve.scalar_tensor_tensor(out=sm[:, 6, :], in0=ps[:, 0, 320:352], scalar=-1.0 / DH, in1=sm[:, 6, :],
                                                   op0=ALU.mult, op1=ALU.add))
                    chain(dve.tensor_tensor(sm[:, 7, :], sm[:, 6, :], sm[:, 6, :], ALU.mult))
                    signal("ssq_ready")
                if c == 4:
                    dve.wait_ge(step("srstd_ready"), after("srstd_ready"))
                    chain(dve.tensor_tensor(sm[:, 6, :], sm[:, 6, :], sm[:, 8, :], ALU.mult))
                    chain(dve.tensor_tensor(featS[:, :, :], hb(sm[:, 6, :]), z[:, O0:O0 + H, SC:ZW], ALU.mult))
                    signal("feats_ready")
                if c in (3, 4, 5, 6):
                    for b in (2 * c - 6, 2 * c - 5):
                        dve.wait_ge(sem("c0_scaled"), H * (b + 1))
                        dve.wait_ge(sem("vB_ps"), b + 1)
                        for h in range(H):
                            dve.scalar_tensor_tensor(out=c0(b, h), in0=ps[:, b % 2, h * DH:(h + 1) * DH],
                                                     scalar=sm[:, 9, h * S + b:h * S + b + 1], in1=c0(b, h),
                                                     op0=ALU.mult, op1=ALU.add).then_inc(sem("cnew_ready"), 1)

            def tile_x2(i, n):
                b = i % 2
                yb, bc_ = (YB, lambda j: bcv[:, j, :]) if i < NC_ else (0, bcs)
                dve.wait_ge(sem("y_ps"), i + 1)
                if i == 0:
                    dve.wait_ge(sem("bcv_ready"), 3)
                elif i == NC_:
                    dve.wait_ge(sem("bcv_ready"), 6)
                if i:
                    dve.wait_ge(sem("h2_out"), 16 * i)
                    dve.wait_ge(sem("h2T_ps"), i)
                chain(dve.tensor_tensor(h2[0:n, :], ps[0:n, yb:yb + 2, :].rearrange("p b n -> p (b n)"), bc_(0), ALU.mult))
                dve.wait_ge(sem(f"xr_in{b}"), 16 * (i // 2 + 1))
                dve.tensor_tensor(x2[0:n, b, :], x2[0:n, b, :], h2[0:n, :], ALU.add).then_inc(sem("x2_ready"), 1)

            def tile_h2(i, n):
                b = i % 2
                bc_ = (lambda j: bcv[:, j, :]) if i < NC_ else bcs
                dve.wait_ge(sem("rs2_ready"), i + 1)

                def dp(ap):
                    return ap.rearrange("t (p k) -> t p k", k=KD)
                hv = h2[0:n, :].rearrange("t (k p) -> t p k", k=KD)
                chain(dve.scalar_tensor_tensor(out=hv, in0=dp(x2[0:n, b, :]), scalar=ssq[0:n, b, 1:2],
                                               in1=dp(bc_(1)), op0=ALU.mult, op1=ALU.mult))
                dve.tensor_tensor(hv, hv, dp(bc_(2)), ALU.add).then_inc(sem("h2_ready"), 1)

            def tile_logits(i, n):
                dve.wait_ge(sem("lg_ps"), i + 1)
                dve.wait_ge(sem("wr_in"), 64)
                dve.tensor_tensor(logits[0:n, i, :], ps[0:n, 5, 0:NR], rbias[0:n, :], ALU.add).then_inc(sem("logit_ready"), 1)

            chain(dve.memset(logits[:, :, :], 0.0))
            for c in range(NC_):
                dve.wait_ge(sem("s_ps"), c + 1)
                dve.wait_ge(sem("wx_ready"), 4 * (c + 1))
                if c:
                    dve.wait_ge(sem("num_ps"), c)
                dve.scalar_tensor_tensor(out=sT[:, :, :], in0=ps[:, 0, :].rearrange("p (h t) -> p h t", h=H), scalar=QK,
                                         in1=wx[:, :, :], op0=ALU.mult, op1=ALU.mult).then_inc(sem("sT_ready"), 1)
                dve.wait_ge(sem("k_ps"), c + 1)
                if c:
                    dve.wait_ge(sem("kv_ps"), c)
                dve.scalar_tensor_tensor(out=kw[:, :, :], in0=ps[:, 2, :].rearrange("p (h t) -> p h t", h=H), scalar=QK,
                                         in1=bc(wx[:, :, P - 1:P], DH), op0=ALU.mult, op1=ALU.mult).then_inc(sem("kw_ready"), 1)
                if c >= 2:
                    tile_h2(c - 2, P)
                dve.wait_ge(sem("num_ps"), c + 1)
                dve.wait_ge(sem("n2_ready"), 4 * (c + 1))
                dve.tensor_tensor(num[:, :, :].rearrange("p (a h) d -> p a h d", a=2),
                                  ps[:, 4:6, 0:2 * VA].rearrange("p a (h d) -> p a h d", h=2),
                                  n2s[:, :, :].rearrange("p (a h) d -> p a h d", a=2), ALU.add).then_inc(sem("num_ready"), 1)
                dve.wait_ge(sem("kv_ps"), c + 1)
                for h in range(H):
                    dve.scalar_tensor_tensor(out=caug[:, h, :], in0=caug[:, h, :], scalar=dec[:, h, c:c + 1],
                                             in1=ps[:, 2 + h // 2, (h % 2) * VA:(h % 2) * VA + VA],
                                             op0=ALU.mult, op1=ALU.add).then_inc(sem("caug_ready"), 1)
                dve.wait_ge(sem("num_ready"), c + 1)
                chain(dve.scalar_tensor_tensor(out=lst[:, 0, :], in0=num[:, :, DH], scalar=-1.0, in1=num[:, :, DH],
                                               op0=ALU.mult, op1=ALU.max))
                chain(dve.tensor_tensor(lst[:, 0, :], lst[:, 0, :], rowsT[:, c, 64:64 + H], ALU.max))
                chain(dve.reciprocal(lst[:, 1, :], lst[:, 0, :]))
                if c:
                    dve.wait_ge(sem("hT_ps"), c)
                chain(dve.tensor_tensor(hn[:, :, :], num[:, :, 0:DH],
                                        bc(lst[:, 1, :].rearrange("p (h o) -> p h o", o=1), DH), ALU.mult))
                for h in range(H):
                    chain.last(dve.bn_stats(bst[:, h, :], hn[:, h, :]))
                chain.wait()
                for h in range(H):
                    chain.last(dve.bn_aggr(bag[:, h, :], bst[:, h, :]))
                signal("var_ready")
                chain(dve.tensor_tensor(hn[:, :, :], hn[:, :, :], bc(bag[:, :, 0:1], DH), ALU.subtract))
                dve.wait_ge(sem("hrstd_ready"), c + 1)
                dve.tensor_tensor(hn[:, :, :], hn[:, :, :], bc(lst[:, 3, :].rearrange("p (h o) -> p h o", o=1), DH),
                                  ALU.mult).then_inc(sem("hn_ready"), 1)
                if c == 0:
                    conv_scale()
                if c >= 2:
                    tile_logits(c - 2, P)
                sample_stage(c)
                dve.wait_ge(sem("hT_ps"), c + 1)
                if c >= 2:
                    dve.wait_ge(sem("y_ps"), c - 1)
                dve.tensor_tensor(featT[:, c % 2, :, :], ps[:, 4, :].rearrange("p (h t) -> p h t", h=H),
                                  z[:, O0:O0 + H, PAD + c * P:PAD + (c + 1) * P], ALU.mult).then_inc(sem("feat_ready"), 1)
                if c:
                    tile_x2(c - 1, P)
            dve.wait_ge(sem("caug_ready"), 1 + H * NC_)
            dve.memset(mark(), 0.0).then_inc(step("mlstm_done"), 1)
            tile_h2(NC_ - 2, P)
            tile_logits(NC_ - 2, P)
            for i, n in ((NC_ - 1, P), (NC_, S)):
                tile_x2(i, n)
                tile_h2(i, n)
                tile_logits(i, n)
            moe_dve(dve, chain)

        def pe_rest(pe):
            pe.wait_ge(sem("crow_in"), 16)
            pe.wait_ge(sem("z_evac"), NZ + 2)
            pe.wait_ge(step("u_ready"), after("u_ready"))
            pe.wait_ge(step("sB_ready"), after("sB_ready"))
            for g in range(2):
                for b in range(CB):
                    mm = pe.transpose(ps[:, 2 + g, b * 4 * PAD:(b + 1) * 4 * PAD], crow[:, g, b * P:(b + 1) * P],
                                      ident[0:4 * PAD, 0:4 * PAD])
            mm.then_inc(step("cT_ps"), 1)
            for b in range(CB):
                pe.transpose(ps[0:PAD, TAILS, b * P:(b + 1) * P], z[:, U0 + b, T:SC], ident[:, :])
                mm = pe.transpose(ps[0:S, TAILS + 1, b * P:(b + 1) * P], z[:, U0 + b, SC:ZW], ident[:, :])
            mm.then_inc(step("tails_ps"), 1)

            def channel_sums(first, name):
                for k in range(3):
                    a, n = (PAD + 512 * k, 512) if k < 2 else (SC, S)
                    out = ps[:, MEAN + k, :] if k < 2 else ps[:, 5, 0:S]
                    for b in range(CB):
                        mm = pe.matmul(out, ones[:, :], z[:, first + b, a:a + n], start=(b == 0), stop=(b == CB - 1))
                mm.then_inc(step(name), 1)

            pe.wait_ge(sem("tails_ready"), 2)
            pe.wait_ge(step("conv_sum"), after("conv_sum"))
            channel_sums(GB0, "mean_ps")

            def broadcasts(k):
                for i, (src, at) in enumerate(((modT, 2 * KD), (A2, 0), (modT, 3 * KD))):
                    if i:
                        pe.wait_ge(sem("bcv_ready"), 3 * k + i)
                    for q in range(KD):
                        if k == 0:
                            out = ps[:, BB[0] + q // 4, (q % 4) * P:(q % 4 + 1) * P]
                            lhs = src[:, at + q, 0:1].broadcast_to([P, P])
                        else:
                            out, lhs = ps[0:S, BB[1] + q // 4, (q % 4) * P:(q % 4 + 1) * P], src[:, at + q, 1:9]
                        mm = pe.matmul(out, lhs, ident[:, :], start=True, stop=True)
                    mm.then_inc(sem("bcv_ps"), 1)

            def sample_stage(c):
                pe.wait_ge(sem("n2_ready"), 4 * (c + 1))
                if c == 0:
                    pe.wait_ge(sem("n0_in"), 16)
                    pe.transpose(ps[:, 0, 0:S * H], ntok[:, :], ident[0:S * H, 0:S * H]).then_inc(step("n0T_ps"), 1)
                    for h in range(H):
                        mm = pe.transpose(ps[0:S, 1, h * DH:(h + 1) * DH], z[:, V0 + h, SC:ZW], ident[:, :])
                    mm.then_inc(step("vtok_ps"), 1)
                if c == 1:
                    pe.matmul(ps[:, 0, 256:320], ones[:, :], sm[:, 0:2, :].rearrange("p f n -> p (f n)"), start=True, stop=True)
                    pe.wait_ge(sem("c0_in"), 64)
                    for b in range(S):
                        for h in range(H):
                            mm = pe.matmul(ps[:, 1, 64 + h * S + b:65 + h * S + b], c0(b, h),
                                           z[:, Q0 + h, SC + b:SC + b + 1], start=True, stop=True)
                    mm.then_inc(step("qc_ps"), 1)
                if c == 2:
                    pe.transpose(ps[0:S * H, 1, 128:128 + DH], sm[:, 11, :], ident[:, :]).then_inc(step("nnew_ps"), 1)
                    pe.matmul(ps[:, 0, 320:352], ones[:, :], sm[:, 6, :], start=True, stop=True).then_inc(step("smean_ps"), 1)
                if c == 3:
                    pe.matmul(ps[:, 0, 384:416], ones[:, :], sm[:, 7, :], start=True, stop=True).then_inc(step("svar_ps"), 1)
                if c in (3, 4, 5, 6):
                    for b in (2 * c - 6, 2 * c - 5):
                        if c == 3:
                            pe.wait_ge(step("srstd_ready"), after("srstd_ready"))
                        pe.matmul(ps[:, b % 2, :], on_all(b, S), vtok[:, :], start=True, stop=True)\
                          .then_inc(sem("vB_ps"), 1)
                if c == NC_ - 1:
                    broadcasts(1)

            sample_read = {0: (once("vtok_ready"), once("snew_ready")), 1: (once("sh_ready"),),
                           2: (once("nnew_ready"), once("ssq_ready")), 3: ((sem("cnew_ready"), 2 * H),),
                           4: ((sem("cnew_ready"), 4 * H),), 5: ((sem("cnew_ready"), 6 * H),),
                           6: ((sem("cnew_ready"), 8 * H),)}

            def out_proj(i, n):
                if i < NC_:
                    pe.wait_ge(sem("feat_ready"), i + 1)
                if i == 0:
                    pe.wait_ge(sem("wout_in"), 16)
                    pe.wait_ge(step("conv_done"), after("conv_done"))
                if i == NC_:
                    pe.wait_ge(step("feats_ready"), after("feats_ready"))
                    pe.wait_ge(sem("bcv_ready"), 6)
                bank = YB if i < NC_ else 0
                for k in range(KD):
                    if k >= H:
                        lhs = z[:, GB0 + k - H, PAD + i * P:PAD + i * P + n]
                    else:
                        lhs = featT[:, i % 2, k, :] if i < NC_ else featS[:, k, :]
                    for a in range(2):
                        mm = pe.matmul(ps[0:n, bank + a, :], lhs, wout[:, k, a * 512:(a + 1) * 512],
                                       start=(k == 0), stop=(k == KD - 1))
                mm.then_inc(sem("y_ps"), 1)

            def h2_transpose(i, n):
                pe.wait_ge(sem("h2_ready"), i + 1)
                for k in range(KD):
                    mm = pe.transpose(ps[:, 6 + k // 4, (k % 4) * P:(k % 4) * P + n], h2[0:n, k * P:(k + 1) * P],
                                      ident[0:n, 0:n])
                mm.then_inc(sem("h2T_ps"), 1)

            def router(i, n):
                pe.wait_ge(sem("h2T_ready"), i + 1)
                if i + 2 < NC_:
                    pe.wait_ge(sem("num_ready"), i + 3)
                elif i:
                    pe.wait_ge(sem("logit_ready"), i)
                if i == 0:
                    pe.wait_ge(sem("wr_in"), 64)
                for k in range(KD):
                    mm = pe.matmul(ps[0:n, 5, 0:NR], h2T[:, k, 0:n], wr[:, k, :], start=(k == 0), stop=(k == KD - 1))
                mm.then_inc(sem("lg_ps"), 1)

            pe.wait_ge(sem("caug_ready"), 1)
            for c in range(NC_):
                tok = slice(PAD + c * P, PAD + (c + 1) * P)
                if c:
                    for reader, count in sample_read[c - 1]:
                        pe.wait_ge(reader, count)
                    pe.wait_ge(sem("n2_ready"), 4 * c)
                    pe.wait_ge(sem("caug_ready"), 1 + H * c)
                for h in range(H):
                    mm = pe.matmul(ps[:, 0, h * P:(h + 1) * P], z[:, K0 + h, tok], z[:, Q0 + h, tok], start=True, stop=True)
                mm.then_inc(sem("s_ps"), 1)
                pe.matmul(ps[:, 1, :], identb[:, :], causal[:, :].rearrange("p (o n) -> p o n", o=1).broadcast_to([P, H, P]),
                          start=True, stop=False, skip_group_check=True)
                for h in range(H):
                    mm = pe.matmul(ps[:, 1, h * P:(h + 1) * P], on_all(h, H), negM[:, c * P:(c + 1) * P], start=False,
                                   stop=(h == H - 1), skip_group_check=True)
                mm.then_inc(sem("w_ps"), 1)
                for h in range(H):
                    mm = pe.transpose(ps[:, 3, h * P:(h + 1) * P], z[:, V0 + h, tok], ident[:, :])
                mm.then_inc(sem("v_ps"), 1)
                for h in range(H):
                    mm = pe.transpose(ps[:, 2, h * P:(h + 1) * P], z[:, K0 + h, tok], ident[:, :])
                mm.then_inc(sem("k_ps"), 1)
                if c == 0:
                    pe.wait_ge(step("squares"), after("squares"))
                    channel_sums(U0, "sumsq_ps")
                pe.wait_ge(sem("sT_ready"), c + 1)
                for h in range(H):
                    mm = pe.matmul(ps[:, h // 2, (h % 2) * VA:(h % 2) * VA + VA], z[:, Q0 + h, tok], caug[:, h, :],
                                   start=True, stop=True)
                mm.then_inc(sem("n2_ps"), 1)
                pe.wait_ge(sem("vaug_ready"), c + 1)
                if c:
                    pe.wait_ge(sem("feat_ready"), c)
                    if c >= 3:
                        pe.wait_ge(sem("logit_ready"), c - 2)
                else:
                    pe.wait_ge(step("crstd_ready"), after("crstd_ready"))
                for h in range(H):
                    mm = pe.matmul(ps[:, 4 + h // 2, (h % 2) * VA:(h % 2) * VA + VA], sT[:, h, :], vaug[:, h, :],
                                   start=True, stop=True)
                mm.then_inc(sem("num_ps"), 1)
                pe.wait_ge(sem("kw_ready"), c + 1)
                for h in range(H):
                    mm = pe.matmul(ps[:, 2 + h // 2, (h % 2) * VA:(h % 2) * VA + VA], kw[:, h, :], vaug[:, h, :],
                                   start=True, stop=True)
                mm.then_inc(sem("kv_ps"), 1)
                if c >= 2:
                    h2_transpose(c - 2, P)
                if c == 0:
                    broadcasts(0)
                sample_stage(c)
                if c >= 2:
                    router(c - 2, P)
                elif c:
                    pe.wait_ge(sem("bcv_ready"), 3)
                if c:
                    out_proj(c - 1, P)
                pe.wait_ge(sem("hn_ready"), c + 1)
                for h in range(H):
                    mm = pe.transpose(ps[:, 4, h * P:(h + 1) * P], hn[:, h, :], ident[:, :])
                mm.then_inc(sem("hT_ps"), 1)
            h2_transpose(NC_ - 2, P)
            router(NC_ - 2, P)
            out_proj(NC_ - 1, P)
            out_proj(NC_, S)
            h2_transpose(NC_ - 1, P)
            router(NC_ - 1, P)
            h2_transpose(NC_, S)
            router(NC_, S)
            moe_pe(pe)

        PAIRS = NE // 2

        def weights(sp, e, b, free):
            def part(dst, w):
                src = w[bass.ds(e, 1), :, :].rearrange("o (p k) f -> p (o k) f", p=P)
                sp.dma_start(dst, src).then_inc(sem(f"w_in{b}"), 16)

            if free is not None:
                sp.wait_ge(sem("elo_ready"), free)
            part(eraw[:, b, :, 0:FE], w_gate)
            part(eraw[:, b, :, FE:2 * FE], w_up)
            if free is not None:
                sp.wait_ge(sem("dlo_ready"), free)
            part(draw[:, b, :, :], w_down)

        def moe_loads(sp):
            sp.wait_ge(sem("h2_ready"), NT)
            for e in range(2):
                weights(sp, e, e, None)
            sp.wait_ge(step("sidx_ready"), after("sidx_ready"))
            sp.wait_ge(sem("list_done"), 16 * 2 * NT)
            sp.dma_start(lists[:, :], list_dram.rearrange("(p m) o -> p (m o)", p=P)).then_inc(sem("lists_in"), 16)
            with sp.Fori(1, PAIRS) as r:
                for b in range(2):
                    weights(sp, r * 2 + b, b, r * 2 - 1 + b)
            def further(j, b, free):
                e = sp.value_load(ovx[0:1, bass.ds(j, 1)], min_val=0, max_val=NE - 1)
                weights(sp, e, b, free)

            sp.wait_ge(step("nov_ready"), after("nov_ready"))
            np_ = sp.value_load(nov[0:1, 0:1], min_val=0, max_val=NOV // 2)
            further(0, 0, NE - 1)
            with sp.Fori(PAIRS, PAIRS + NOV // 2) as r:
                with sp.If(np_ + PAIRS > r):
                    for b in range(2):
                        further(r * 2 + (b + 1 - NE), 1 - b, r * 2 + b)
            sp.wait_ge(step("experts_done"), after("experts_done"))
            sp.dma_start(fgb[:, :], final_g.rearrange("(o n) -> o n", o=1).broadcast_to([P, D])).then_inc(sem("fg_in"), 16)
            sp.wait_ge(sem("x2_out0"), 16 * 5)
            for t in range(NT):
                b, m = t % 2, rows[t]
                if t >= 2:
                    sp.wait_ge(sem(f"y_out{b}"), 16 * (t // 2))
                sp.dma_start(xf[0:m, b, :], x2_dram[t * P:t * P + m, :]).then_inc(sem(f"xf_in{b}"), 16)
                sp.dma_start(y12[0:m, b, :, :].rearrange("p c n -> p (c n)"),
                             ye_dram[2 * t * P:2 * (t * P + m), :].rearrange("(t c) n -> t (c n)", c=2))\
                  .then_inc(sem(f"y12_in{b}"), 16)
                if t == 0:
                    sp.wait_ge(step("g2b_ready"), after("g2b_ready"))
                if t >= 1:
                    y_out(sp, t - 1)
            y_out(sp, NT - 1)
            for s, v in (("out_done", 16 * 4), ("m_out", 32), ("c_out", 64), ("state_out", 32), ("x2_out1", 16 * 4),
                         ("h2_out", 16 * NT), ("y_out0", 16 * 5), ("y_out1", 16 * 4)):
                sp.wait_ge(sem(s), v)

        def y_out(sp, t):
            sp.wait_ge(sem("of_ready"), t + 1)
            sp.dma_start(y_d[t], of[0:rows[t], t % 2, :]).then_inc(sem(f"y_out{t % 2}"), 16)

        def moe_pool(pool, chain):
            pool.wait_ge(step("lists_zero"), after("lists_zero"))
            pool.dma_start(list_dram.rearrange("(p m) o -> p (m o)", p=P), lists[:, :]).then_inc(sem("list_init"), 16)
            pool.wait_ge(step("stage1_over"), after("stage1_over"))
            pool.iota(ioti[:, :], pattern=[[1, NE]], base=0, channel_multiplier=0).then_inc(step("iota_ready"), 1)
            pool.wait_ge(sem("list_init"), 16)
            pool.wait_ge(step("sidx_ready"), after("sidx_ready"))
            for t in range(NT):
                for c in range(2):
                    pool.indirect_dma_start(
                        out=list_dram, out_offset=bass.IndirectOffsetOnAxis(ap=sidx[0:rows[t], c, t:t + 1], axis=0),
                        in_=tokid[0:rows[t], c, t:t + 1], in_offset=None).then_inc(sem("list_done"), 16)

            def gather(e, b, free):
                if free is not None:
                    pool.wait_ge(sem("xgT_ps"), free)
                pool.tensor_copy(gcur[:, b, :], glists[:, bass.ds(e, 1)]).then_inc(sem("gcur_ready"), 1)
                pool.wait_ge(sem("gcur_ready"), e * 2 + 1)
                pool.tensor_tensor(passed[0:1, 0:1], ones[0:1, 0:1], ones[0:1, 0:1], ALU.add).then_inc(sem("gcur_ready"), 1)
                pool.wait_ge(sem("h2_out"), 16 * NT)
                pool.indirect_dma_start(out=xg[:, b, :], out_offset=None, in_=h2_dram,
                                        in_offset=bass.IndirectOffsetOnAxis(ap=gcur[:, b, :], axis=0),
                                        bounds_check=NTOK - 1, oob_is_err=False).then_inc(sem(f"xg_in{b}"), 16)

            def scatter(e, b, free):
                if free is not None:
                    pool.wait_ge(sem(f"ye_out{b}"), free)
                pool.tensor_copy(scur[:, b, :], lists[:, bass.ds(e, 1)]).then_inc(sem("scur_ready"), 1)
                pool.wait_ge(sem("scur_ready"), e * 2 + 1)
                pool.wait_ge(sem("y_sb"), e * 2 + 2)
                pool.tensor_tensor(passed[0:1, 1:2], ones[0:1, 0:1], ones[0:1, 0:1], ALU.add).then_inc(sem("scur_ready"), 1)
                pool.indirect_dma_start(out=ye_dram, in_=ysb[:, b, :], in_offset=None,
                                        out_offset=bass.IndirectOffsetOnAxis(ap=scur[:, b, :], axis=0),
                                        bounds_check=2 * NTOK - 1, oob_is_err=False).then_inc(sem(f"ye_out{b}"), 16)

            def dlo_part(e, b):
                pool.wait_ge(sem("ehi_ready"), e * 2 + 2)
                pool.tensor_tensor(dlo[:, b, :, :], draw[:, b, :, :], dhi[:, b, :, :].bitcast(F32), ALU.subtract)\
                    .then_inc(sem("dlo_ready"), 1)

            pool.memset(xg[:, :, :], 0.0).then_inc(sem("xg_zero"), 1)
            pool.wait_ge(sem("xg_zero"), 1)
            pool.wait_ge(step("glists_ready"), after("glists_ready"))
            for b in range(2):
                gather(b, b, None)
            dlo_part(0, 0)
            gather(2, 0, 1)
            dlo_part(1, 1)
            gather(3, 1, 2)
            scatter(0, 0, None)
            for b in range(2):
                dlo_part(2 + b, b)
                gather(4 + b, b, 3 + b)
                scatter(1 + b, 1 - b, 16 if b else None)
            def expert(e, b, free):
                dlo_part(e, b)
                gather(e + 2, b, e + 1)
                scatter(e - 1, 1 - b, free)

            with pool.Fori(2, PAIRS) as r:
                for b in range(2):
                    expert(r * 2 + b, b, r * 16 + (16 * b - 16))
            pool.wait_ge(step("nov_ready"), after("nov_ready"))
            np_ = pool.value_load(nov[0:1, 0:1], min_val=0, max_val=NOV // 2)
            with pool.Fori(PAIRS, PAIRS + NOV // 2) as r:
                with pool.If(np_ + PAIRS > r):
                    for b in range(2):
                        expert(r * 2 + b, b, r * 16 + (16 * b - 16))
            scatter(np_ * 2 + (NE - 1), 1, np_ * 16 + 16 * (PAIRS - 1))

        def moe_act(act, chain):
            act.wait_ge(step("gmax_ready"), after("gmax_ready"))
            act.activation(gb_[:, :, :], gb_[:, :, :], ACT.Exp).then_inc(step("gexp_ready"), 1)
            act.wait_ge(step("ediff_ready"), after("ediff_ready"))
            act.activation(r9[:, 5, :], r9[:, 5, :], ACT.Exp).then_inc(step("eexp_ready"), 1)

            def e_hi(e, b, landed, free):
                act.wait_ge(sem(f"w_in{b}"), landed)
                if free is not None:
                    act.wait_ge(sem("gu_ps"), free)
                act.activation(ehi[:, b, :, :], eraw[:, b, :, :], ACT.Copy).then_inc(sem("ehi_ready"), 1)

            def d_hi(e, b, free):
                if free is not None:
                    act.wait_ge(sem("down_ps"), free)
                act.activation(dhi[:, b, :, :], draw[:, b, :, :], ACT.Copy).then_inc(sem("ehi_ready"), 1)

            def x_hi(e, b):
                act.wait_ge(sem("xgT_ps"), e + 1)
                act.activation(xhi[:, b, :, :], ps[:, 0:2, :].rearrange("p a (k n) -> p (a k) n", k=4), ACT.Copy)\
                   .then_inc(sem("xhi_ready"), 1)

            def silu(e):
                act.wait_ge(sem("gu_ps"), e + 1)
                act.activation(gs[:, :], ps[:, 2, 0:FE], ACT.Silu).then_inc(sem("gs_ready"), 1)

            def t_hi(e):
                act.wait_ge(sem("hidT_ps"), e + 1)
                act.activation(thi[:, :, :], ps[:, 3, 0:2 * P].rearrange("p (j n) -> p j n", j=2), ACT.Copy)\
                   .then_inc(sem("thi_ready"), 1)

            def y_copy(e, b, free):
                act.wait_ge(sem("down_ps"), e + 1)
                if free is not None:
                    act.wait_ge(sem(f"ye_out{b}"), free)
                act.activation(ysb[:, b, 0:512], ps[:, 4 + 2 * b, :], ACT.Copy).then_inc(sem("y_sb"), 1)

            act.wait_ge(step("experts_go"), after("experts_go"))
            for b in range(2):
                e_hi(b, b, 48, None)
                d_hi(b, b, None)
            x_hi(0, 0)
            silu(0)
            x_hi(1, 1)
            t_hi(0)

            def expert(e, b, landed, free):
                e_hi(e + 1, 1 - b, landed, e)
                silu(e)
                x_hi(e + 1, 1 - b)
                y_copy(e - 1, 1 - b, free)
                d_hi(e + 1, 1 - b, e)
                t_hi(e)

            for e in (1, 2, 3):
                expert(e, e % 2, 48 * ((e + 1) // 2 + 1), 16 if e == 3 else None)
            with act.Fori(2, PAIRS) as r:
                for b in range(2):
                    expert(r * 2 + b, b, r * 48 + (48 + 48 * b), r * 16 - 16 + 16 * b)
            act.wait_ge(step("nov_ready"), after("nov_ready"))
            np_ = act.value_load(nov[0:1, 0:1], min_val=0, max_val=NOV // 2)
            with act.Fori(PAIRS, PAIRS + NOV // 2) as r:
                with act.If(np_ + PAIRS > r):
                    for b in range(2):
                        expert(r * 2 + b, b, r * 48 + (48 + 48 * b), r * 16 - 16 + 16 * b)
            y_copy(np_ * 2 + (NE - 1), 1, np_ * 16 + 16 * (PAIRS - 1))
            act.wait_ge(step("experts_done"), after("experts_done"))
            act.preload_act_table_set(LNEXP)
            for k in range(2):
                act.wait_ge(sem("g2b_ps"), k + 1)
                m = (S, P)[k]
                act.activation(g2b[0:m, 1 - k, :], ps[0:m, 4 + 2 * k:6 + 2 * k, :].rearrange("p b n -> p (b n)"), ACT.Copy)\
                   .then_inc(sem("g2b_copied"), 1)
            act.wait_ge(sem("g2b_copied"), 2)
            act.activation(mark(), epst[0:1, 0:1], ACT.Copy).then_inc(step("g2b_ready"), 1)
            for t in range(NT):
                b, m = t % 2, rows[t]
                act.wait_ge(sem("xsum_ready"), t + 1)
                if t >= 2:
                    act.wait_ge(sem(f"y_out{b}"), 16 * (t // 2))
                chain(act.activation(of[0:m, b, :], xf[0:m, b, :], ACT.Square, accum_out=ssq[0:m, b, 0:1]))
                chain(act.activation(ssq[0:m, b, 1:2], ssq[0:m, b, 0:1], ACT.Ln, bias=epst[0:m, :], scale=1.0 / D))
                act.activation(ssq[0:m, b, 1:2], ssq[0:m, b, 1:2], ACT.Exp, scale=-0.5).then_inc(sem("rf_ready"), 1)

        def moe_dve(dve, chain):
            def signal(name):
                chain.wait()
                dve.memset(mark(), 0.0).then_inc(step(name) if name in STEP else sem(name), 1)

            def by9(ap, n):
                return ap.rearrange("p (t o) -> p t o", o=1).broadcast_to([P, NT, n])

            def cols(ap, n):
                return ap.rearrange("p (o n) -> p o n", o=1).broadcast_to([P, NT, n])

            for s, v in (("state_out", 32), ("x2_out0", 16 * 5), ("x2_out1", 16 * 4), ("h2_out", 16 * NT)):
                dve.wait_ge(sem(s), v)
            signal("stage1_over")
            dve.wait_ge(step("iota_ready"), after("iota_ready"))
            chain(dve.tensor_copy(iot[:, :], ioti[:, :]))
            lg, le = logits[:, :, 0:NG], logits[:, :, NG:NR]

            def first_max(vals, best, tmp, onehot, n):
                chain(dve.tensor_reduce(best, vals, AXX, ALU.max))
                chain(dve.tensor_tensor(tmp, vals, by9(best, n), ALU.is_equal))
                chain(dve.tensor_scalar(tmp, tmp, -float(n), float(n), ALU.mult, ALU.add))
                chain(dve.tensor_tensor(tmp, tmp, cols(iot[:, 0:n], n), ALU.add))
                chain(dve.tensor_reduce(r9[:, 9, :], tmp, AXX, ALU.min))
                chain(dve.tensor_tensor(onehot, cols(iot[:, 0:n], n), by9(r9[:, 9, :], n), ALU.is_equal))

            first_max(lg, r9[:, 0, :], gb_[:, :, :], ga_[:, :, :], NG)
            chain(dve.tensor_tensor(gb_[:, :, :], lg, by9(r9[:, 0, :], NG), ALU.subtract))
            signal("gmax_ready")
            chain(dve.tensor_scalar(ga_[:, :, :], ga_[:, :, :], BIG, -BIG, ALU.mult, ALU.add))
            for g in range(NG):
                chain.last(dve.tensor_tensor(ex[:, :, g * EPG:(g + 1) * EPG], le[:, :, g * EPG:(g + 1) * EPG],
                                             ga_[:, :, g:g + 1].broadcast_to([P, NT, EPG]), ALU.add))
            chain.wait()
            first_max(ex[:, :, :], r9[:, 1, :], et[:, :, :], oh[:, 0, :, :], NE)
            chain(dve.scalar_tensor_tensor(out=ex[:, :, :], in0=oh[:, 0, :, :], scalar=-2 * BIG, in1=ex[:, :, :],
                                           op0=ALU.mult, op1=ALU.add))
            first_max(ex[:, :, :], r9[:, 2, :], et[:, :, :], oh[:, 1, :, :], NE)
            chain(dve.tensor_tensor(r9[:, 5, :], r9[:, 2, :], r9[:, 1, :], ALU.subtract))
            signal("ediff_ready")
            dve.wait_ge(step("gexp_ready"), after("gexp_ready"))
            chain(dve.tensor_reduce(r9[:, 3, :], gb_[:, :, :], AXX, ALU.add))
            dve.wait_ge(step("eexp_ready"), after("eexp_ready"))
            chain(dve.tensor_scalar(r9[:, 6, :], r9[:, 5, :], 1.0, None, ALU.add))
            chain(dve.tensor_tensor(r9[:, 6, :], r9[:, 6, :], r9[:, 3, :], ALU.mult))
            chain(dve.reciprocal(wts[:, 0, :], r9[:, 6, :]))
            chain(dve.tensor_tensor(wts[:, 1, :], wts[:, 0, :], r9[:, 5, :], ALU.mult))
            chain(dve.tensor_tensor(em_[:, :, :], oh[:, 0, :, :], oh[:, 1, :, :], ALU.add))
            chain(dve.tensor_scalar(em_[:, NT - 1, :], em_[:, NT - 1, :], rowmask[:, :], None, ALU.mult))
            signal("mask_ready")
            dve.wait_ge(step("rank_ps"), after("rank_ps"))
            chain.last(dve.memset(tot[:, 0, :], 0.0))
            chain(dve.tensor_copy(pos[:, :, :], ps[:, 1, 0:NT * NE].rearrange("p (t e) -> p t e", t=NT)))
            for t in range(NT):
                chain(dve.tensor_tensor(tot[:, t + 1, :], tot[:, t, :], ps[:, 0, t * NE:(t + 1) * NE], ALU.add))
            chain(dve.tensor_tensor(pos[:, :, :], pos[:, :, :], tot[:, 0:NT, :], ALU.add))
            cnt = tot[:, NT, :]
            for j in range(NT):
                chain.last(dve.tensor_scalar(thr[:, :, j], cnt, float(P * (j + 1)), None, ALU.is_gt))
            chain.wait()
            chain(dve.tensor_reduce(ov[:, 0, :], thr[:, :, :], AXX, ALU.add))
            chain.last(dve.memset(ov[:, 3, :], 0.0))
            chain.wait()
            chain(dve.tensor_tensor_scan(ov[:, 1, :], ov[:, 0, :], ov[:, 3, :], 0.0, ALU.add, ALU.add))
            chain(dve.tensor_tensor(ov[:, 2, :], ov[:, 1, :], ov[:, 0, :], ALU.subtract))
            chain(dve.tensor_tensor(ov[:, 2, :], ov[:, 2, :], iot[:, :], ALU.subtract))
            chain(dve.tensor_scalar(ov[:, 2, :], ov[:, 2, :], float(NE - 1), float(P), ALU.add, ALU.mult))
            chain(dve.tensor_scalar(et[:, :, :], pos[:, :, :], float(P), None, ALU.is_ge))
            chain(dve.tensor_tensor(et[:, :, :], et[:, :, :], cols(ov[:, 2, :], NE), ALU.mult))
            chain(dve.tensor_tensor(et[:, :, :], et[:, :, :], pos[:, :, :], ALU.add))
            chain(dve.tensor_scalar(ov[:, 3, :], iot[:, :], float(P), None, ALU.mult))
            chain(dve.tensor_tensor(et[:, :, :], et[:, :, :], cols(ov[:, 3, :], NE), ALU.add))
            for c in range(2):
                chain(dve.tensor_tensor(oh[:, c, :, :], oh[:, c, :, :], et[:, :, :], ALU.mult))
                chain(dve.tensor_reduce(r9[:, 7 + c, :], oh[:, c, :, :], AXX, ALU.add))
            chain(dve.tensor_copy(slots[:, :, :], r9[:, 7:9, :]))
            chain.last(dve.tensor_scalar(sidx[:, :, :], slots[:, :, :], P - 1, None, ALU.bitwise_and))
            chain(dve.tensor_scalar(sloti[:, :, :], slots[:, :, :], 7, None, ALU.logical_shift_right))
            chain(dve.tensor_scalar(sidx[:, :, :], sidx[:, :, :], MT, None, ALU.mult))
            chain(dve.tensor_tensor(sidx[:, :, :], sidx[:, :, :], sloti[:, :, :], ALU.add))
            signal("sidx_ready")
            for j in range(NOV + 2):
                chain.last(dve.tensor_scalar(ovc[:, j, :], ov[0:1, 1, :], float(j), None, ALU.is_le))
            chain.wait()
            chain(dve.tensor_reduce(ovf[:, :], ovc[:, :, :], AXX, ALU.add))
            chain(dve.tensor_scalar(ovf[:, :], ovf[:, :], float(NE - 1), None, ALU.min))
            chain.last(dve.tensor_copy(ovx[:, :], ovf[:, :]))
            chain(dve.tensor_copy(nov[:, :], ov[0:1, 1, NE - 1:NE]))
            chain(dve.tensor_scalar(nov[:, :], nov[:, :], 1, None, ALU.add))
            chain(dve.tensor_scalar(nov[:, :], nov[:, :], 1, None, ALU.logical_shift_right))
            signal("nov_ready")
            dve.wait_ge(sem("list_done"), 16 * 2 * NT)
            dve.wait_ge(sem("lists_in"), 16)
            dve.tensor_scalar(glists[:, :], lists[:, :], 1, None, ALU.logical_shift_right).then_inc(step("glists_ready"), 1)
            signal("experts_go")

            def split_lo(e, b):
                dve.wait_ge(sem("ehi_ready"), e * 2 + 1)
                dve.tensor_tensor(elo[:, b, :, :], eraw[:, b, :, :], ehi[:, b, :, :].bitcast(F32), ALU.subtract)\
                   .then_inc(sem("elo_ready"), 1)

            def x_lo(e, b):
                dve.wait_ge(sem("xhi_ready"), e + 1)
                dve.tensor_tensor(xlo[:, b, :, :], ps[:, 0:2, :].rearrange("p a (k n) -> p (a k) n", k=4),
                                  xhi[:, b, :, :].bitcast(F32), ALU.subtract).then_inc(sem("xlo_ready"), 1)

            def hidden(e):
                dve.wait_ge(sem("gs_ready"), e + 1)
                dve.tensor_tensor(hid[:, :].rearrange("t (j p) -> t p j", j=2), gs[:, :].rearrange("t (p j) -> t p j", j=2),
                                  ps[:, 2, FE:2 * FE].rearrange("t (p j) -> t p j", j=2), ALU.mult).then_inc(sem("hid_ready"), 1)

            def t_lo(e):
                dve.wait_ge(sem("thi_ready"), e + 1)
                dve.tensor_tensor(tlo[:, :, :], ps[:, 3, 0:2 * P].rearrange("p (j n) -> p j n", j=2),
                                  thi[:, :, :].bitcast(F32), ALU.subtract).then_inc(sem("tlo_ready"), 1)

            def y_copy(e, b, free):
                dve.wait_ge(sem("down_ps"), e + 1)
                if free is not None:
                    dve.wait_ge(sem(f"ye_out{b}"), free)
                dve.tensor_copy(ysb[:, b, 512:D], ps[:, 5 + 2 * b, :]).then_inc(sem("y_sb"), 1)

            for b in range(2):
                split_lo(b, b)
            x_lo(0, 0)
            hidden(0)
            x_lo(1, 1)
            t_lo(0)

            def expert(e, b, free):
                split_lo(e + 1, 1 - b)
                hidden(e)
                x_lo(e + 1, 1 - b)
                y_copy(e - 1, 1 - b, free)
                t_lo(e)

            for e in (1, 2, 3):
                expert(e, e % 2, 16 if e == 3 else None)
            with dve.Fori(2, PAIRS) as r:
                for b in range(2):
                    expert(r * 2 + b, b, r * 16 - 16 + 16 * b)
            np_ = dve.value_load(nov[0:1, 0:1], min_val=0, max_val=NOV // 2)
            with dve.Fori(PAIRS, PAIRS + NOV // 2) as r:
                with dve.If(np_ + PAIRS > r):
                    for b in range(2):
                        expert(r * 2 + b, b, r * 16 - 16 + 16 * b)
            y_copy(np_ * 2 + (NE - 1), 1, np_ * 16 + 16 * (PAIRS - 1))
            for b in range(2):
                dve.wait_ge(sem(f"ye_out{b}"), np_ * 16 + 16 * PAIRS)
                dve.wait_ge(sem(f"xg_in{b}"), np_ * 16 + 16 * (PAIRS + 1))
            dve.memset(mark(), 0.0).then_inc(step("experts_done"), 1)
            dve.wait_ge(step("g2b_ready"), after("g2b_ready"))
            dve.wait_ge(sem("fg_in"), 16)
            for t in range(NT):
                b, m = t % 2, rows[t]
                dve.wait_ge(sem(f"y12_in{b}"), 16 * (t // 2 + 1))
                ya, yb = y12[0:m, b, 0, :], y12[0:m, b, 1, :]
                chain(dve.tensor_scalar(ya, ya, wts[0:m, 0, t:t + 1], None, ALU.mult))
                chain(dve.scalar_tensor_tensor(out=ya, in0=yb, scalar=wts[0:m, 1, t:t + 1], in1=ya, op0=ALU.mult, op1=ALU.add))
                chain(dve.tensor_tensor(ya, ya, g2b[0:m, t // NC_, :], ALU.mult))
                dve.wait_ge(sem(f"xf_in{b}"), 16 * (t // 2 + 1))
                dve.tensor_tensor(xf[0:m, b, :], xf[0:m, b, :], ya, ALU.add).then_inc(sem("xsum_ready"), 1)
                dve.wait_ge(sem("rf_ready"), t + 1)
                dve.scalar_tensor_tensor(out=of[0:m, b, :], in0=xf[0:m, b, :], scalar=ssq[0:m, b, 1:2], in1=fgb[0:m, :],
                                         op0=ALU.mult, op1=ALU.mult).then_inc(sem("of_ready"), 1)

        def moe_pe(pe):
            pe.wait_ge(step("mask_ready"), after("mask_ready"))
            m = em_[:, :, :].rearrange("p t e -> p (t e)")
            pe.matmul(ps[:, 1, 0:NT * NE], ustrict[:, :], m, start=True, stop=True)
            pe.matmul(ps[:, 0, 0:NT * NE], ones[:, :], m, start=True, stop=True).then_inc(step("rank_ps"), 1)

            def x_transpose(e, b, landed):
                pe.wait_ge(sem(f"xg_in{b}"), landed)
                pe.wait_ge(sem("xlo_ready"), e)
                for k in range(KD):
                    mm = pe.transpose(ps[:, k // 4, (k % 4) * P:(k % 4 + 1) * P], xg[:, b, k * P:(k + 1) * P], ident[:, :])
                mm.then_inc(sem("xgT_ps"), 1)

            def gate_up(e, b):
                pe.wait_ge(sem("xlo_ready"), e + 1)
                pe.wait_ge(sem("ehi_ready"), e * 2 + 1)
                pe.wait_ge(sem("elo_ready"), e + 1)
                pe.wait_ge(sem("hid_ready"), e)
                for i, (x, w) in enumerate(((xhi, ehi), (xlo, ehi), (xhi, elo))):
                    for k in range(KD):
                        mm = pe.matmul(ps[:, 2, :], x[:, b, k, :], w[:, b, k, :], start=(i + k == 0),
                                       stop=(i == 2 and k == KD - 1))
                mm.then_inc(sem("gu_ps"), 1)

            def hid_transpose(e):
                pe.wait_ge(sem("hid_ready"), e + 1)
                pe.wait_ge(sem("tlo_ready"), e)
                for j in range(2):
                    mm = pe.transpose(ps[:, 3, j * P:(j + 1) * P], hid[:, j * P:(j + 1) * P], ident[:, :])
                mm.then_inc(sem("hidT_ps"), 1)

            def down(e, b, free):
                pe.wait_ge(sem("tlo_ready"), e + 1)
                pe.wait_ge(sem("dlo_ready"), e + 1)
                if free is not None:
                    pe.wait_ge(sem("y_sb"), free)
                for a in range(2):
                    for i, (x, w) in enumerate(((thi, dhi), (tlo, dhi), (thi, dlo))):
                        for j in range(2):
                            mm = pe.matmul(ps[:, 4 + 2 * b + a, :], x[:, j, :], w[:, b, j, a * 512:(a + 1) * 512],
                                           start=(i + j == 0), stop=(i == 2 and j == 1))
                mm.then_inc(sem("down_ps"), 1)

            pe.wait_ge(step("experts_go"), after("experts_go"))
            x_transpose(0, 0, 16)
            gate_up(0, 0)
            x_transpose(1, 1, 16)
            hid_transpose(0)

            def expert(e, b, landed, free):
                gate_up(e, b)
                x_transpose(e + 1, 1 - b, landed)
                down(e - 1, 1 - b, free)
                hid_transpose(e)

            for e in (1, 2, 3):
                expert(e, e % 2, 16 * ((e + 1) // 2 + 1), 2 if e == 3 else None)
            with pe.Fori(2, PAIRS) as r:
                for b in range(2):
                    expert(r * 2 + b, b, r * 16 + (16 + 16 * b), r * 4 + (2 * b - 4))
            pe.wait_ge(step("nov_ready"), after("nov_ready"))
            np_ = pe.value_load(nov[0:1, 0:1], min_val=0, max_val=NOV // 2)
            with pe.Fori(PAIRS, PAIRS + NOV // 2) as r:
                with pe.If(np_ + PAIRS > r):
                    for b in range(2):
                        expert(r * 2 + b, b, r * 16 + (16 + 16 * b), r * 4 + (2 * b - 4))
            down(np_ * 2 + (NE - 1), 1, np_ * 4 + 2 * (NE - 2))
            pe.wait_ge(step("experts_done"), after("experts_done"))
            for k in range(2):
                n_ = (S, P)[k]
                for q in range(KD):
                    lhs = modT[:, 5 * KD + q, 1:9] if k == 0 else modT[:, 5 * KD + q, 0:1].broadcast_to([P, P])
                    mm = pe.matmul(ps[0:n_, 4 + 2 * k + q // 4, (q % 4) * P:(q % 4 + 1) * P], lhs, ident[:, :],
                                   start=True, stop=True)
                mm.then_inc(sem("g2b_ps"), 1)

        block = ctx.enter_context(nc.Block())

        @block.sync
        def _(sp):
            def load(dst, src, s):
                sp.dma_start(dst, src).then_inc(sem(s), 16)

            load(c9[0:1, :], c_prompt, "c_in")
            load(c9[1:9, :], c_sample, "c_in")
            for at, n, v in ((0, MB, b_ada), (MB, KD, norm1_g), (MB + KD, KD, norm2_g), (MB + 2 * KD, H, mh_g),
                             (MB + 2 * KD + 4, CB, b_dw), (MB + 2 * KD + 8, CB, cln_g),
                             (MB + 2 * KD + 12, CB, cln_b)):
                load(vecs[at:at + n, :], v if len(v.shape) == 2 else v.rearrange("(b p) -> b p", p=P), "vec_in")
            load(wdw[:, :], w_dw, "vec_in")
            load(bi[:, :], b_ig.rearrange("(h o) -> h o", o=1), "gbias_in")
            load(bf[:, :], b_fg.rearrange("(h o) -> h o", o=1), "gbias_in")
            def ada_load(n):
                g, k = divmod(n, KD)
                if g:
                    sp.wait_ge(sem("ada_used"), n - 7)
                load(wada[:, k, :], w_ada[k * P:(k + 1) * P, g * AG:(g + 1) * AG], f"wada_in{k}")

            for t in range(NT):
                if t >= 2:
                    sp.wait_ge(sem("xn_done"), t - 1)
                load(xt[0:rows[t], t % 2, :], x_d[t], f"x_in{t % 2}")
                if 1 <= t:
                    ada_load(t - 1)
                if t == NT - 2:
                    load(wraw[:, 0, :, :], w_in_v[:, :, C0_CONV:C0_CONV + 256], "wraw_in0")
            for u in range(1, 2):
                load(wraw[:, u, :, :], w_in_v[:, :, C0_CONV + 256 * u:C0_CONV + 256 * (u + 1)], f"wraw_in{u}")
            load(wgt[:, :, :], w_in_v[:, :, 4 * H * DH:4 * H * DH + 2 * H], "wgt_in")
            load(m0t[:, :], m0.rearrange("b h -> h b"), "m0_in")

            def w_in_load(m, u, col):
                sp.wait_ge(sem("z_done"), m * 4 + 2 * u)
                sp.dma_start(wraw[:, u, :, :], w_in_v[:, :, bass.ds(m * 512 + (col + 256 * u), 256)])\
                  .then_inc(sem(f"wraw_in{u}"), 16)

            for n in range(KD, 2 * KD):
                ada_load(n)
            for u in range(2):
                w_in_load(1, u, C0_CONV)
            for n in range(2 * KD, 3 * KD):
                ada_load(n)
            w_in_load(CROUNDS, 0, -512 * CROUNDS)
            w_in_load(CROUNDS, 1, -512 * CROUNDS)
            w_in_load(CROUNDS + 1, 0, -512 * CROUNDS)
            w_in_load(CROUNDS + 1, 1, -512 * CROUNDS)
            sp.wait_ge(step("rows_in"), after("rows_in"))
            load(m_p.rearrange("(h o) -> h o", o=1), mrow[:, T - 1:T], "m_out")
            load(m_s.rearrange("b h -> h b"), mrow[:, T:NTOK], "m_out")
            with sp.Fori(CROUNDS + 2, SPLITS) as m:
                for u in range(2):
                    w_in_load(m, u, -512 * CROUNDS)
            sp.wait_ge(sem("z_done"), NZ + 2)
            load(crow[:, :, :], cache.rearrange("(g b) w c -> (b w) g c", g=2), "crow_in")
            load(wout[:, :, :], w_out.rearrange("(k p) n -> p k n", p=P), "wout_in")
            load(wr[:, :, 0:NG], w_grp.rearrange("(p k) n -> p k n", p=P), "wr_in")
            load(wr[:, :, NG:NR], w_er.rearrange("(p k) n -> p k n", p=P), "wr_in")
            load(rbias[:, 0:NG], b_grp.rearrange("(o n) -> o n", o=1).broadcast_to([P, NG]), "wr_in")
            load(rbias[:, NG:NR], b_er.rearrange("(o n) -> o n", o=1).broadcast_to([P, NE]), "wr_in")
            load(conv_s[:, 0:PAD - 1, :], cache[:, 1:PAD, :], "out_done")
            load(ntok[:, :], n0.rearrange("b h d -> (b h) d"), "n0_in")
            sp.wait_ge(sem("tails_ready"), 2)
            load(conv_p, utail[:, :], "out_done")
            load(conv_s[:, PAD - 1, :], usam[:, :], "out_done")
            sp.wait_ge(step("sumsq_ps"), after("sumsq_ps"))
            for i in range(4):
                load(z[:, U0 + i, 0:8 * DH].rearrange("p (x e) -> p x e", x=8),
                     C0[2 * i:2 * i + 2].rearrange("b h d e -> d (b h) e"), "c0_in")
            sp.wait_ge(step("conv_scaled"), after("conv_scaled"))
            for t in range(NT):
                b = t % 2
                if t == 7:
                    sp.wait_ge(sem("cnew_ready"), S * H)
                    for i in range(4):
                        load(C_s[2 * i:2 * i + 2].rearrange("b h d e -> d (b h) e"),
                             z[:, U0 + i, 0:8 * DH].rearrange("p (x e) -> p x e", x=8), "c_out")
                if t >= 2:
                    sp.wait_ge(sem(f"x2_out{b}"), 16 * (t // 2))
                    sp.wait_ge(sem("h2_ready"), t - 1)
                load(x2[0:rows[t], b, :], x_d[t], f"xr_in{b}")
                if t >= 1:
                    store_tile(sp, t - 1)
                if t == 3:
                    sp.wait_ge(step("nnew_ready"), after("nnew_ready"))
                    load(n_s.rearrange("b h d -> (b h) d"), ntok[:, :], "out_done")
            store_tile(sp, NT - 1)
            sp.wait_ge(step("mlstm_done"), after("mlstm_done"))
            load(C_p.rearrange("h d e -> d h e"), caug[:, :, 0:DH], "state_out")
            load(n_p.rearrange("h d -> d h"), caug[:, :, DH], "state_out")
            moe_loads(sp)

        @block.gpsimd
        def _(pool):
            chain = Chain(pool, sem("pool_chain"))
            pool.memset(ident[:, :], 0.0).then_inc(sem("pool_chain"), 1)
            pool.memset(identb[:, :], 0.0).then_inc(sem("pool_chain"), 1)
            pool.memset(causal[:, :], 0.0).then_inc(sem("pool_chain"), 1)
            pool.memset(ones[:, :], 1.0).then_inc(sem("pool_chain"), 1)
            chain.n = 4
            chain.wait()
            for m in (ident, identb):
                pool.affine_select(out=m[:, :], in_=m[:, :], compare_op=ALU.not_equal, fill=1.0, base=0,
                                   pattern=[[-1, P]], channel_multiplier=1).then_inc(sem("consts"), 1)
            pool.affine_select(out=causal[:, :], in_=causal[:, :], compare_op=ALU.is_ge, fill=-BIG, base=0,
                               pattern=[[1, P]], channel_multiplier=-1).then_inc(sem("consts"), 1)
            pool.affine_select(out=ustrict[:, :], in_=ones[:, :], compare_op=ALU.is_gt, fill=0.0, base=0,
                               pattern=[[1, P]], channel_multiplier=-1).then_inc(sem("consts"), 1)
            pool.iota(tokid[:, :, :], pattern=[[1, 2], [2 * P, NT]], base=0, channel_multiplier=2).then_inc(sem("consts"), 1)
            def lo(j, u, v):
                pool.wait_ge(sem("whi_ready"), j + 1)
                block = slice(v * P, (v + 1) * P)
                pool.tensor_tensor(wlo[:, u, :, block], wraw[:, u, :, block], whi[:, v, :, :].bitcast(F32), ALU.subtract)\
                    .then_inc(sem("wlo_ready"), 1)

            lo(0, 0, 0)
            for k in range(1, KD, 2):
                pool.wait_ge(sem("hhi_done"), k + 1)
                pool.tensor_tensor(hlo[:, k, :], hf[:, k, :], hhi[:, k, :].bitcast(F32), ALU.subtract)\
                    .then_inc(sem("hlo_odd"), 1)

            def lo_rounds(first, end):
                with pool.Fori(first, end) as m:
                    for q in range(1, 5):
                        lo(m * 4 + q, (q // 2) % 2, q % 2)

            lo_rounds(0, GROUND - 1)
            pool.wait_ge(sem("ada_used"), NAG * KD)
            chain.last(pool.memset(glo[:, :, :].bitcast(F32), 0.0))
            chain(pool.memset(ghi[:, :, :].bitcast(F32), 0.0))
            pool.memset(mark(), 0.0).then_inc(step("gate_zeroed"), 1)
            lo_rounds(GROUND - 1, GROUND)
            pool.wait_ge(sem("ghi_ready"), 2)
            for i in range(2):
                pool.tensor_tensor(glo[:, :, 32 * i:32 * i + H], wgt[:, :, i * H:(i + 1) * H],
                                   ghi[:, :, 32 * i:32 * i + H].bitcast(F32), ALU.subtract)\
                    .then_inc(sem("glo_ready"), 1)
            lo_rounds(GROUND, SPLITS - 1)
            for j in range(NZ - 3, NZ):
                lo(j, (j // 2) % 2, j % 2)
            moe_pool(pool, chain)

        @block.scalar
        def _(act):
            chain = Chain(act, sem("act_chain"))
            act.wait_ge(sem("c_in"), 32)
            act.activation(c9[:, :], c9[:, :], ACT.Silu).then_inc(step("csilu"), 1)
            act.wait_ge(step("dve_consts"), after("dve_consts"))
            act.preload_act_table_set(LNEXP)
            for t in range(NT):
                b, n = t % 2, rows[t]
                act.wait_ge(sem(f"x_in{b}"), 16 * (t // 2 + 1))
                if t >= 2:
                    act.wait_ge(sem("xT_done"), t - 1)
                chain(act.activation(xn[0:n, b, :], xt[0:n, b, :], ACT.Square, accum_out=ssq[0:n, b, 0:1]))
                chain(act.activation(ssq[0:n, b, 1:2], ssq[0:n, b, 0:1], ACT.Ln, bias=epst[0:n, :], scale=1.0 / D))
                act.activation(ssq[0:n, b, 1:2], ssq[0:n, b, 1:2], ACT.Exp, scale=-0.5).then_inc(sem("rstd_ready"), 1)

            def mod_rows(g):
                act.wait_ge(sem("ada_used"), KD * (g + 1))
                if g == 0:
                    act.wait_ge(step("modr_zero"), after("modr_zero"))
                else:
                    act.wait_ge(sem("modT_ps"), g)
                for j in range(4):
                    act.activation(modr[32 * j:32 * j + 9, :], ps[32 * j:32 * j + 9, ACC[g], :], ACT.Copy)\
                       .then_inc(sem("modr_ready"), 1)

            def hi(j, u, v, landed):
                act.wait_ge(sem(f"wraw_in{u}"), landed)
                act.wait_ge(sem("z_done"), j + 1)
                act.activation(whi[:, v, :, :], wraw[:, u, :, v * P:(v + 1) * P], ACT.Copy)\
                   .then_inc(sem("whi_ready"), 1)

            def evac(j, v):
                act.wait_ge(sem("z_done"), j + 3)
                act.activation(z[:, bass.ds(j, 1), PAD:ZW].rearrange("p o (c n) -> p (o c) n", c=3),
                               ps[:, 3 * v:3 * v + 3, 0:TW], ACT.Copy).then_inc(sem("z_evac"), 1)

            def split_rounds(first, end):
                with act.Fori(first, end) as m:
                    for q in range(4):
                        n = q + 1
                        hi(m * 4 + n, (n // 2) % 2, n % 2, m * 16 + (16 if n < 4 else 32))
                        evac(m * 4 + q, q % 2)

            for _ in range(2):
                act.activation(mark(), epst[0:1, 0:1], ACT.Copy).then_inc(sem("z_evac"), 1)
            hi(0, 0, 0, 16)
            mod_rows(0)
            for k in range(KD):
                act.wait_ge(sem("hf_ready"), k + 1)
                act.activation(hhi[:, k, :], hf[:, k, :], ACT.Copy).then_inc(sem("hhi_done"), 1)
            split_rounds(0, 1)
            mod_rows(1)
            split_rounds(1, CROUNDS)
            mod_rows(2)
            act.wait_ge(sem("z_evac"), 2 + 4 * CROUNDS)
            for b in range(CB):
                act.activation(z[:, GB0 + b, PAD:ZW], z[:, GB0 + b, PAD:ZW], ACT.Sigmoid).then_inc(sem("sig_gb"), 1)
            act.wait_ge(step("gate_zeroed"), after("gate_zeroed"))
            act.wait_ge(sem("wgt_in"), 16)
            for i in range(2):
                act.activation(ghi[:, :, 32 * i:32 * i + H], wgt[:, :, i * H:(i + 1) * H], ACT.Copy)\
                   .then_inc(sem("ghi_ready"), 1)
            split_rounds(CROUNDS, GROUND)
            act.wait_ge(step("gates_ps"), after("gates_ps"))
            act.wait_ge(sem("gbias_in"), 32)
            act.activation(gi[:, :].rearrange("h (c n) -> h c n", c=3), ps[0:H, 0:3, 0:TW], ACT.Identity,
                           bias=bi[:, :]).then_inc(sem("gates_ready"), 1)
            chain(act.activation(gf[:, :].rearrange("h (c n) -> h c n", c=3), ps[32:32 + H, 0:3, 0:TW], ACT.Identity,
                                 bias=bf[:, :]))
            act.activation(mark(), epst[0:1, 0:1], ACT.Copy).then_inc(sem("gates_ready"), 1)
            chain(act.activation(gt[:, :], gf[:, :], ACT.Abs))
            act.preload_act_table_set(LNEXP)
            chain(act.activation(gt[:, :], gt[:, :], ACT.Exp, scale=-1.0))
            act.activation(gt[:, :], gt[:, :], ACT.Ln, bias=ones[0:H, 0:1]).then_inc(step("softplus_ready"), 1)
            split_rounds(GROUND, GROUND + 1)
            act.wait_ge(step("rows_in"), after("rows_in"))
            chain.last(act.activation(rows_[0:H, :], rows_[0:H, :], ACT.Exp))
            chain.last(act.activation(rows_[64:64 + H, :], rows_[64:64 + H, :], ACT.Exp, scale=-1.0))
            chain.last(act.activation(srow[:, :, :], srow[:, :, :], ACT.Exp))
            chain.wait()
            act.activation(mark(), epst[0:1, 0:1], ACT.Copy).then_inc(step("srow_ready"), 1)
            act.wait_ge(step("rowsT_ps"), after("rowsT_ps"))
            act.wait_ge(sem("m_out"), 32)
            split_rounds(GROUND + 1, SPLITS - 1)
            for q in range(3):
                n, m = q + 1, SPLITS - 1
                hi(m * 4 + n, n // 2, n % 2, 16 * (m + 1))
                evac(m * 4 + q, q % 2)
            evac(NZ - 1, 1)
            act.wait_ge(sem("z_evac"), NZ + 2)
            for b in range(H):
                act.activation(z[:, O0 + b, PAD:ZW], z[:, O0 + b, PAD:ZW], ACT.Sigmoid).then_inc(sem("sig_o"), 1)
            act.preload_act_table_set(LNEXP)
            act_rest(act, chain)

        @block.vector
        def _(dve):
            chain = Chain(dve, sem("dve_chain"))
            dve.memset(modr[:, :], 0.0).then_inc(step("modr_zero"), 1)
            dve.memset(epst[:, :], EPS).then_inc(step("dve_consts"), 1)
            dve.memset(lists[:, :], NOTOK).then_inc(step("lists_zero"), 1)
            chain(dve.memset(rowmask[:, :], 0.0))
            chain.last(dve.memset(rowmask[0:S, :], 1.0))
            dve.wait_ge(step("c9T_ps"), after("c9T_ps"))
            dve.tensor_copy(c9T[:, :, :], ps[:, 4, 0:16 * KD].rearrange("p (k r) -> p k r", k=KD)[:, :, 0:9])\
               .then_inc(step("c9T_ready"), 1)
            dve.wait_ge(step("vT_ps"), after("vT_ps"))
            chain.last(dve.tensor_copy(vT[:, :], ps[:, 5, 0:NV]))
            chain(dve.tensor_copy(wdT[:, :, :], ps[:, 5, P:P + 32 * CB].rearrange("p (b w) -> p b w", b=CB)[:, :, 0:CW]))
            def xnorm(t):
                b, n = t % 2, rows[t]
                dve.wait_ge(sem("rstd_ready"), t + 1)
                dve.tensor_scalar(xn[0:n, b, :], xt[0:n, b, :], ssq[0:n, b, 1:2], None, ALU.mult)\
                   .then_inc(sem("xn_done"), 1)

            xnorm(0)
            for t in range(NT):
                b, n = t % 2, rows[t]
                if t + 1 < NT:
                    xnorm(t + 1)
                dve.wait_ge(sem("xT_done"), t + 1)
                dve.tensor_copy(hf[:, :, t * P:t * P + n],
                                ps[:, 2 * b:2 * b + 2, :].rearrange("p a (k n) -> p (a k) n", k=4)[:, :, 0:n])\
                   .then_inc(sem("xT_copied"), 1)

            def modulation(g):
                dve.wait_ge(sem("modT_ps"), g + 1)
                dve.tensor_tensor(
                    modT[:, 16 * g:16 * g + 16, :].rearrange("p (j q) r -> p j q r", j=4),
                    ps[:, 7 - ACC[g] + 6, :].rearrange("p (q j r) -> p j q r", q=4, j=4)[:, :, :, 0:9],
                    vT[:, 16 * g:16 * g + 16].rearrange("p (j q o) -> p j q o", j=4, o=1).broadcast_to([P, 4, 4, 9]),
                    ALU.add).then_inc(sem("modT_done"), 1)
                dve.wait_ge(sem("modT_done"), g + 1)

            def norm_factor(a, sc, nrm):
                chain(dve.scalar_tensor_tensor(
                    out=a[:, :, :], in0=modT[:, sc:sc + KD, :], scalar=1.0,
                    in1=vT[:, nrm:nrm + KD].rearrange("p (k o) -> p k o", o=1).broadcast_to([P, KD, 9]),
                    op0=ALU.add, op1=ALU.mult))

            chain.wait()
            modulation(0)
            norm_factor(A1, KD, MB)
            dve.wait_ge(sem("xT_copied"), NT)
            hs = hf[:, :, T:NTOK]
            chain(dve.tensor_tensor(hs, hs, A1[:, :, 1:9], ALU.mult))
            chain(dve.tensor_tensor(hs, hs, modT[:, 0:KD, 1:9], ALU.add))

            def even_lo(k):
                dve.wait_ge(sem("hhi_done"), k + 1)
                dve.tensor_tensor(hlo[:, k, :], hf[:, k, :], hhi[:, k, :].bitcast(F32), ALU.subtract)\
                   .then_inc(sem("hlo_even"), 1)

            for k in range(KD):
                hp = hf[:, k, 0:T]
                dve.tensor_scalar(hp, hp, A1[:, k, 0:1], modT[:, k, 0:1], ALU.mult, ALU.add).then_inc(sem("hf_ready"), 1)
                if k >= 1 and k % 2:
                    even_lo(k - 1)
            modulation(1)
            dve.wait_ge(sem("z_evac"), 2 + 4 * CROUNDS)
            chain.last(dve.memset(z[:, U0:U0 + CB, 0:PAD], 0.0))
            dve.wait_ge(sem("sig_gb"), CB)
            chain(dve.tensor_tensor(z[:, U0:U0 + CB, PAD:ZW], z[:, U0:U0 + CB, PAD:ZW], z[:, GB0:GB0 + CB, PAD:ZW], ALU.mult))
            dve.memset(mark(), 0.0).then_inc(step("u_ready"), 1)
            for b in range(CB):
                dve.tensor_scalar(z[:, GB0 + b, PAD:SC], u_at(b, 0, T), wdT[:, b, 0:1], vT[:, VB + b:VB + b + 1],
                                  ALU.mult, ALU.add).then_inc(sem("conv_taps"), 1)
            def taps(first, end):
                chain.wait()
                with dve.Fori(first, end) as w:
                    for b in range(CB):
                        dve.wait_ge(sem("conv_taps"), w * CB + (b + 1 - CB))
                        dve.scalar_tensor_tensor(
                            out=z[:, GB0 + b, PAD:SC], in0=z[:, U0 + b, bass.ds(w, T)], scalar=wdT[:, b, bass.ds(w, 1)],
                            in1=z[:, GB0 + b, PAD:SC], op0=ALU.mult, op1=ALU.add).then_inc(sem("conv_taps"), 1)

            taps(1, TAPS1)
            modulation(2)
            norm_factor(A2, 4 * KD, MB + KD)
            gate_rows(dve, chain)
            taps(TAPS1, CW)
            dve.wait_ge(sem("conv_taps"), CB * CW)
            dve_rest(dve, chain)

        @block.tensor
        def _(pe):
            pe.wait_ge(sem("consts"), 5)
            for _ in range(2):
                pe.matmul(ps[0:1, 6, 0:1], ones[0:1, 0:1], ones[0:1, 0:1], start=True, stop=True)\
                  .then_inc(sem("z_done"), 1)
            pe.wait_ge(step("csilu"), after("csilu"))
            for k in range(KD):
                mm = pe.transpose(ps[:, 4, 16 * k:16 * k + 9], c9[:, k * P:(k + 1) * P], ident[0:9, 0:9])
            mm.then_inc(step("c9T_ps"), 1)
            pe.wait_ge(sem("vec_in"), 16 * 8)
            pe.transpose(ps[:, 5, 0:NV], vecs[:, :], ident[0:NV, 0:NV])
            for b in range(CB):
                mm = pe.transpose(ps[:, 5, P + 32 * b:P + 32 * b + CW], wdw[:, b * P:(b + 1) * P], ident[0:CW, 0:CW])
            mm.then_inc(step("vT_ps"), 1)
            pe.wait_ge(step("c9T_ready"), after("c9T_ready"))
            def ada(g, k):
                pe.wait_ge(sem(f"wada_in{k}"), 16 * (g + 1))
                if g and k == 0:
                    pe.wait_ge(sem("modT_done"), g)
                for j in range(4):
                    mm = pe.matmul(ps[32 * j:32 * j + 9, ACC[g], :], c9T[:, k, :], wada[:, k, j * 512:(j + 1) * 512],
                                   start=(k == 0), stop=(k == KD - 1), skip_group_check=True)
                mm.then_inc(sem("ada_used"), 1)

            def ada_transpose(g):
                pe.wait_ge(sem("modr_ready"), 4 * g + 4)
                for q in range(4):
                    mm = pe.transpose(ps[:, 7 - ACC[g] + 6, q * P:(q + 1) * P], modr[:, q * P:(q + 1) * P], ident[:, :])
                mm.then_inc(sem("modT_ps"), 1)

            for t in range(NT):
                b, n = t % 2, rows[t]
                pe.wait_ge(sem("xn_done"), t + 1)
                if t >= 2:
                    pe.wait_ge(sem("xT_copied"), t - 1)
                for k in range(KD):
                    mm = pe.transpose(ps[:, 2 * b + k // 4, (k % 4) * P:(k % 4) * P + n], xn[0:n, b, k * P:(k + 1) * P],
                                      ident[0:n, 0:n])
                mm.then_inc(sem("xT_done"), 1)
                if t < KD:
                    ada(0, t)
            ada_transpose(0)

            def products(whi_k, wlo_k, bank, n, lo_waits):
                for k in range(KD):
                    for i, (w, h) in enumerate(((whi_k, hhi), (wlo_k, hhi), (whi_k, hlo))):
                        first, last = k == 0 and i == 0, k == KD - 1 and i == 2
                        if lo_waits and i == 0:
                            pe.wait_ge(sem("hhi_done"), k + 1)
                        if lo_waits and i == 2:
                            pe.wait_ge(sem("hlo_odd" if k % 2 else "hlo_even"), k // 2 + 1)
                        for c in range(3):
                            mm = pe.matmul(ps[0:n, bank + c, 0:TW], w(k), h[:, k, c * TW:(c + 1) * TW], start=first, stop=last)
                return mm

            def project(j, u, v):
                pe.wait_ge(sem("whi_ready"), j + 1)
                pe.wait_ge(sem("wlo_ready"), j + 1)
                pe.wait_ge(sem("z_evac"), j + 1)
                products(lambda k: whi[:, v, k, :], lambda k: wlo[:, u, k, v * P:(v + 1) * P], 3 * v, P, (u, v) == (0, 0))\
                    .then_inc(sem("z_done"), 1)

            def rounds(first, end):
                with pe.Fori(first, end) as m:
                    for q in range(4):
                        project(m * 4 + q, q // 2, q % 2)

            rounds(0, 1)
            for k in range(KD):
                ada(1, k)
            rounds(1, CROUNDS)
            ada_transpose(1)
            for k in range(KD):
                ada(2, k)
            rounds(CROUNDS, GROUND)
            ada_transpose(2)
            pe.wait_ge(sem("ghi_ready"), 2)
            pe.wait_ge(sem("glo_ready"), 2)
            pe.wait_ge(sem("z_evac"), 4 * GROUND + 1)
            products(lambda k: ghi[:, k, :], lambda k: glo[:, k, :], 0, 32 + H, False).then_inc(step("gates_ps"), 1)
            pe.wait_ge(sem("gates_ready"), 2)
            rounds(GROUND, GROUND + 1)
            pe.wait_ge(step("srow_ready"), after("srow_ready"))
            pe.wait_ge(sem("modT_done"), NAG)
            for c in range(NC_):
                pe.transpose(ps[:, 6 + c // 4, (c % 4) * 72:(c % 4) * 72 + 68], rows_[:, c * P:(c + 1) * P], ident[0:68, 0:68])
            for h in range(H):
                pe.matmul(ps[:, 6, 300 + h * NC_:300 + (h + 1) * NC_], on_all(h, H), rows_[0:H, P - 1:T:P],
                          start=True, stop=True)
                mm = pe.matmul(ps[:, 7, 300 + h * 3 * S:300 + (h + 1) * 3 * S], on_all(h, H),
                               srow[:, :, :].rearrange("h f b -> h (f b)"), start=True, stop=True)
            mm.then_inc(step("rowsT_ps"), 1)
            rounds(GROUND + 1, SPLITS)
            pe_rest(pe)


_INS = ["x_prompt", "x_sample", "c_prompt", "c_sample", "state_mlstm_C", "state_mlstm_n", "state_mlstm_m", "cache_conv",
        "w_ada", "b_ada", "norm1_g", "w_in", "b_igate", "b_fgate", "mh_norm_g", "w_dw", "b_dw", "conv_ln_g",
        "conv_ln_b", "w_out", "norm2_g", "w_grp_router", "b_grp_router", "w_exp_router", "b_exp_router", "w_gate",
        "w_up", "w_down", "final_g"]
_OUTS = [(1, T, D), (S, 1, D), (1, 1, H, DH, DH), (1, 1, H, DH), (1, 1, H), (1, 1, PAD, CB * P),
         (1, S, H, DH, DH), (1, S, H, DH), (1, S, H), (1, S, PAD, CB * P)]
_NO_DEPTH = {"x_prompt", "x_sample", "c_prompt", "c_sample", "final_g"}


def kernel(**inputs):
    import numpy as _np
    import concourse.bacc as _bacc
    from concourse.bass_utils import run_bass_kernel_spmd as _run

    nc = _bacc.Bacc("TRN2", target_bir_lowering=False, num_devices=1)
    arrays, args = {}, []
    for name in _INS:
        a = _np.ascontiguousarray(inputs[name])
        arrays[f"in_{name}"] = a
        ap = nc.dram_tensor(f"in_{name}", a.shape, mybir.dt.from_np(a.dtype), kind="ExternalInput").ap()
        if name == "w_dw":
            ap = ap[0, :, 0, :]
        elif name not in _NO_DEPTH:
            ap = ap[0]
        args.append(ap)
    outs = []
    for i, shape in enumerate(_OUTS):
        ap = nc.dram_tensor(f"out_{i}", shape, F32, kind="ExternalOutput").ap()
        outs.append(ap if i < 2 else ap[0] if i >= 6 else ap[0, 0])
    build(nc, *args, *outs)
    r = _run(nc, [arrays], core_ids=[0])
    return tuple(r.results[0][f"out_{i}"] for i in range(len(_OUTS)))
```
